# Optimizing a Trainium2 kernel written in Bass

```python
import math
import jax, jax.numpy as jnp
from jax import lax
import numpy as np

D_MODEL = 2048
BATCH = 1
SEQ = 512
DEPTH = 1
DEC_BATCH = 8
DEC_SEQ = 1
PAST_LEN = 512
PAGE_SIZE = 128

ATTN_HEADS = 8
ATTN_HEAD_DIM = 128
IDX_HEADS = 16
IDX_HEAD_DIM = 64
TOPK_MAX = 256
Q_BLOCK = 128
RET_HEADS = 8
RET_DK = 128
RET_DV = 128
RET_CHUNK = 128
ROPE_BASE = 10000.0
D_FF = 4 * D_MODEL
EPS = 1e-6
MIX_WIDTH = ATTN_HEADS * ATTN_HEAD_DIM + RET_HEADS * RET_DV
PROJ_SPLITS = (ATTN_HEADS * ATTN_HEAD_DIM, ATTN_HEAD_DIM, ATTN_HEAD_DIM,
               IDX_HEADS * IDX_HEAD_DIM, IDX_HEAD_DIM, IDX_HEADS,
               RET_HEADS * RET_DK, RET_HEADS * RET_DK, RET_HEADS * RET_DV, RET_HEADS * RET_DV)
PROJ_WIDTH = sum(PROJ_SPLITS)

kernel_name = 'dsa_retention_parallel_hybrid_step'

def rmsnorm(x, g):
    xf = x.astype(jnp.float32)
    y = xf * lax.rsqrt(jnp.mean(jnp.square(xf), -1, keepdims=True) + EPS)
    return (y * g.astype(jnp.float32)).astype(x.dtype)

def layernorm(x, g, b):
    xf = x.astype(jnp.float32)
    mu = jnp.mean(xf, -1, keepdims=True)
    var = jnp.mean(jnp.square(xf - mu), -1, keepdims=True)
    y = (xf - mu) * lax.rsqrt(var + EPS) * g.astype(jnp.float32) + b.astype(jnp.float32)
    return y.astype(x.dtype)

def rotary(x, pos):
    half = x.shape[-1] // 2
    inv = ROPE_BASE ** (-jnp.arange(half, dtype=jnp.float32) / half)
    ang = pos[:, None] * inv[None, :]
    cos = jnp.cos(ang)[None, :, None, :]
    sin = jnp.sin(ang)[None, :, None, :]
    xf = x.astype(jnp.float32)
    x1, x2 = xf[..., :half], xf[..., half:]
    return jnp.concatenate([x1 * cos - x2 * sin, x2 * cos + x1 * sin], -1).astype(x.dtype)

def ret_log_gamma():
    return jnp.log1p(-jnp.exp2(-5.0 - jnp.arange(RET_HEADS, dtype=jnp.float32)))

def mixer_inputs(x, pos0, norm1_g, w_in, idx_k_norm_g, idx_k_norm_b):
    b, n, _ = x.shape
    h = rmsnorm(x, norm1_g)
    proj = h @ w_in
    cuts = np.cumsum(PROJ_SPLITS)[:-1].tolist()
    qa, ka, va, qi, ki, wi, qr, kr, vr, gr = jnp.split(proj, cuts, axis=-1)
    qa = qa.reshape(b, n, ATTN_HEADS, ATTN_HEAD_DIM)
    qi = qi.reshape(b, n, IDX_HEADS, IDX_HEAD_DIM)
    ki = layernorm(ki, idx_k_norm_g, idx_k_norm_b)
    wi = wi * (IDX_HEADS ** -0.5)
    pos = jnp.arange(n, dtype=jnp.float32) + pos0
    qr = rotary(qr.reshape(b, n, RET_HEADS, RET_DK), pos)
    kr = rotary(kr.reshape(b, n, RET_HEADS, RET_DK), pos) * (RET_DK ** -0.5)
    vr = vr.reshape(b, n, RET_HEADS, RET_DV)
    return qa, ka, va, qi, ki, wi, qr, kr, vr, gr

def dsa_attend(q, qi, wi, k, v, ki, q_pos0):
    b, nq = q.shape[:2]
    L = k.shape[1]
    k_sel = min(TOPK_MAX, L // 4)
    qb = Q_BLOCK if nq % Q_BLOCK == 0 else nq
    nb = nq // qb
    kpos = jnp.arange(L, dtype=jnp.int32)
    qpos = (jnp.arange(nq, dtype=jnp.int32) + q_pos0).reshape(nb, qb)
    kif = ki.astype(jnp.float32)

    def to_blocks(a):
        return a.reshape((b, nb, qb) + a.shape[2:]).swapaxes(0, 1)

    def block(args):
        qq, qqi, ww, pp = args
        s = jnp.einsum('bqhd,bkd->bqhk', qqi.astype(jnp.float32), kif)
        score = jnp.einsum('bqhk,bqh->bqk', jax.nn.relu(s), ww.astype(jnp.float32)) * (IDX_HEAD_DIM ** -0.5)
        causal = kpos[None, None, :] <= pp[None, :, None]
        score = jnp.where(causal, score, -jnp.inf)
        _, idx = lax.top_k(score, k_sel)
        kg = jax.vmap(lambda kk, ii: kk[ii])(k, idx)
        vg = jax.vmap(lambda vv, ii: vv[ii])(v, idx)
        valid = idx <= pp[None, :, None]
        sc = jnp.einsum('bqhd,bqkd->bqhk', qq, kg).astype(jnp.float32) * (ATTN_HEAD_DIM ** -0.5)
        sc = jnp.where(valid[:, :, None, :], sc, -jnp.inf)
        p = jax.nn.softmax(sc, axis=-1)
        return jnp.einsum('bqhk,bqkd->bqhd', p.astype(vg.dtype), vg)

    out = lax.map(block, (to_blocks(q), to_blocks(qi), to_blocks(wi), qpos))
    return out.swapaxes(0, 1).reshape(b, nq, ATTN_HEADS * ATTN_HEAD_DIM)

def ret_chunk(R, q, k, v, lg):
    q = q.astype(jnp.float32)
    k = k.astype(jnp.float32)
    v = v.astype(jnp.float32)
    n = q.shape[1]
    i = jnp.arange(n, dtype=jnp.float32)
    diff = i[:, None] - i[None, :]
    decay = jnp.where(diff[None] >= 0, jnp.exp(jnp.maximum(diff, 0.0)[None] * lg[:, None, None]), 0.0)
    inner = jnp.einsum('bhij,bjhe->bihe', jnp.einsum('bihd,bjhd->bhij', q, k) * decay[None], v)
    cross = jnp.einsum('bihd,bhde->bihe', q, R) * jnp.exp((i + 1.0)[:, None] * lg[None, :])[None, :, :, None]
    zeta = jnp.exp((n - 1.0 - i)[:, None] * lg[None, :])
    R_new = jnp.exp(n * lg)[None, :, None, None] * R + jnp.einsum('bjhd,bjhe,jh->bhde', k, v, zeta)
    return R_new, inner + cross

def retention_prompt(q, k, v):
    b, n = q.shape[:2]
    c = RET_CHUNK if n % RET_CHUNK == 0 else n
    nc = n // c
    lg = ret_log_gamma()

    def chunks(a):
        return a.reshape((b, nc, c) + a.shape[2:]).swapaxes(0, 1)

    R0 = jnp.zeros((b, RET_HEADS, RET_DK, RET_DV), jnp.float32)
    R, out = lax.scan(lambda R, xs: ret_chunk(R, xs[0], xs[1], xs[2], lg), R0, (chunks(q), chunks(k), chunks(v)))
    return out.swapaxes(0, 1).reshape(b, n, RET_HEADS, RET_DV), R

def finish(x, attn_o, ret_o, gr, w_out, norm2_g, w_up, w_down, final_norm_g):
    b, n, _ = x.shape
    rn = ret_o * lax.rsqrt(jnp.mean(jnp.square(ret_o), -1, keepdims=True) + EPS)
    rg = rn.reshape(b, n, RET_HEADS * RET_DV) * jax.nn.silu(gr.astype(jnp.float32))
    mixed = jnp.concatenate([attn_o.astype(x.dtype), rg.astype(x.dtype)], -1) @ w_out
    x = x + mixed
    u = rmsnorm(x, norm2_g) @ w_up
    x = x + jnp.square(jax.nn.relu(u)) @ w_down
    return rmsnorm(x, final_norm_g)

def gather_pages(cache, page_table):
    return cache[page_table].reshape(page_table.shape[0], -1, cache.shape[-1])

def setup_inputs(seed: int = 0) -> dict:
    key = jax.random.key(seed)
    ks = jax.random.split(key, 17)
    n_pages = PAST_LEN // PAGE_SIZE
    used = DEC_BATCH * n_pages
    n_pool = used + max(1, used // 4)
    f32 = jnp.float32
    gamma = 1.0 - jnp.exp2(-5.0 - jnp.arange(RET_HEADS, dtype=f32))
    ret_std = jnp.sqrt(1.0 / (1.0 - gamma ** 2)) * (RET_DK ** -0.5)
    page_table = jax.random.permutation(ks[6], n_pool)[:used].reshape(DEC_BATCH, n_pages).astype(jnp.int32)
    return {
        'x_prompt': jax.random.normal(ks[0], (BATCH, SEQ, D_MODEL), f32),
        'x_sample': jax.random.normal(ks[1], (DEC_BATCH, DEC_SEQ, D_MODEL), f32),
        'cache_k': jax.random.normal(ks[2], (n_pool, PAGE_SIZE, ATTN_HEAD_DIM), f32),
        'cache_v': jax.random.normal(ks[3], (n_pool, PAGE_SIZE, ATTN_HEAD_DIM), f32),
        'cache_idx_k': jax.random.normal(ks[4], (n_pool, PAGE_SIZE, IDX_HEAD_DIM), f32),
        'state_ret': jax.random.normal(ks[5], (DEC_BATCH, RET_HEADS, RET_DK, RET_DV), f32) * ret_std[None, :, None, None],
        'page_table': page_table,
        'norm1_g': 1.0 + 0.02 * jax.random.normal(ks[7], (D_MODEL,), f32),
        'w_in': jax.random.normal(ks[8], (D_MODEL, PROJ_WIDTH), f32) * (D_MODEL ** -0.5),
        'idx_k_norm_g': 1.0 + 0.02 * jax.random.normal(ks[9], (IDX_HEAD_DIM,), f32),
        'idx_k_norm_b': 0.02 * jax.random.normal(ks[10], (IDX_HEAD_DIM,), f32),
        'w_out': jax.random.normal(ks[11], (MIX_WIDTH, D_MODEL), f32) * (MIX_WIDTH ** -0.5),
        'norm2_g': 1.0 + 0.02 * jax.random.normal(ks[12], (D_MODEL,), f32),
        'w_up': jax.random.normal(ks[13], (D_MODEL, D_FF), f32) * (D_MODEL ** -0.5),
        'w_down': jax.random.normal(ks[14], (D_FF, D_MODEL), f32) * (D_FF ** -0.5),
        'final_norm_g': 1.0 + 0.02 * jax.random.normal(ks[15], (D_MODEL,), f32),
    }

def reference(x_prompt, x_sample, cache_k, cache_v, cache_idx_k, state_ret, page_table,
              norm1_g, w_in, idx_k_norm_g, idx_k_norm_b, w_out, norm2_g, w_up, w_down, final_norm_g):
    past_len = page_table.shape[1] * cache_k.shape[1]
    y_prompt = x_prompt
    y_sample = x_sample
    for _layer in range(DEPTH):
        qa, ka, va, qi, ki, wi, qr, kr, vr, gr = mixer_inputs(
            y_prompt, 0, norm1_g, w_in, idx_k_norm_g, idx_k_norm_b)
        attn_p = dsa_attend(qa, qi, wi, ka, va, ki, 0)
        ret_p, ret_state_p = retention_prompt(qr, kr, vr)
        y_prompt = finish(y_prompt, attn_p, ret_p, gr, w_out, norm2_g, w_up, w_down, final_norm_g)
        sqa, ska, sva, sqi, ski, swi, sqr, skr, svr, sgr = mixer_inputs(
            y_sample, past_len, norm1_g, w_in, idx_k_norm_g, idx_k_norm_b)
        k_all = jnp.concatenate([gather_pages(cache_k, page_table), ska.astype(cache_k.dtype)], 1)
        v_all = jnp.concatenate([gather_pages(cache_v, page_table), sva.astype(cache_v.dtype)], 1)
        ik_all = jnp.concatenate([gather_pages(cache_idx_k, page_table), ski.astype(cache_idx_k.dtype)], 1)
        attn_s = dsa_attend(sqa, sqi, swi, k_all, v_all, ik_all, past_len)
        ret_state_s, ret_s = ret_chunk(state_ret.astype(jnp.float32), sqr, skr, svr, ret_log_gamma())
        y_sample = finish(y_sample, attn_s, ret_s, sgr, w_out, norm2_g, w_up, w_down, final_norm_g)
    return (y_prompt, y_sample, ka, va, ki, ret_state_p, ska, sva, ski, ret_state_s)


_drawn_inputs = setup_inputs


def setup_inputs(seed=0):
    import zlib

    import numpy as np

    out = dict(_drawn_inputs(seed))
    spreads = {}
    factors = {'norm2_g': 3.364, 'final_norm_g': 2.733}
    for name, (base, spread) in spreads.items():
        noise = np.random.default_rng([zlib.crc32(name.encode()), seed]).standard_normal(out[name].shape)
        drawn = base * np.exp(spread * noise) if base else spread * noise
        out[name] = __import__('jax').numpy.asarray(drawn.astype(out[name].dtype))
    for name, factor in factors.items():
        out[name] = (out[name] * factor).astype(out[name].dtype)
    return out
```

```python
from contextlib import ExitStack, contextmanager

import concourse.bass as bass
from concourse import mybir

P = 128
D = 2048
KT = D // P
NP_, NS = 512, 8
T = NP_ + NS
HT = T // 2
QB = NP_ // P
NH = 8
IH, ID = 16, 64
TOPK = 128
PAGES = 4
CL = PAGES * P
CW = CL + 2
DFF = 4 * D
CH = 8
NCHUNK = DFF // (CH * P)
EPS = 1e-6
MASKED = -1e30
TAKEN = -3.0e38
OFF_QA, OFF_KA, OFF_VA, OFF_QI = 0, 1024, 1152, 1280
OFF_KI, OFF_QR, OFF_KR, OFF_VR, OFF_GR = 2304, 2384, 3408, 4432, 5456
KIWI = ID + IH
RING = 4

TILE_QI, TILE_QA, TILE_HEAD, TILE_OUT, TILE_MLP = 3, 11, 19, 51, 67
TAKEN0 = 2
UNITS = 2 * TILE_MLP + NCHUNK * (2 * CH + KT)
LAST_TILE, LAST_UNIT = TILE_MLP + 24 * (NCHUNK - 1), UNITS - 2 * CH - KT

PIECES = [(0, 1, 0, 0), (1, 1, 2, 1), (0, 2, 0, 1), (0, 3, 1, 0), (1, 2, 3, 0), (0, 4, 1, 1), (0, 5, 2, 0), (1, 3, 3, 1)]
ACT_PIECES = 3

F32, F32R, BF16, I32 = mybir.dt.float32, mybir.dt.float32r, mybir.dt.bfloat16, mybir.dt.int32
ALU = mybir.AluOpType
ACT = mybir.ActivationFunctionType
X = mybir.AxisListType.X


def unit_of(tile):
    return 2 * tile


class Chain:

    def __init__(self, eng, sem):
        self.eng, self.sem, self.n, self.at = eng, sem, 0, 0

    def __call__(self, ins):
        ins.then_inc(self.sem, 1)
        self.n += 1
        self.eng.wait_ge(self.sem, self.at + self.n)

    @contextmanager
    def loop(self, count, per):
        at, n = self.at, self.n
        with self.eng.Fori(0, count) as i:
            self.at, self.n = at + i * per, n
            yield i
            assert self.n - n == per, f"{self.n - n} steps in a round, not {per}"
        self.at, self.n = at, n + count * per


def build(nc, x_prompt, x_sample, cache_k, cache_v, cache_idx_k, state_ret, page_table, norm1_g, w_in,
          idx_k_norm_g, idx_k_norm_b, w_out, norm2_g, w_up, w_down, final_norm_g, shapes_const, rotary, decay,
          y_p, y_s, k_p, v_p, ik_p, rs_p, k_s, v_s, ik_s, rs_s):
    ctx = ExitStack()
    with ctx:
        BASE = 16512

        def at(name, offset, shape, dt=F32):
            return nc.alloc_sbuf_tensor_at(name, shape, dt, offset=BASE + offset)

        def sem(name):
            return ctx.enter_context(nc.semaphore(name))

        a_hi = at("a_hi", 0, [P, KT, T], F32R)
        a_lo = at("a_lo", 33280, [P, KT, T], F32R)
        w_raw = at("w_raw", 66560, [P, 2, 8, P])
        w_hi = at("w_hi", 74752, [P, RING, 8, P], F32R)
        w_lo = at("w_lo", 91136, [P, RING, 8, P], F32R)
        M0 = 107520
        mix = at("mix", M0, [P, KT, T])
        b_hi = at("b_hi", M0, [P, CH, T], F32R)
        b_lo = at("b_lo", M0 + 16640, [P, CH, T], F32R)
        x_in = at("x_in", M0, [P, QB, D])
        kpages = at("kpages", M0, [P, NS * PAGES, P])
        vpages = at("vpages", M0 + 16640, [P, NS * PAGES, P])
        R0 = 140800
        xr = at("xr", R0, [P, KT, T])
        qi = at("qi", R0, [P, 8, T])
        qa = at("qa", R0 + 16640, [P, NH, T])
        ipages = at("ipages", R0 + 16640, [P, NS * PAGES, ID])
        relu_p = at("relu_p", R0 + 16640 + 8192, [P, 2, NP_])
        ki_dup = at("ki_dup", R0 + 16640 + 12288, [P, 5, 2 * ID])
        kt_b = at("kt_b", R0, [P, 2, CW])
        am_s = at("am_s", R0 + 4128, [64, CW])
        p_s = at("p_s", R0 + 6208, [64, CW])
        pt_s = at("pt_s", R0 + 8288, [P, PAGES, 64])
        diag_s = at("diag_s", R0 + 9312, [64, 64])
        pown_s = at("pown_s", R0 + 9568, [NS, 64])
        rq = at("rq", R0, [P, T])
        rk = at("rk", R0 + 2080, [P, T])
        rv = at("rv", R0 + 4160, [P, T])
        rg = at("rg", R0 + 6240, [P, T])
        dh = at("dh", R0 + 8320, [P, NP_])
        ro = at("ro", R0 + 10368, [P, T])
        rs = at("rs", R0 + 12448, [P, NS, P])

        o = 174080
        small = {}
        for name, shape, dt, nbytes in (
                ("const", [P, 368], F32, 1472), ("ones", [P, P], F32, 512), ("gcol", [P, 48], F32, 192),
                ("rb", [P, T], F32, 2080), ("kt", [P, T], F32, 2080), ("vtok", [P, QB, P], F32, 2048),
                ("vs", [NS, P], F32, 512), ("kit", [P, T], F32, 2080), ("wi", [P, 5, IH], F32, 320),
                ("am", [P, QB - 1, NP_], BF16, 3072), ("st", [P, 96], F32, 384), ("pt_i", [1, 32], I32, 128)):
            small[name] = at(name, o, shape, dt)
            o += nbytes
        const, ones, gcol, rb, kt, vtok, vs, kit, wi, am, st, pt_i = small.values()
        assert o <= 188960
        cs = at("cs", 188960, [P, 2, T])
        H0 = 193120
        xs_in = at("xs_in", H0, [NS, D])
        graw = at("graw", H0 + 8192, [48, P])
        lng = at("lng", H0 + 8704, [P, 2, ID])
        rdiag = at("rdiag", H0 + 11296, [P, 5, P])
        kout = at("kout", H0, [P, QB, P])
        kout_s = at("kout_s", H0 + 2048, [NS, P])
        vt = at("vt", H0 + 2560, [P, T])
        kiwi = at("kiwi", H0 + 11296, [KIWI, T])
        ki5 = at("ki5", H0 + 13376, [P, 5, KIWI])
        xc = at("xc", H0 + 14976, [P, 5, ID])
        sq5 = at("sq5", H0 + 16256, [P, 5, ID])
        score = at("score", H0, [P, QB - 1, NP_])
        score_s = at("score_s", H0 + 6144, [NS, CW])
        qam = at("qam", H0 + 8224, [P, NS * 72])
        qis = at("qis", H0 + 10528, [ID, NS, IH])
        wis = at("wis", H0 + 11040, [IH, 64])
        kis = at("kis", H0 + 11296, [ID, 2, CW])
        relu_s = at("relu_s", H0 + 15424, [IH, 2, CW])
        p_h = at("p_h", H0, [P, 1280])
        sd_h = at("sd_h", H0, [P, 1280])
        pt_h = at("pt_h", H0 + 5120, [P, 1280])
        vbd = at("vbd", H0 + 5120, [NS, NS, P])
        ktok = at("ktok", H0 + 10240, [P, QB, P])
        rst = at("rst", H0 + 10240, [P, P])
        ks_tok = at("ks_tok", H0 + 12288, [NS, P])
        vtok_r = at("vtok_r", H0 + 12800, [P, QB, P])
        vs_tok = at("vs_tok", H0 + 14848, [NS, P])
        qc = at("qc", H0 + 15360, [P, NP_])
        t2 = at("t2", H0 + 17408, [P, T])
        sq = at("sq", H0, [P, T])
        ssum = at("ssum", H0 + 2080, [P, T])
        u1 = at("u1", H0 + 4160, [P, T])
        u2 = at("u2", H0 + 6240, [P, T])
        nv = at("nv", H0 + 8320, [P, T])
        ny = at("ny", H0 + 10400, [P, T])
        yt = at("yt", H0 + 12480, [P, 2, T])
        out_t = at("out_t", 0, [P, QB, D])
        out_s = at("out_s", 33280, [NS, D])

        ident, cmask = const[:, 0:P], const[:, P:2 * P]
        zeta, gamma = const[:, 256:288].rearrange("p (k h) -> p k h", h=NH), const[:, 288:296]
        expand, fold = const[0:NS, 296:360], const[0:64, 360:368]
        g1, g2, gf = gcol[:, 0:16], gcol[:, 16:32], gcol[:, 32:48]

        G = ctx.enter_context(nc.psum_tensor("product", [P, 4, 512], F32))
        B = ctx.enter_context(nc.psum_tensor("banks", [P, 4, 512], F32))

        def pair(p, rows=P):
            return G[0:rows, 2 * p:2 * p + 2, 0:HT]

        def halves(x):
            return x.rearrange("p (a b) -> p a b", a=2)

        def one(i):
            return bass.ds(i, 1)

        def row(x, i):
            return x[:, one(i), :].rearrange("p o n -> p (o n)")

        QOFF = [0, 128, 384, 768]
        KOFF = [0, 512, 896, 1152]
        xt_dram = nc.dram_tensor("x_transposed", (P, KT * T), F32).ap()

        s_raw = [sem(f"weights_loaded_{u}") for u in range(2)]
        s_hi, s_lo, s_used = sem("weights_hi"), sem("weights_lo"), sem("weights_used")
        s_evac = sem("tile_taken")
        s_x = [sem(f"x_loaded_{u}") for u in range(5)]
        (s_cst, s_rot, s_gr, s_lng, s_pt, s_set, s_ssq, s_gt, s_gc, s_xt, s_xr, s_a0, s_spill, s_var, s_sqrt,
         s_diag, s_rbm, s_rbd, s_y, s_yd, s_kvo, s_lnv, s_lns, s_ln, s_kit, s_kitd, s_is, s_rl, s_ic) = (
            sem(n) for n in (
                "consts_loaded", "rotary_loaded", "gains_loaded", "ln_loaded", "pages_listed", "set_up",
                "squares_summed", "gains_turned", "gains_ready", "x_turned", "xr_ready", "a0_ready", "x_spilled",
                "var_ready", "sqrt_ready", "diag_ready", "rms_spread", "rms_ready", "kv_turned", "kv_taken",
                "kv_stored", "ln_var", "ln_sqrt", "ln_done", "kit_turned", "kit_ready",
                "index_dots", "index_relu", "index_added"))
        (s_pi, s_pk, s_pv, s_qis, s_st, s_sk, s_ss, s_sr, s_sw, s_scs, s_ams, s_qam, s_at, s_ak, s_aq, s_ax,
         s_nms, s_exps, s_ps, s_dg, s_apt, s_so) = (
            sem(n) for n in (
                "ipages_loaded", "kpages_loaded", "vpages_loaded", "sample_iq", "ipages_turned", "sample_ik",
                "sample_dots", "sample_relu", "sample_weighed", "sample_scores", "sample_mask", "sample_q",
                "kpages_turned", "sample_k", "sample_qk", "mask_spread", "sample_max", "sample_exp", "sample_p",
                "own_diag", "sample_p_turned", "sample_o"))
        (s_qc, s_swap, s_rq, s_rk, s_xp, s_xd, s_nm, s_exp, s_pn, s_dh, s_rs, s_rst, s_rso, s_rv, s_vbd, s_sq,
         s_th, s_hs, s_head) = (
            sem(n) for n in (
                "head_q", "halves_swapped", "ret_q", "ret_k", "head_bank_full", "head_bank_taken", "head_max",
                "head_exp", "head_p", "decay_loaded", "state_loaded", "prompt_state_stored",
                "sample_state_stored", "ret_v", "values_diagonal", "ret_squared", "gate_tanh",
                "ret_sqrt", "head_done"))
        (s_t1h, s_t1p, s_t1, s_xb, s_n2, s_n2m, s_n2v, s_n2s, s_rb2, s_t2h, s_t2, s_b, s_nf, s_nfm, s_nfv, s_nfs, s_yt,
         s_yx, s_ye, s_out, s_rn, s_chain) = (
            sem(n) for n in (
                "mixed_hi", "mixed_lo_pool", "mixed_lo", "x_back", "sum2", "sum2_spread", "var2", "sqrt2", "rms2_ready", "h2_hi",
                "h2_lo", "hidden_ready", "sumf", "sumf_spread", "varf", "sqrtf", "y_scaled", "y_turned",
                "y_taken", "y_stored", "rmsf_ready", "vector_step"))

        s_fin = [sem("rows_scaled_vector"), sem("rows_scaled_scalar")]

        block = ctx.enter_context(nc.Block())

        @block.sync
        def _(sp):
            def load_unit(slot, n, src, cols=P):
                if not isinstance(n, int) or n >= 2:
                    sp.wait_ge(s_lo, n - 1)
                sp.dma_start(w_raw[:, slot, :, 0:cols], src.rearrange("(k p) c -> p k c", p=P)).then_inc(s_raw[slot], 16)

            def rows(w, half, col, cols=P):
                return w[half * 1024:half * 1024 + 1024, bass.ds(col, cols)]

            sp.dma_start(pt_i[:, :], page_table.rearrange("b j -> (b j)")[None, :]).then_inc(s_pt, 16)
            for tb in range(QB):
                sp.dma_start(x_in[:, tb, :], x_prompt[0, tb * P:(tb + 1) * P, :]).then_inc(s_x[tb], 16)
            sp.dma_start(xs_in[:, :], x_sample.rearrange("b o d -> (b o) d")).then_inc(s_x[4], 16)
            load_unit(0, 0, rows(w_in, 0, OFF_KA))
            load_unit(1, 1, rows(w_in, 1, OFF_KA))
            sp.wait_ge(s_xr, KT)
            sp.dma_start(xt_dram, xr[:, :, :].rearrange("p k t -> p (k t)")).then_inc(s_spill, 16)
            load_unit(0, 2, rows(w_in, 0, OFF_VA))
            load_unit(1, 3, rows(w_in, 1, OFF_VA))
            load_unit(0, 4, rows(w_in, 0, OFF_KI, KIWI), KIWI)
            load_unit(1, 5, rows(w_in, 1, OFF_KI, KIWI), KIWI)
            sp.wait_ge(s_pt, 16)
            sp.wait_ge(s_spill, 16)
            with sp.Fori(0, 4) as i:
                for u in range(4):
                    load_unit(u % 2, unit_of(TILE_QI) + 4 * i + u, rows(w_in, u % 2, OFF_QI + 256 * i + P * (u // 2)))
                    for v in range(2):
                        j = 8 * i + 2 * u + v
                        page = sp.value_load(pt_i[0:1, one(j)])
                        for dst, cache, s in ((ipages, cache_idx_k, s_pi), (kpages, cache_k, s_pk),
                                              (vpages, cache_v, s_pv)):
                            sp.dma_start(dst[:, one(j), :], cache[one(page), :, :].rearrange("a p d -> p a d")
                                         ).then_inc(s, 16)
            with sp.Fori(0, 4) as i:
                for u in range(4):
                    load_unit(u % 2, unit_of(TILE_QA) + 4 * i + u, rows(w_in, u % 2, OFF_QA + 256 * i + P * (u // 2)))
            with sp.Fori(0, NH) as i:
                for u in range(8):
                    off = (OFF_VR, OFF_QR, OFF_KR, OFF_GR)[u // 2]
                    load_unit(u % 2, unit_of(TILE_HEAD) + 8 * i + u, rows(w_in, u % 2, off + P * i))
                    if u == 4:
                        sp.wait_ge(s_head, i + 1)
                        sp.dma_start(dh[:, :], decay[one(i), :, :].rearrange("a p n -> (a p) n")).then_inc(s_dh, 16)
                        sp.wait_ge(s_rso, 16 * i + 16)
                        sp.dma_start(rs[:, :, :], state_ret[:, one(i), :, :].rearrange("b a d e -> d (b a) e")
                                     ).then_inc(s_rs, 16)
            with sp.Fori(0, KT // 2) as i:
                for u in range(4):
                    load_unit(u % 2, unit_of(TILE_OUT) + 4 * i + u, rows(w_out, u % 2, 256 * i + P * (u // 2)))
            with sp.Fori(0, NCHUNK) as c:
                n0 = unit_of(TILE_MLP) + 32 * c
                with sp.Fori(0, CH // 2) as i:
                    for u in range(4):
                        load_unit(u % 2, n0 + 4 * i + u, rows(w_up, u % 2, 1024 * c + 256 * i + P * (u // 2)))
                with sp.Fori(0, KT // 4) as i:
                    for u in range(4):
                        load_unit(u % 2, n0 + 16 + 4 * i + u,
                                  w_down[bass.ds(1024 * c, 1024), bass.ds(512 * i + P * u, P)])
            sp.wait_ge(s_kvo, 64)
            sp.wait_ge(s_rst, 16 * NH + 16)
            sp.wait_ge(s_rso, 16 * NH + 16)
            for n, (s, count, tb, half) in enumerate(PIECES):
                sp.wait_ge(s_fin[s], count)
                cols = slice(half * D // 2, (half + 1) * D // 2)
                sp.dma_start(y_p[0, tb * P:(tb + 1) * P, cols], out_t[:, tb, cols]).then_inc(s_out, 16)
            sp.wait_ge(s_fin[1], ACT_PIECES + 1)
            sp.dma_start(y_s.rearrange("b o d -> (b o) d"), out_s[:, :]).then_inc(s_out, 16)
            sp.wait_ge(s_out, 16 * (2 * QB + 1))

        @block.gpsimd
        def _(pool):
            def low(n, slot, raw, cols=P):
                pool.wait_ge(s_hi, n + 1)
                pool.wait_ge(s_raw[raw], 16 * (n // 2 + 1) if isinstance(n, int) else 0)
                nc.gpsimd.tensor_tensor(w_lo[:, slot, :, 0:cols], w_raw[:, raw, :, 0:cols],
                                        w_hi[:, slot, :, 0:cols].bitcast(F32), ALU.subtract).then_inc(s_lo, 1)

            for n in range(6):
                low(n, n % RING, n % 2, KIWI if n >= 4 else P)
            def low_units(first, last):
                with pool.Fori(0, (last - first) // RING) as i:
                    for u in range(RING):
                        slot, raw = (first + u) % RING, u % 2
                        pool.wait_ge(s_hi, first + 4 * i + u + 1)
                        pool.wait_ge(s_raw[raw], 16 * (2 * i + (first + u) // 2 + 1))
                        nc.gpsimd.tensor_tensor(w_lo[:, slot, :, :], w_raw[:, raw, :, :],
                                                w_hi[:, slot, :, :].bitcast(F32), ALU.subtract).then_inc(s_lo, 1)

            low_units(6, unit_of(TILE_OUT) + 4)
            for k in range(NH):
                pool.wait_ge(s_t1h, k + 1)
                nc.gpsimd.tensor_tensor(a_lo[:, k, :], mix[:, k, :], a_hi[:, k, :].bitcast(F32), ALU.subtract
                                        ).then_inc(s_t1p, 1)
            low_units(unit_of(TILE_OUT) + 4, UNITS)

        @block.tensor
        def _(pe):
            def unit(n, slot, hi, lo, out, first, last, k0=0, cols=P, ready=None, ready_at=0):
                pe.wait_ge(s_lo, n + 1)
                for k in range(8):
                    if ready is not None:
                        if ready is s_t1:
                            pe.wait_ge(*((s_t1p, k0 + k + 1) if k0 + k < NH else (s_t1, k0 + k + 1 - NH)))
                        else:
                            pe.wait_ge(ready, ready_at + k0 + k + 1)
                    for part, (w, a) in enumerate(((w_hi, hi), (w_hi, lo), (w_lo, hi))):
                        for half in range(2):
                            last_mm = nc.tensor.matmul(
                                out[:, half, :], w[:, slot, k, 0:cols], a[:, k0 + k, half * HT:(half + 1) * HT],
                                start=(first and k == 0 and part == 0), stop=(last and k == 7 and part == 2))
                return last_mm

            def tile(m, m_static, n, base_unit, cols=P, ready=None, between=None):
                out = pair(m_static % 2)[0:cols]
                if m_static >= 2:
                    pe.wait_ge(s_evac, m - 1)
                a = unit(n, base_unit % RING, a_hi, a_lo, out, True, False, 0, cols, ready)
                a.then_inc(s_used, 1)
                if between:
                    between()
                b = unit(n + 1, (base_unit + 1) % RING, a_hi, a_lo, out, False, True, 8, cols, ready)
                b.then_inc(s_used, 1)

            def turn(out, x, n):
                return nc.tensor.transpose(out, x, ident[0:n, 0:n])

            def mm(out, lhsT, rhs, start=True, stop=True):
                return nc.tensor.matmul(out, lhsT, rhs, start=start, stop=stop, skip_group_check=True)

            pe.wait_ge(s_cst, 16)
            pe.wait_ge(s_gr, 48)
            turn(B[:, 3, 0:48], graw[:, :], 48).then_inc(s_gt, 1)
            for tb in range(5):
                pe.wait_ge(s_x[tb], 16)
            for f in range(KT):
                b = 2 * (f % 2)
                if f == 1:
                    pe.wait_ge(s_gc, 1)
                if f >= 2:
                    pe.wait_ge(s_xr, f - 1)
                for tb in range(QB):
                    turn(B[:, b, tb * P:(tb + 1) * P], x_in[:, tb, f * P:(f + 1) * P], P)
                turn(B[:, b + 1, 0:NS], xs_in[:, f * P:(f + 1) * P], NS).then_inc(s_xt, 1)
            tile(0, 0, 0, 0, ready=s_a0)
            pe.wait_ge(s_xr, KT)
            pe.wait_ge(s_diag, 1)
            for tb in range(QB):
                mm(B[:, 0, tb * P:(tb + 1) * P], ones[:, :], rdiag[:, tb, :])
            mm(B[:, 1, 0:NS], ones[0:NS, :], rdiag[0:NS, 4, 0:NS]).then_inc(s_rbm, 1)
            tile(1, 1, 2, 2)
            tile(2, 2, 4, 4, KIWI)
            for step, (src, rows_) in enumerate(((kt, P), (vt, P), (kiwi, KIWI))):
                b = (2, 0, 2)[step]
                pe.wait_ge(s_evac, step + 1)
                if step == 1:
                    pe.wait_ge(s_rbd, 1)
                if step == 2:
                    pe.wait_ge(s_yd, 2)
                for tb in range(QB):
                    last = turn(B[:, b, tb * rows_:(tb + 1) * rows_], src[:, tb * P:(tb + 1) * P], rows_)
                last.then_inc(s_y, 1)
                turn(B[0:NS, b + 1, 0:rows_], src[:, NP_:T], rows_).then_inc(s_y, 1)

            with pe.Fori(0, 4) as i:
                for u in range(2):
                    tile(TILE_QI + 2 * i + u, TILE_QI + u, unit_of(TILE_QI) + 4 * i + 2 * u, unit_of(TILE_QI) + 2 * u)

            pe.wait_ge(s_ln, 1)
            pe.wait_ge(s_yd, 6)
            for tb in range(QB):
                last = turn(B[:, 0, tb * P:(tb + 1) * P], ki_dup[:, tb, :], P)
            last.then_inc(s_kit, 1)
            turn(B[:, 1, 0:NS], ki_dup[0:NS, 4, :], NS).then_inc(s_kit, 1)
            pe.wait_ge(s_kitd, 2)
            pe.wait_ge(s_evac, TILE_QA)
            j = 0
            for b in range(1, QB):
                for h in range(IH):
                    if j >= 4:
                        pe.wait_ge(s_rl, j - 3)
                    r = slice(ID * (h % 2), ID * (h % 2) + ID)
                    mm(B[:, j % 4, 0:P * (b + 1)], qi[r, h // 2, b * P:(b + 1) * P], kit[r, 0:P * (b + 1)]
                       ).then_inc(s_is, 1)
                    j += 1
            pe.wait_ge(s_rl, j)
            pe.wait_ge(s_pi, 16 * NS * PAGES)
            pe.wait_ge(s_qis, 1)
            for step in range(NS + 2):
                if step < NS:
                    if step >= 2:
                        pe.wait_ge(s_sk, step - 1)
                    for g in range(PAGES):
                        last = turn(B[0:ID, step % 2, g * P:(g + 1) * P], ipages[:, PAGES * step + g, :], P)
                    last.then_inc(s_st, 1)
                if 1 <= step <= NS:
                    b = step - 1
                    pe.wait_ge(s_sk, b + 1)
                    if b:
                        pe.wait_ge(s_sr, b)
                    for half in range(2):
                        last = mm(B[0:IH, 2 + half, 0:257], qis[:, b, :], kis[:, b % 2, 257 * half:257 * half + 257])
                    last.then_inc(s_ss, 1)
                if step >= 2:
                    b = step - 2
                    pe.wait_ge(s_sr, b + 1)
                    for half in range(2):
                        last = mm(G[0:NS, half, 0:257], wis[:, NS * b:NS * b + NS],
                                  relu_s[:, b % 2, 257 * half:257 * half + 257], start=(b == 0), stop=(b == NS - 1))
                    last.then_inc(s_sw, 1)
            pe.wait_ge(s_scs, 1)

            with pe.Fori(0, 4) as i:
                for u in range(2):
                    tile(TILE_QA + 2 * i + u, TILE_QA + u, unit_of(TILE_QA) + 4 * i + 2 * u, unit_of(TILE_QA) + 2 * u)

            pe.wait_ge(s_pk, 16 * NS * PAGES)
            pe.wait_ge(s_qam, 1)
            for step in range(NS + 1):
                if step < NS:
                    if step >= 2:
                        pe.wait_ge(s_ak, step - 1)
                    for g in range(PAGES):
                        last = turn(B[:, step % 2, g * P:(g + 1) * P], kpages[:, PAGES * step + g, :], P)
                    last.then_inc(s_at, 1)
                if step >= 1:
                    b = step - 1
                    pe.wait_ge(s_ak, b + 1)
                    for half in range(2):
                        last = mm(B[0:64, 2 + half, 0:257], qam[:, 64 * b:64 * b + 64],
                                  kt_b[:, b % 2, 257 * half:257 * half + 257], start=(b == 0), stop=(b == NS - 1))
                    last.then_inc(s_aq, 1)
            pe.wait_ge(s_ams, 1)
            for half in range(2):
                last = mm(B[0:64, half, 0:257], expand, score_s[:, 257 * half:257 * half + 257])
            last.then_inc(s_ax, 1)
            pe.wait_ge(s_ps, 1)
            for g in range(PAGES):
                last = turn(B[:, 0, g * 64:(g + 1) * 64], p_s[:, g * P:(g + 1) * P], 64)
            last.then_inc(s_apt, 1)
            pe.wait_ge(s_dg, 1)
            mm(B[0:NS, 1, 0:64], fold, diag_s[:, :]).then_inc(s_apt, 1)
            pe.wait_ge(s_xd, TAKEN0)
            pe.wait_ge(s_pv, 16 * NS * PAGES)
            mm(B[:, 2, 0:64], vs[:, :], pown_s[:, :], stop=False)
            for b in range(NS):
                for g in range(PAGES):
                    last = mm(B[:, 2, NH * b:NH * b + NH], vpages[:, PAGES * b + g, :], pt_s[:, g, NH * b:NH * b + NH],
                              start=False, stop=(g == PAGES - 1))
            last.then_inc(s_so, 1)
            pe.wait_ge(s_head, 1)

            with pe.Fori(0, NH) as i:
                m0, n0 = TILE_HEAD + 4 * i, unit_of(TILE_HEAD) + 8 * i
                e0 = 24 * i

                def head_tile(u, between=None):
                    tile(m0 + u, TILE_HEAD + u, n0 + 2 * u, unit_of(TILE_HEAD) + 2 * u, between=between)

                def fill(e):
                    pe.wait_ge(s_xd, e0 + TAKEN0 + max(e - 3, 0))
                    return e % 4

                def values_and_scores():
                    pe.wait_ge(s_evac, m0 + 1)
                    x = fill(0)
                    for k in range(QB):
                        last = turn(B[:, x, k * P:(k + 1) * P], rv[:, k * P:(k + 1) * P], P)
                    last.then_inc(s_xp, 1)
                    turn(B[0:NS, fill(1), 0:P], rv[:, NP_:T], P).then_inc(s_xp, 1)
                    pe.wait_ge(s_qc, i + 1)
                    for b in range(QB):
                        mm(B[:, fill(2 + b), 0:P * (b + 1)], qc[:, b * P:(b + 1) * P], kt[:, 0:P * (b + 1)]
                           ).then_inc(s_xp, 1)

                def output_and_decay():
                    x = fill(10)
                    pe.wait_ge(s_xd, e0 + TAKEN0 + 10)
                    for k in range(QB):
                        last = mm(B[:, x, k * P:NP_], vtok[:, k, :], pt_h[:, KOFF[k]:KOFF[k] + NP_ - k * P],
                                  start=(k == 0), stop=(k == QB - 1))
                    last.then_inc(s_xp, 1)
                    pe.wait_ge(s_rk, i + 1)
                    for k in range(QB):
                        mm(B[:, fill(11 + k), 0:NP_ - k * P], rk[:, k * P:(k + 1) * P], rq[:, k * P:NP_]
                           ).then_inc(s_xp, 1)
                    x = fill(15)
                    for k in range(QB):
                        last = turn(B[:, x, k * P:(k + 1) * P], rk[:, k * P:(k + 1) * P], P)
                    last.then_inc(s_xp, 1)
                    turn(B[0:NS, fill(16), 0:P], rk[:, NP_:T], P).then_inc(s_xp, 1)

                head_tile(0)
                head_tile(1, between=values_and_scores)
                head_tile(2)
                pe.wait_ge(s_pn, i + 1)
                for k in range(QB):
                    x = fill(6 + k)
                    for b in range(k, QB):
                        last = turn(B[:, x, (b - k) * P:(b - k + 1) * P],
                                    p_h[:, QOFF[b] + k * P:QOFF[b] + (k + 1) * P], P)
                    last.then_inc(s_xp, 1)
                head_tile(3, between=output_and_decay)
                pe.wait_ge(s_vbd, i + 1)
                for j in range(2):
                    x = fill(17 + j)
                    pe.wait_ge(s_xd, e0 + TAKEN0 + 17)
                    mm(B[:, x, :], ks_tok[:, :], vbd[:, 4 * j:4 * j + 4, :]).then_inc(s_xp, 1)
                x = fill(19)
                for k in range(QB):
                    last = mm(B[:, x, k * P:NP_], vtok_r[:, k, :], sd_h[:, KOFF[k]:KOFF[k] + NP_ - k * P],
                              start=(k == 0), stop=(k == QB - 1))
                last.then_inc(s_xp, 1)
                x = fill(20)
                for k in range(QB):
                    last = mm(B[:, x, 0:P], ktok[:, k, :], vtok_r[:, k, :], start=(k == 0), stop=(k == QB - 1))
                last.then_inc(s_xp, 1)
                x = fill(21)
                pe.wait_ge(s_xd, e0 + TAKEN0 + 19)
                for b in range(NS):
                    last = mm(B[:, x, b:b + 1], rs[:, b, :], rq[:, NP_ + b:NP_ + b + 1])
                last.then_inc(s_xp, 1)
                for n, cols in enumerate((slice(0, NP_), slice(NP_, T))):
                    pe.wait_ge(s_sq, 2 * i + 1 + n)
                    mm(B[:, fill(22 + n), 0:cols.stop - cols.start], ones[:, :], rv[:, cols]).then_inc(s_xp, 1)

            with pe.Fori(0, KT // 2) as i:
                for u in range(2):
                    tile(TILE_OUT + 2 * i + u, TILE_OUT + u, unit_of(TILE_OUT) + 4 * i + 2 * u,
                         unit_of(TILE_OUT) + 2 * u, ready=s_t1)
            pe.wait_ge(s_n2, KT + 1)
            for half in range(2):
                last = mm(B[:, half, 0:HT], ones[:, :], ssum[:, half * HT:(half + 1) * HT])
            last.then_inc(s_n2m, 1)

            def up(m0, n0):
                with pe.Fori(0, CH // 2) as i:
                    for u in range(2):
                        tile(m0 + 2 * i + u, TILE_MLP + u, n0 + 4 * i + 2 * u, unit_of(TILE_MLP) + 2 * u, ready=s_t2)

            def down(m0, n0, ready_at, t, u):
                pe.wait_ge(s_evac, m0 + CH + t - 1)
                unit(n0 + 16 + t, (unit_of(TILE_MLP) + u) % RING, b_hi, b_lo, pair((TILE_MLP + u) % 2), True, True,
                     ready=s_b, ready_at=ready_at).then_inc(s_used, 1)

            def turn_rows(f):
                pe.wait_ge(s_yt, f + 1)
                if f >= 2:
                    pe.wait_ge(s_ye, f - 1)
                b = 2 * (f % 2)
                for tb in range(QB):
                    turn(B[:, b, tb * P:(tb + 1) * P], yt[:, f % 2, tb * P:(tb + 1) * P], P)
                turn(B[0:NS, b + 1, 0:P], yt[:, f % 2, NP_:T], P).then_inc(s_yx, 1)

            with pe.Fori(0, NCHUNK - 1) as c:
                m0, n0 = TILE_MLP + 24 * c, unit_of(TILE_MLP) + 32 * c
                up(m0, n0)
                with pe.Fori(0, KT // 4) as i:
                    for u in range(4):
                        down(m0, n0, CH * c, 4 * i + u, u)
            up(LAST_TILE, LAST_UNIT)
            for t in range(KT):
                down(LAST_TILE, LAST_UNIT, CH * (NCHUNK - 1), t, t)
                if t:
                    turn_rows(t - 1)
            pe.wait_ge(s_nf, 1)
            for tb in range(5):
                tok = slice(tb * P, min(tb * P + P, T))
                for n, x in enumerate((ssum, sq)):
                    last = mm(G[0:tok.stop - tok.start, 2, tb:tb + 1], x[:, tok], ones[:, 0:1], start=(n == 0),
                              stop=(n == 1))
            last.then_inc(s_nfm, 1)
            turn_rows(KT - 1)

        @block.scalar
        def _(act):
            def high(n, slot, raw, cols=P, first=False):
                act.wait_ge(s_raw[raw], 16 * (n // 2 + 1) if isinstance(n, int) else n)
                if not first:
                    act.wait_ge(s_used, n - 3)
                nc.scalar.copy(w_hi[:, slot, :, 0:cols], w_raw[:, raw, :, 0:cols]).then_inc(s_hi, 1)

            def high_at(base, four_i, u):
                act.wait_ge(s_raw[u % 2], 8 * four_i + 16 * ((base + u) // 2 + 1))
                act.wait_ge(s_used, four_i + base + u - 3)
                nc.scalar.copy(w_hi[:, (base + u) % RING, :, :], w_raw[:, u % 2, :, :]).then_inc(s_hi, 1)

            def act_fn(out, in_, fn, **kw):
                return nc.scalar.activation(out, in_, fn, **kw)

            act.dma_start(const[:, :], shapes_const).then_inc(s_cst, 16)
            for n, g in enumerate((norm1_g, norm2_g, final_norm_g)):
                act.dma_start(graw[16 * n:16 * n + 16, :], g.rearrange("(k p) -> k p", p=P)).then_inc(s_gr, 16)
            act.dma_start(cs[:, :, :], rotary).then_inc(s_rot, 16)
            for n, g in enumerate((idx_k_norm_g, idx_k_norm_b)):
                act.dma_start(lng[:, n, :], g[None, :].to_broadcast([P, ID])).then_inc(s_lng, 16)
            act.wait_ge(s_set, 1)
            for tb in range(5):
                act.wait_ge(s_x[tb], 16)
                if tb:
                    act.wait_ge(s_ssq, tb)
                if tb < QB:
                    sqs = act_fn(G[:, :, :].rearrange("p a b -> p (a b)"), x_in[:, tb, :], ACT.Square,
                                 accum_out=st[:, tb:tb + 1])
                else:
                    sqs = act_fn(G[0:NS, :, :].rearrange("p a b -> p (a b)"), xs_in[:, :], ACT.Square,
                                 accum_out=st[0:NS, 4:5])
                sqs.then_inc(s_ssq, 1)
            for f in range(KT):
                if f == 8:
                    high(0, 0, 0, first=True)
                    high(1, 1, 1, first=True)
                b = 2 * (f % 2)
                act.wait_ge(s_xt, f + 1)
                nc.scalar.copy(xr[:, f, 0:NP_], B[:, b, :])
                nc.scalar.copy(xr[:, f, NP_:T], B[:, b + 1, 0:NS]).then_inc(s_xr, 1)
            high(2, 2, 0, first=True)
            high(3, 3, 1, first=True)
            act.wait_ge(s_var, 1)
            act_fn(st[:, 10:15], st[:, 5:10], ACT.Sqrt).then_inc(s_sqrt, 1)
            high(4, 0, 0, KIWI)
            high(5, 1, 1, KIWI)
            high(6, 2, 0)
            high(7, 3, 1)
            act.wait_ge(s_yd, 2)
            act.dma_start(k_p[0].rearrange("(k p) d -> p k d", p=P), kout[:, :, :]).then_inc(s_kvo, 16)
            act.dma_start(k_s.rearrange("b o d -> (b o) d"), kout_s[:, :]).then_inc(s_kvo, 16)
            act.wait_ge(s_yd, 4)
            act.dma_start(v_p[0].rearrange("(k p) d -> p k d", p=P), vtok[:, :, :]).then_inc(s_kvo, 16)
            act.dma_start(v_s.rearrange("b o d -> (b o) d"), vs[:, :]).then_inc(s_kvo, 16)
            act.wait_ge(s_lnv, 1)
            act_fn(st[:, 10:15], st[:, 5:10], ACT.Sqrt).then_inc(s_lns, 1)
            act.wait_ge(s_ln, 1)
            act.dma_start(ik_p[0].rearrange("(k p) d -> p k d", p=P), ki_dup[:, 0:QB, 0:ID]).then_inc(s_rst, 16)
            act.dma_start(ik_s.rearrange("b o d -> (b o) d"), ki_dup[0:NS, 4, 0:ID]).then_inc(s_rso, 16)
            with act.Fori(0, 4) as i:
                for u in range(4):
                    high_at(unit_of(TILE_QI) + 2, 4 * i, u)
            j = 0
            for b in range(1, QB):
                for h in range(IH):
                    act.wait_ge(s_is, j + 1)
                    if j >= 2:
                        act.wait_ge(s_ic, j - 1)
                    act_fn(relu_p[:, j % 2, 0:P * (b + 1)], B[:, j % 4, 0:P * (b + 1)], ACT.Relu).then_inc(s_rl, 1)
                    j += 1
            for b in range(NS):
                act.wait_ge(s_ss, b + 1)
                if b >= 2:
                    act.wait_ge(s_sw, b - 1)
                act_fn(halves(relu_s[:, b % 2, :]), B[0:IH, 2:4, 0:257], ACT.Relu).then_inc(s_sr, 1)
            with act.Fori(0, 4) as i:
                for u in range(4):
                    high_at(unit_of(TILE_QA) + 2, 4 * i, u)
            act.wait_ge(s_qam, 1)
            for b in range(NS):
                act.wait_ge(s_at, b + 1)
                if b >= 2:
                    act.wait_ge(s_aq, b - 1)
                nc.scalar.copy(kt_b[:, b % 2, 0:CL], B[:, b % 2, :])
                nc.scalar.copy(kt_b[:, b % 2, CL:CL + 1], kt[:, NP_ + b:NP_ + b + 1]).then_inc(s_ak, 1)
            act.wait_ge(s_nms, 1)
            act_fn(p_s[:, :], p_s[:, :], ACT.Exp, bias=st[0:64, 42:43], accum_out=st[0:64, 43:44]).then_inc(s_exps, 1)

            for u in range(2):
                high_at(unit_of(TILE_HEAD) + 2, 0, u)
            with act.Fori(0, NH) as i:
                base, i8 = unit_of(TILE_HEAD) + 4, 8 * i

                def swap(m, done):
                    act.wait_ge(s_used, 2 * m + 2)
                    p = m_pair
                    nc.scalar.copy(t2[0:64, :].rearrange("p (a b) -> p a b", a=2), G[64:128, 2 * p:2 * p + 2, 0:HT])
                    nc.scalar.copy(t2[64:128, :].rearrange("p (a b) -> p a b", a=2), G[0:64, 2 * p:2 * p + 2, 0:HT]
                                   ).then_inc(s_swap, 1)

                high_at(base, i8, 0)
                high_at(base, i8, 1)
                for b in range(QB):
                    act.wait_ge(s_nm, 4 * i + b + 1)
                    n = slice(QOFF[b], QOFF[b] + P * (b + 1))
                    act_fn(p_h[:, n], p_h[:, n], ACT.Exp, bias=st[:, 25 + b:26 + b],
                           accum_out=st[:, 29 + b:30 + b]).then_inc(s_exp, 1)
                high_at(base, i8, 2)
                high_at(base, i8, 3)
                m_pair = (TILE_HEAD + 1) % 2
                swap(TILE_HEAD + 1 + 4 * i, 0)
                high_at(base, i8, 4)
                high_at(base, i8, 5)
                act.wait_ge(s_rq, i + 1)
                m_pair = (TILE_HEAD + 2) % 2
                swap(TILE_HEAD + 2 + 4 * i, 1)
                high_at(base, i8, 6)
                high_at(base, i8, 7)
                act.wait_ge(s_evac, TILE_HEAD + 4 * i + 4)
                act_fn(t2[:, :], rg[:, :], ACT.Tanh, scale=0.5).then_inc(s_th, 1)
                act.wait_ge(s_xd, 24 * i + TAKEN0 + 20)
                act_fn(rv[:, 0:NP_], ro[:, 0:NP_], ACT.Square).then_inc(s_sq, 1)
                act.wait_ge(s_xd, 24 * i + TAKEN0 + 22)
                act_fn(rv[:, NP_:T], ro[:, NP_:T], ACT.Square).then_inc(s_sq, 1)
                act.dma_start(rs_p[0, one(i), :, :].rearrange("a d e -> (a d) e"), rst[:, :]).then_inc(s_rst, 16)
                act.dma_start(rs_s[:, one(i), :, :].rearrange("b a d e -> d (b a) e"), rs[:, :, :]).then_inc(s_rso, 16)
                act.wait_ge(s_xd, 24 * i + TAKEN0 + 24)
                act_fn(rk[:, :], rv[:, :], ACT.Sqrt).then_inc(s_hs, 1)

            act.wait_ge(s_used, unit_of(TILE_OUT))
            for k in range(KT):
                if k == KT - 1:
                    act.wait_ge(s_head, NH + 1)
                nc.scalar.copy(a_hi[:, k, :], mix[:, k, :]).then_inc(s_t1h, 1)
            act.dma_start(xr[:, :, :].rearrange("p k t -> p (k t)"), xt_dram).then_inc(s_xb, 16)
            with act.Fori(0, KT // 2) as i:
                for u in range(4):
                    high_at(unit_of(TILE_OUT) + 4, 4 * i, u)
            act.wait_ge(s_evac, TILE_MLP)
            for k in range(KT):
                act_fn(a_hi[:, k, :], xr[:, k, :], ACT.Identity, scale=g2[:, k:k + 1]).then_inc(s_t2h, 1)
            act.wait_ge(s_n2v, 1)
            act_fn(ny[:, :], nv[:, :], ACT.Sqrt).then_inc(s_n2s, 1)
            first, last_down = unit_of(TILE_MLP) + 4, UNITS - KT
            with act.Fori(0, (last_down - first) // 4) as i:
                for u in range(4):
                    high_at(first, 4 * i, u)

            def rows_of(f):
                act.wait_ge(s_yx, f + 1)
                b = 2 * (f % 2)
                nc.scalar.copy(out_t[:, :, f * P:(f + 1) * P], B[:, b, :].rearrange("p (k d) -> p k d", d=P))
                nc.scalar.copy(out_s[:, f * P:(f + 1) * P], B[0:NS, b + 1, 0:P]).then_inc(s_ye, 1)

            for t in range(KT):
                high(last_down + t, (last_down + t) % RING, t % 2)
                if t >= 5:
                    rows_of(t - 5)
            for f in range(KT - 5, KT):
                if f == KT - 1:
                    act.wait_ge(s_nfv, 1)
                    act_fn(st[:, 75:80], st[:, 70:75], ACT.Sqrt).then_inc(s_nfs, 1)
                rows_of(f)
            act.wait_ge(s_rn, 1)
            act.wait_ge(s_ye, KT)
            for s, _, tb, half in PIECES:
                if s == 1:
                    x = out_t[:, tb, half * D // 2:(half + 1) * D // 2]
                    act_fn(x, x, ACT.Identity, scale=st[:, 75 + tb:76 + tb]).then_inc(s_fin[1], 1)
            act_fn(out_s[:, :], out_s[:, :], ACT.Identity, scale=st[0:NS, 79:80]).then_inc(s_fin[1], 1)

        @block.vector
        def _(dve):
            v = nc.vector
            step = Chain(dve, s_chain)

            def newton(y, var, t):
                step(v.reciprocal(y, y))
                step(v.tensor_tensor(t, var, y, ALU.mult))
                step(v.tensor_tensor(t, t, y, ALU.mult))
                step(v.tensor_scalar(t, t, -0.5, 1.5, ALU.mult, ALU.add))
                step(v.tensor_tensor(y, y, t, ALU.mult))

            step(v.memset(ones[:, :], 1.0))
            v.memset(st[:, :], 1.0).then_inc(s_set, 1)
            dve.wait_ge(s_gt, 1)
            v.tensor_copy(gcol[:, :], B[:, 3, 0:48]).then_inc(s_gc, 1)
            dve.wait_ge(s_gc, 1)
            for f in range(KT):
                dve.wait_ge(s_xr, f + 1)
                step(v.tensor_scalar(a_hi[:, f, :], xr[:, f, :], g1[:, f:f + 1], None, ALU.mult))
                v.scalar_tensor_tensor(out=a_lo[:, f, :], in0=xr[:, f, :], scalar=g1[:, f:f + 1],
                                       in1=a_hi[:, f, :].bitcast(F32), op0=ALU.mult, op1=ALU.subtract).then_inc(s_a0, 1)
            dve.wait_ge(s_ssq, 5)
            v.tensor_scalar(st[:, 5:10], st[:, 0:5], 1.0 / D, EPS, ALU.mult, ALU.add).then_inc(s_var, 1)
            dve.wait_ge(s_sqrt, 1)
            newton(st[:, 10:15], st[:, 5:10], st[:, 15:20])
            dve.wait_ge(s_cst, 16)
            for tb in range(5):
                last = v.tensor_scalar(rdiag[:, tb, :], ident, st[:, 10 + tb:11 + tb], None, ALU.mult)
            last.then_inc(s_diag, 1)
            dve.wait_ge(s_rbm, 1)
            v.tensor_copy(rb[:, 0:NP_], B[:, 0, :])
            v.tensor_copy(rb[:, NP_:T], B[:, 1, 0:NS]).then_inc(s_rbd, 1)
            dve.wait_ge(s_rbd, 1)
            dve.wait_ge(s_rot, 16)
            for n in range(2):
                step(v.tensor_tensor(cs[:, n, :], cs[:, n, :], rb[:, :], ALU.mult))

            def scaled(out, m, p, rows_=P):
                dve.wait_ge(s_used, 2 * m + 2)
                v.tensor_tensor(out, pair(p, rows_), halves(rb[0:rows_, :]), ALU.mult).then_inc(s_evac, 1)

            scaled(halves(kt[:, :]), 0, 0)
            scaled(halves(vt[:, :]), 1, 1)
            dve.wait_ge(s_y, 1)
            v.tensor_copy(kout[:, :, :], B[:, 2, :].rearrange("p (k d) -> p k d", d=P)).then_inc(s_yd, 1)
            dve.wait_ge(s_y, 2)
            v.tensor_copy(kout_s[:, :], B[0:NS, 3, 0:P]).then_inc(s_yd, 1)
            scaled(halves(kiwi[:, :]), 2, 0, KIWI)
            dve.wait_ge(s_y, 3)
            v.tensor_copy(vtok[:, :, :], B[:, 0, :].rearrange("p (k d) -> p k d", d=P)).then_inc(s_yd, 1)
            dve.wait_ge(s_y, 4)
            v.tensor_copy(vs[:, :], B[0:NS, 1, 0:P]).then_inc(s_yd, 1)
            step(v.memset(ki5[:, 4, :], 0.0))
            step(v.memset(wis[:, :], 0.0))
            dve.wait_ge(s_y, 5)
            v.tensor_copy(ki5[:, 0:QB, :], B[:, 2, 0:QB * KIWI].rearrange("p (k d) -> p k d", d=KIWI)).then_inc(s_yd, 1)
            dve.wait_ge(s_y, 6)
            v.tensor_copy(ki5[0:NS, 4, :], B[0:NS, 3, 0:KIWI]).then_inc(s_yd, 1)
            dve.wait_ge(s_yd, 6)
            dve.wait_ge(s_lng, 32)
            ki, mu, var, y5, t5 = ki5[:, :, 0:ID], st[:, 20:25], st[:, 5:10], st[:, 10:15], st[:, 15:20]

            def spread(x):
                return x.unsqueeze(2).to_broadcast([P, 5, ID])

            def per_column(x):
                return x.unsqueeze(1).to_broadcast([P, 5, ID])

            wscale = IH ** -0.5 * ID ** -0.5
            v.tensor_scalar(wi[:, :, :], ki5[:, :, ID:KIWI], wscale, None, ALU.mult)
            step(v.tensor_scalar(st[0:IH, 56:64], kiwi[ID:KIWI, NP_:T], wscale, None, ALU.mult))
            step(v.tensor_copy(wis[:, 0:64].rearrange("p (b x) -> p b x", x=8)[:, 0, 0:1], st[0:IH, 56:57]))
            for b in range(1, NS):
                last = v.tensor_copy(wis[:, 9 * b:9 * b + 1], st[0:IH, 56 + b:57 + b])
            step(last)
            step(v.tensor_reduce(mu, ki, X, ALU.add))
            step(v.tensor_scalar(mu, mu, 1.0 / ID, None, ALU.mult))
            step(v.tensor_tensor(xc[:, :, :], ki, spread(mu), ALU.subtract))
            step(v.tensor_tensor(sq5[:, :, :], xc[:, :, :], xc[:, :, :], ALU.mult))
            step(v.tensor_reduce(var, sq5[:, :, :], X, ALU.add))
            step(v.tensor_scalar(var, var, 1.0 / ID, EPS, ALU.mult, ALU.add))
            last = v.tensor_copy(t5, var)
            last.then_inc(s_lnv, 1)
            dve.wait_ge(s_lns, 1)
            newton(y5, var, t5)
            step(v.tensor_tensor(xc[:, :, :], xc[:, :, :], spread(y5), ALU.mult))
            step(v.tensor_tensor(xc[:, :, :], xc[:, :, :], per_column(lng[:, 0, :]), ALU.mult))
            dve.wait_ge(s_spill, 16)
            v.tensor_tensor(ki_dup[:, :, 0:ID], xc[:, :, :], per_column(lng[:, 1, :]), ALU.add)
            v.tensor_tensor(ki_dup[:, :, ID:2 * ID], xc[:, :, :], per_column(lng[:, 1, :]), ALU.add).then_inc(s_ln, 1)
            dve.wait_ge(s_ln, 1)
            step(v.memset(qam[:, :], 0.0))

            with dve.Fori(0, 4) as i:
                for u in range(2):
                    t = 2 * i + u
                    scaled(halves(row(qi, t)), TILE_QI + t, (TILE_QI + u) % 2)
            dve.wait_ge(s_kit, 2)
            v.tensor_copy(kit[:, 0:NP_], B[:, 0, :]).then_inc(s_kitd, 1)
            v.tensor_copy(kit[:, NP_:T], B[:, 1, 0:NS]).then_inc(s_kitd, 1)
            dve.wait_ge(s_evac, TILE_QA)
            q4 = qis[:, :, :].rearrange("p b (t two) -> p t b two", two=2)
            v.tensor_copy(q4[:, :, :, 0], qi[0:ID, :, NP_:T])
            v.tensor_copy(q4[:, :, :, 1], qi[ID:P, :, NP_:T]).then_inc(s_qis, 1)
            dve.wait_ge(s_kvo, 64)
            v.memset(score[:, 0, 2 * P:NP_], MASKED)
            v.memset(score[:, 1, 3 * P:NP_], MASKED)
            step(v.memset(kis[:, :, CL + 1:CW], 0.0))
            j = 0
            for b in range(1, QB):
                n = P * (b + 1)
                for h in range(IH):
                    dve.wait_ge(s_rl, j + 1)
                    if h == 0:
                        ins = v.tensor_scalar(score[:, b - 1, 0:n], relu_p[:, j % 2, 0:n], wi[:, b, h:h + 1], None,
                                              ALU.mult)
                    else:
                        dve.wait_ge(s_ic, j)
                        ins = v.scalar_tensor_tensor(out=score[:, b - 1, 0:n], in0=relu_p[:, j % 2, 0:n],
                                                     scalar=wi[:, b, h:h + 1], in1=score[:, b - 1, 0:n],
                                                     op0=ALU.mult, op1=ALU.add)
                    ins.then_inc(s_ic, 1)
                    j += 1
                dve.wait_ge(s_ic, j)
                diag = score[:, b - 1, b * P:(b + 1) * P]
                step(v.tensor_tensor(diag, diag, cmask, ALU.add))
            for b in range(NS):
                dve.wait_ge(s_st, b + 1)
                if b >= 2:
                    dve.wait_ge(s_ss, b - 1)
                v.tensor_copy(kis[:, b % 2, 0:CL], B[0:ID, b % 2, :])
                v.tensor_copy(kis[:, b % 2, CL:CL + 1], kit[0:ID, NP_ + b:NP_ + b + 1]).then_inc(s_sk, 1)
            dve.wait_ge(s_sw, NS)
            v.tensor_copy(halves(score_s[:, :]), G[0:NS, 0:2, 0:257]).then_inc(s_scs, 1)
            dve.wait_ge(s_scs, 1)
            step(v.memset(score_s[:, CL + 1:CW], MASKED))

            dve.wait_ge(s_rst, 16)
            dve.wait_ge(s_rso, 16)
            with step.loop(4, 4 * 4 * 2) as i:
                def take(scores, n_rows):
                    for _ in range(TOPK // 8 // 4):
                        m8 = st[0:n_rows, 48:56]
                        step(v.max(m8, scores))
                        v.tensor_copy(st[:, 65:66], st[:, 64:65])
                        step(v.match_replace(scores, m8, scores, TAKEN))
                        v.tensor_copy(st[:, 65:66], st[:, 64:65])

                for u in range(2):
                    take(score[:, 2 * u, :] if u == 0 else score[:, 2, :], P)
                    take(score[:, 1, :] if u == 0 else score_s[:, :], P if u == 0 else NS)
                    t = 2 * i + u
                    scaled(halves(row(qa, t)), TILE_QA + t, (TILE_QA + u) % 2)
            v.tensor_scalar(score_s[:, :], score_s[:, :], TAKEN, MASKED, ALU.not_equal, ALU.mult).then_inc(s_ams, 1)
            v.memset(kt_b[:, :, CL + 1:CW], 0.0)
            dve.wait_ge(s_evac, TILE_HEAD)
            v.tensor_copy(qam[:, :].rearrange("p (b x) -> p b x", x=72)[:, :, 0:NH],
                          qa[:, :, NP_:T].rearrange("p h b -> p b h")).then_inc(s_qam, 1)
            step(v.tensor_scalar(am[:, :, :], score[:, :, :], TAKEN, MASKED, ALU.not_equal, ALU.mult))
            scale = P ** -0.5
            dve.wait_ge(s_ax, 1)
            step(v.tensor_copy(halves(am_s[:, :]), B[0:64, 0:2, 0:257]))
            dve.wait_ge(s_aq, NS)
            step(v.scalar_tensor_tensor(out=halves(p_s[:, :]), in0=B[0:64, 2:4, 0:257], scalar=scale,
                                        in1=halves(am_s[:, :]), op0=ALU.mult, op1=ALU.add))
            v.tensor_reduce(st[0:64, 42:43], p_s[:, :], X, ALU.max, negate=True).then_inc(s_nms, 1)
            dve.wait_ge(s_exps, 1)
            step(v.reciprocal(st[0:64, 44:45], st[0:64, 43:44]))
            v.tensor_scalar(p_s[:, :], p_s[:, :], st[0:64, 44:45], None, ALU.mult).then_inc(s_ps, 1)
            dve.wait_ge(s_ps, 1)
            v.tensor_scalar(diag_s[:, :], ident[0:64, 0:64], p_s[:, CL:CL + 1], None, ALU.mult).then_inc(s_dg, 1)
            dve.wait_ge(s_apt, 1)
            v.tensor_copy(pt_s[:, :, :], B[:, 0, 0:256].rearrange("p (k n) -> p k n", n=64)).then_inc(s_xd, 1)
            dve.wait_ge(s_apt, 2)
            v.tensor_copy(pown_s[:, :], B[0:NS, 1, 0:64]).then_inc(s_xd, 1)
            dve.wait_ge(s_so, 1)
            v.tensor_copy(mix[:, 0:NH, NP_:T], B[:, 2, 0:64].rearrange("p (b h) -> p h b", h=NH)).then_inc(s_head, 1)

            with step.loop(NH, 12) as i:
                m0, e0 = TILE_HEAD + 4 * i, 24 * i

                def full(e):
                    dve.wait_ge(s_xp, e0 + e + 1)
                    return e % 4

                def rotate(out, m, p, s_out, nth, c):
                    dve.wait_ge(s_used, 2 * m + 2)
                    dve.wait_ge(s_swap, 2 * i + nth)
                    v.scalar_tensor_tensor(out=halves(out), in0=pair(p), scalar=c, in1=halves(cs[:, 0, :]),
                                           op0=ALU.mult, op1=ALU.mult)
                    v.scalar_tensor_tensor(out=t2[:, :], in0=t2[:, :], scalar=c, in1=cs[:, 1, :],
                                           op0=ALU.mult, op1=ALU.mult).then_inc(s_evac, 1)
                    dve.wait_ge(s_evac, m + 1)
                    v.tensor_tensor(out, out, t2[:, :], ALU.add).then_inc(s_out, 1)

                v.tensor_copy(st[:, 37:41], zeta[:, :, one(i)].rearrange("p k o -> p (k o)"))
                step(v.tensor_copy(st[:, 41:42], gamma[:, one(i)]))
                v.tensor_copy(qc[:, :], row(qa, i)[:, 0:NP_]).then_inc(s_qc, 1)
                scaled(halves(rv[:, :]), m0, TILE_HEAD % 2)
                v.tensor_copy(vtok_r[:, :, :], B[:, full(0), :].rearrange("p (k d) -> p k d", d=P)).then_inc(s_xd, 1)
                v.tensor_copy(vs_tok[:, :], B[0:NS, full(1), 0:P]).then_inc(s_xd, 1)
                for b in range(QB):
                    n = slice(QOFF[b], QOFF[b] + P * (b + 1))
                    x = full(2 + b)
                    v.scalar_tensor_tensor(out=p_h[:, n], in0=B[:, x, 0:P * (b + 1)], scalar=scale,
                                           in1=cmask if b == 0 else am[:, b - 1, 0:P * (b + 1)],
                                           op0=ALU.mult, op1=ALU.add).then_inc(s_xd, 1)
                    dve.wait_ge(s_xd, e0 + TAKEN0 + b + 3)
                    v.tensor_reduce(st[:, 25 + b:26 + b], p_h[:, n], X, ALU.max, negate=True).then_inc(s_nm, 1)
                for b in range(QB):
                    n = slice(QOFF[b], QOFF[b] + P * (b + 1))
                    dve.wait_ge(s_exp, 4 * i + b + 1)
                    step(v.reciprocal(st[:, 33 + b:34 + b], st[:, 29 + b:30 + b]))
                    last = v.tensor_scalar(p_h[:, n], p_h[:, n], st[:, 33 + b:34 + b], None, ALU.mult)
                last.then_inc(s_pn, 1)
                rotate(rq[:, :], m0 + 1, (TILE_HEAD + 1) % 2, s_rq, 1, 1.0)
                for k in range(QB):
                    n = NP_ - k * P
                    v.tensor_copy(pt_h[:, KOFF[k]:KOFF[k] + n], B[:, full(6 + k), 0:n]).then_inc(s_xd, 1)
                rotate(rk[:, :], m0 + 2, TILE_HEAD % 2, s_rk, 2, P ** -0.5)
                v.tensor_copy(row(mix, i)[:, 0:NP_], B[:, full(10), :]).then_inc(s_xd, 1)
                dve.wait_ge(s_dh, 16 * i + 16)
                for k in range(QB):
                    n = NP_ - k * P
                    v.tensor_tensor(sd_h[:, KOFF[k]:KOFF[k] + n], B[:, full(11 + k), 0:n], dh[:, 0:n], ALU.mult
                                    ).then_inc(s_xd, 1)
                dve.wait_ge(s_rst, 16 * i + 16)
                v.tensor_tensor(ktok[:, :, :], B[:, full(15), :].rearrange("p (k d) -> p k d", d=P),
                                st[:, 37:41].unsqueeze(2).to_broadcast([P, QB, P]), ALU.mult).then_inc(s_xd, 1)
                v.tensor_copy(ks_tok[:, :], B[0:NS, full(16), 0:P]).then_inc(s_xd, 1)
                v.tensor_tensor(vbd[:, :, :], vs_tok[:, :].unsqueeze(1).to_broadcast([NS, NS, P]),
                                ident[0:NS, 0:NS].unsqueeze(2).to_broadcast([NS, NS, P]), ALU.mult).then_inc(s_vbd, 1)
                scaled(halves(rg[:, :]), m0 + 3, (TILE_HEAD + 1) % 2)
                dve.wait_ge(s_rs, 16 * i + 16)
                for j in range(2):
                    r4 = rs[:, 4 * j:4 * j + 4, :]
                    v.scalar_tensor_tensor(out=r4, in0=r4, scalar=st[:, 41:42],
                                           in1=B[:, full(17 + j), :].rearrange("p (b e) -> p b e", e=P),
                                           op0=ALU.mult, op1=ALU.add).then_inc(s_xd, 1)
                v.tensor_copy(ro[:, 0:NP_], B[:, full(19), :]).then_inc(s_xd, 1)
                v.tensor_copy(rst[:, :], B[:, full(20), 0:P]).then_inc(s_xd, 1)
                v.tensor_copy(ro[:, NP_:T], B[:, full(21), 0:NS]).then_inc(s_xd, 1)
                for n, cols in enumerate((slice(0, NP_), slice(NP_, T))):
                    v.tensor_scalar(rv[:, cols], B[:, full(22 + n), 0:cols.stop - cols.start], 1.0 / P, EPS,
                                    ALU.mult, ALU.add).then_inc(s_xd, 1)
                dve.wait_ge(s_th, i + 1)
                step(v.scalar_tensor_tensor(out=rg[:, :], in0=t2[:, :], scalar=1.0, in1=rg[:, :],
                                            op0=ALU.add, op1=ALU.mult))
                dve.wait_ge(s_hs, i + 1)
                newton(rk[:, :], rv[:, :], rq[:, :])
                step(v.tensor_tensor(rk[:, :], rk[:, :], ro[:, :], ALU.mult))
                v.scalar_tensor_tensor(out=row(mix, i + NH), in0=rk[:, :], scalar=0.5, in1=rg[:, :],
                                       op0=ALU.mult, op1=ALU.mult).then_inc(s_head, 1)

            for k in range(NH, KT):
                dve.wait_ge(s_t1h, k + 1)
                v.tensor_tensor(a_lo[:, k, :], mix[:, k, :], a_hi[:, k, :].bitcast(F32), ALU.subtract
                                ).then_inc(s_t1, 1)
            v.memset(ssum[:, :], 0.0).then_inc(s_n2, 1)
            dve.wait_ge(s_xb, 16)
            with step.loop(KT // 2, 2) as i:
                for u in range(2):
                    t = 2 * i + u
                    m = TILE_OUT + t
                    dve.wait_ge(s_used, 2 * m + 2)
                    xt = row(xr, t)
                    v.tensor_tensor(halves(xt), pair((TILE_OUT + u) % 2), halves(xt), ALU.add).then_inc(s_evac, 1)
                    dve.wait_ge(s_evac, m + 1)
                    step(v.tensor_tensor(sq[:, :], xt, xt, ALU.mult))
                    dve.wait_ge(s_n2, t + 1)
                    v.tensor_tensor(ssum[:, :], ssum[:, :], sq[:, :], ALU.add).then_inc(s_n2, 1)

            def inverse_rms(s_m, s_v, s_s, between=None):
                dve.wait_ge(s_m, 1)
                v.tensor_scalar(halves(nv[:, :]), B[:, 0:2, 0:HT], 1.0 / D, EPS, ALU.mult, ALU.add).then_inc(s_v, 1)
                if between:
                    between()
                dve.wait_ge(s_s, 1)
                newton(ny[:, :], nv[:, :], u1[:, :])
                step(v.tensor_copy(rb[:, :], ny[:, :]))

            def split_h2():
                for k in range(KT):
                    dve.wait_ge(s_t2h, k + 1)
                    v.scalar_tensor_tensor(out=a_lo[:, k, :], in0=xr[:, k, :], scalar=g2[:, k:k + 1],
                                           in1=a_hi[:, k, :].bitcast(F32), op0=ALU.mult, op1=ALU.subtract
                                           ).then_inc(s_t2, 1)

            inverse_rms(s_n2m, s_n2v, s_n2s, split_h2)

            def hidden(m0, n0):
                with step.loop(CH // 2, 4) as i:
                    for u in range(2):
                        t = 2 * i + u
                        dve.wait_ge(s_used, n0 + 4 * i + 2 * u + 2)
                        v.scalar_tensor_tensor(out=halves(u1[:, :]), in0=pair((TILE_MLP + u) % 2), scalar=0.0,
                                               in1=halves(rb[:, :]), op0=ALU.max, op1=ALU.mult).then_inc(s_evac, 1)
                        dve.wait_ge(s_evac, m0 + t + 1)
                        step(v.tensor_tensor(u2[:, :], u1[:, :], u1[:, :], ALU.mult))
                        step(v.tensor_copy(row(b_hi, t), u2[:, :]))
                        v.tensor_tensor(row(b_lo, t), u2[:, :], row(b_hi, t).bitcast(F32), ALU.subtract
                                        ).then_inc(s_b, 1)

            def add_down(n0, t, u, xt):
                dve.wait_ge(s_used, n0 + 16 + t + 1)
                v.tensor_tensor(halves(xt), pair((TILE_MLP + u) % 2), halves(xt), ALU.add).then_inc(s_evac, 1)

            with step.loop(NCHUNK - 1, 2 * CH) as c:
                m0, n0 = TILE_MLP + 24 * c, unit_of(TILE_MLP) + 32 * c
                hidden(m0, n0)
                with dve.Fori(0, KT // 4) as i:
                    for u in range(4):
                        t = 4 * i + u
                        add_down(n0, t, u, row(xr, t))
            hidden(LAST_TILE, LAST_UNIT)
            for f in range(KT):
                xt = xr[:, f, :]

                def scaled_tile():
                    if f >= 2:
                        dve.wait_ge(s_yx, f - 1)
                    v.tensor_scalar(yt[:, f % 2, :], xt, gf[:, f:f + 1], None, ALU.mult).then_inc(s_yt, 1)

                add_down(LAST_UNIT, f, f % 2, xt)
                dve.wait_ge(s_evac, LAST_TILE + CH + f + 1)
                if f < KT - 1:
                    scaled_tile()
                    step(v.tensor_tensor(sq[:, :] if f else ssum[:, :], xt, xt, ALU.mult))
                    if f:
                        step(v.tensor_tensor(ssum[:, :], ssum[:, :], sq[:, :], ALU.add))
                else:
                    v.tensor_tensor(sq[:, :], xt, xt, ALU.mult).then_inc(s_nf, 1)
                    scaled_tile()
            dve.wait_ge(s_nfm, 1)
            step(v.tensor_scalar(st[:, 70:74], G[:, 2, 0:4], 1.0 / D, EPS, ALU.mult, ALU.add))
            v.tensor_scalar(st[0:NS, 74:75], G[0:NS, 2, 4:5], 1.0 / D, EPS, ALU.mult, ALU.add).then_inc(s_nfv, 1)
            dve.wait_ge(s_nfs, 1)
            newton(st[:, 75:80], st[:, 70:75], st[:, 80:85])
            v.tensor_copy(st[:, 85:86], st[:, 75:76]).then_inc(s_rn, 1)
            dve.wait_ge(s_ye, KT)
            for s, _, tb, half in PIECES:
                if s == 0:
                    x = out_t[:, tb, half * D // 2:(half + 1) * D // 2]
                    v.tensor_scalar(x, x, st[:, 75 + tb:76 + tb], None, ALU.mult).then_inc(s_fin[0], 1)


_INS = ['x_prompt', 'x_sample', 'cache_k', 'cache_v', 'cache_idx_k', 'state_ret', 'page_table', 'norm1_g', 'w_in',
        'idx_k_norm_g', 'idx_k_norm_b', 'w_out', 'norm2_g', 'w_up', 'w_down', 'final_norm_g']
_OUTS = [(1, 512, 2048), (8, 1, 2048), (1, 512, 128), (1, 512, 128), (1, 512, 64), (1, 8, 128, 128),
         (8, 1, 128), (8, 1, 128), (8, 1, 64), (8, 8, 128, 128)]


def shape_constants():
    import numpy as np
    lg = np.log1p(-np.exp2(-5.0 - np.arange(NH, dtype=np.float64)))
    p = np.arange(P)
    const = np.zeros((P, 368), np.float32)
    const[:, 0:P] = np.eye(P)
    const[:, P:2 * P] = np.where(p[None, :] <= p[:, None], 0.0, MASKED)
    const[:, 256:288] = np.exp((NP_ - 1.0 - (p[:, None, None] + P * np.arange(QB)[None, :, None]))
                               * lg[None, None, :]).reshape(P, 32)
    const[:, 288:296] = np.exp(lg)[None, :]
    const[0:NS, 296:360] = np.repeat(np.eye(NS), 8, axis=1)
    const[0:64, 360:368] = np.repeat(np.eye(NS), 8, axis=0)
    diff = np.arange(NP_)[None, :] - p[:, None]
    decay = np.where(diff[None] >= 0, np.exp(np.maximum(diff, 0)[None] * lg[:, None, None]), 0.0).astype(np.float32)
    inv = (np.float32(10000.0) ** (-np.arange(64, dtype=np.float32) / np.float32(64))).astype(np.float32)
    pos = np.concatenate([np.arange(NP_), np.full(NS, CL)]).astype(np.float32)
    ang = (inv[:, None] * pos[None, :]).astype(np.float32)
    cos, sin = np.cos(ang), np.sin(ang)
    rotary = np.stack([np.concatenate([cos, cos]), np.concatenate([-sin, sin])], axis=1).astype(np.float32)
    return {"shape_const": const, "shape_rotary": rotary, "shape_decay": decay}


def kernel(**inputs):
    import numpy as _np
    import concourse.bacc as _bacc
    from concourse import mybir as _mybir
    from concourse.bass_utils import run_bass_kernel_spmd as _run

    nc = _bacc.Bacc("TRN2", target_bir_lowering=False, num_devices=1)
    arrays, args = {}, []
    for name in _INS:
        arrays[f"in_{name}_dram"] = _np.ascontiguousarray(inputs[name])
    for name, a in shape_constants().items():
        arrays[f"{name}_dram"] = a
    for name, a in arrays.items():
        args.append(nc.dram_tensor(name, a.shape, _mybir.dt.from_np(a.dtype), kind="ExternalInput").ap())
    for i, shape in enumerate(_OUTS):
        args.append(nc.dram_tensor(f"out_{i}_dram", shape, _mybir.dt.float32, kind="ExternalOutput").ap())
    build(nc, *args)
    r = _run(nc, [arrays], core_ids=[0])
    return tuple(r.results[0][f"out_{i}_dram"] for i in range(len(_OUTS)))
```

```python
from contextlib import ExitStack, contextmanager

import concourse.bass as bass
from concourse import mybir

P = 128
D = 2048
KT = D // P
NP_, NS = 512, 8
T = NP_ + NS
HT = T // 2
QB = NP_ // P
NH = 8
IH, ID = 16, 64
TOPK = 128
PAGES = 4
CL = PAGES * P
CW = CL + 2
DFF = 4 * D
CH = 8
NCHUNK = DFF // (CH * P)
EPS = 1e-6
MASKED = -1e30
TAKEN = -3.0e38
OFF_QA, OFF_KA, OFF_VA, OFF_QI = 0, 1024, 1152, 1280
OFF_KI, OFF_QR, OFF_KR, OFF_VR, OFF_GR = 2304, 2384, 3408, 4432, 5456
KIWI = ID + IH
RING = 4

TILE_QI, TILE_QA, TILE_VA, TILE_HEAD, TILE_OUT, TILE_MLP = 2, 10, 18, 19, 51, 67
TAKEN0 = 2
UNITS = 2 * TILE_MLP + NCHUNK * (2 * CH + KT)
LAST_TILE, LAST_UNIT = TILE_MLP + 24 * (NCHUNK - 1), UNITS - 2 * CH - KT

PIECES = [(0, 1, 0, 0), (1, 1, 2, 1), (0, 2, 0, 1), (0, 3, 1, 0), (1, 2, 3, 0), (0, 4, 1, 1), (0, 5, 2, 0), (1, 3, 3, 1)]
ACT_PIECES = 3

F32, F32R, BF16, I32 = mybir.dt.float32, mybir.dt.float32r, mybir.dt.bfloat16, mybir.dt.int32
ALU = mybir.AluOpType
ACT = mybir.ActivationFunctionType
X = mybir.AxisListType.X


def unit_of(tile):
    return 2 * tile


class Chain:

    def __init__(self, eng, sem):
        self.eng, self.sem, self.n, self.at = eng, sem, 0, 0

    def __call__(self, ins):
        ins.then_inc(self.sem, 1)
        self.n += 1
        self.eng.wait_ge(self.sem, self.at + self.n)

    def mark(self, ins):
        ins.then_inc(self.sem, 1)
        self.n += 1
        return self.n

    def wait(self, n):
        self.eng.wait_ge(self.sem, self.at + n)

    @contextmanager
    def loop(self, count, per):
        at, n = self.at, self.n
        with self.eng.Fori(0, count) as i:
            self.at, self.n = at + i * per, n
            yield i
            assert self.n - n == per, f"{self.n - n} steps in a round, not {per}"
        self.at, self.n = at, n + count * per


def build(nc, x_prompt, x_sample, cache_k, cache_v, cache_idx_k, state_ret, page_table, norm1_g, w_in,
          idx_k_norm_g, idx_k_norm_b, w_out, norm2_g, w_up, w_down, final_norm_g, shapes_const, rotary, decay,
          y_p, y_s, k_p, v_p, ik_p, rs_p, k_s, v_s, ik_s, rs_s):
    ctx = ExitStack()
    with ctx:
        BASE = 16512

        def at(name, offset, shape, dt=F32):
            return nc.alloc_sbuf_tensor_at(name, shape, dt, offset=BASE + offset)

        def sem(name):
            return ctx.enter_context(nc.semaphore(name))

        a_hi = at("a_hi", 0, [P, KT, T], F32R)
        a_lo = at("a_lo", 33280, [P, KT, T], F32R)
        w_raw = at("w_raw", 66560, [P, 2, 8, P])
        w_hi = at("w_hi", 74752, [P, RING, 8, P], F32R)
        w_lo = at("w_lo", 91136, [P, RING, 8, P], F32R)
        M0 = 107520
        mix = at("mix", M0, [P, KT, T])
        b_hi = at("b_hi", M0, [P, CH, T], F32R)
        b_lo = at("b_lo", M0 + 16640, [P, CH, T], F32R)
        x_in = at("x_in", M0, [P, QB, D])
        kpages = at("kpages", M0, [P, NS * PAGES, P])
        vpages = at("vpages", M0 + 16640, [P, NS * PAGES, P])
        R0 = 140800
        xr = at("xr", R0, [P, KT, T])
        qi = at("qi", R0, [P, 8, T])
        qa = at("qa", R0 + 16640, [P, NH, T])
        ipages = at("ipages", R0 + 16640, [P, NS * PAGES, ID])
        relu_p = at("relu_p", R0 + 16640 + 8192, [P, 2, NP_])
        ki_dup = at("ki_dup", R0 + 16640 + 12288, [P, 5, 2 * ID])
        kt_b = at("kt_b", R0, [P, 2, CW])
        am_s = at("am_s", R0 + 4128, [64, CW])
        p_s = at("p_s", R0 + 6208, [64, CW])
        pt_s = at("pt_s", R0 + 8288, [P, PAGES, 64])
        diag_s = at("diag_s", R0 + 9312, [64, 64])
        pown_s = at("pown_s", R0 + 9568, [NS, 64])
        vt = at("vt", R0 + 9856, [P, T])
        relu_s = at("relu_s", R0, [P, 2, 257])
        rq = at("rq", R0, [P, T])
        rk = at("rk", R0 + 2080, [P, T])
        rv = at("rv", R0 + 4160, [P, T])
        rg = at("rg", R0 + 6240, [P, T])
        dh = at("dh", R0 + 8320, [P, NP_])
        ro = at("ro", R0 + 10368, [P, T])
        rs = at("rs", R0 + 12448, [P, NS, P])

        o = 174080
        small = {}
        for name, shape, dt, nbytes in (
                ("const", [P, 368], F32, 1472), ("ones", [P, P], F32, 512), ("gcol", [P, 48], F32, 192),
                ("rb", [P, T], F32, 2080), ("kt", [P, T], F32, 2080), ("vtok", [P, QB, P], F32, 2048),
                ("vs", [NS, P], F32, 512), ("kit", [P, T], F32, 2080), ("wi", [P, 5, IH], F32, 320),
                ("am", [P, QB - 1, NP_], BF16, 3072), ("st", [P, 96], F32, 384), ("pt_i", [1, 32], I32, 128)):
            if name == "am":
                AM_OFFSET = o - 174080
            small[name] = at(name, o, shape, dt)
            o += nbytes
        const, ones, gcol, rb, kt, vtok, vs, kit, wi, am, st, pt_i = small.values()
        assert o <= 188960
        kit_o = at("kit_o", 174080 + AM_OFFSET, [P, NP_])
        cs = at("cs", 188960, [P, 2, T])
        H0 = 193120
        xs_in = at("xs_in", H0, [NS, D])
        graw = at("graw", H0 + 8192, [48, P])
        lng = at("lng", H0 + 8704, [P, 2, ID])
        rdiag = at("rdiag", H0 + 11296, [P, 5, P])
        kout = at("kout", H0, [P, QB, P])
        kout_s = at("kout_s", H0 + 2048, [NS, P])
        zw = at("zw", H0 + 5120, [NS, NS, IH])
        kiwi = at("kiwi", H0 + 11296, [KIWI, T])
        ki5 = at("ki5", H0 + 13376, [P, 5, KIWI])
        xc = at("xc", H0 + 14976, [P, 5, ID])
        sq5 = at("sq5", H0 + 16256, [P, 5, ID])
        score = at("score", H0, [P, QB - 1, NP_])
        score_s = at("score_s", H0 + 6144, [NS, CW])
        qam = at("qam", H0 + 8224, [P, NS * 72])
        kis = at("kis", H0 + 10528, [P, 2, 2, 257])
        qis = at("qis", H0 + 14656, [P, NS * 144])
        wis = at("wis", H0 + 19264, [P, NS])
        p_h = at("p_h", H0, [P, 1280])
        sd_h = at("sd_h", H0, [P, 1280])
        pt_h = at("pt_h", H0 + 5120, [P, 1280])
        vbd = at("vbd", H0 + 5120, [NS, NS, P])
        ktok = at("ktok", H0 + 10240, [P, QB, P])
        rst = at("rst", H0 + 10240, [P, P])
        ks_tok = at("ks_tok", H0 + 12288, [NS, P])
        vtok_r = at("vtok_r", H0 + 12800, [P, QB, P])
        vs_tok = at("vs_tok", H0 + 14848, [NS, P])
        qc = at("qc", H0 + 15360, [P, NP_])
        t2 = at("t2", H0 + 17408, [P, T])
        sq = at("sq", H0, [P, T])
        ssum = at("ssum", H0 + 2080, [P, T])
        u1 = at("u1", H0 + 4160, [P, T])
        u2 = at("u2", H0 + 6240, [P, T])
        nv = at("nv", H0 + 8320, [P, T])
        ny = at("ny", H0 + 10400, [P, T])
        yt = at("yt", H0 + 12480, [P, 2, T])
        out_t = at("out_t", 0, [P, QB, D])
        out_s = at("out_s", 33280, [NS, D])

        ident, cmask = const[:, 0:P], const[:, P:2 * P]
        zeta, gamma = const[:, 256:288].rearrange("p (k h) -> p k h", h=NH), const[:, 288:296]
        expand, fold = const[0:NS, 296:360], const[0:64, 360:368]
        g1, g2, gf = gcol[:, 0:16], gcol[:, 16:32], gcol[:, 32:48]

        G = ctx.enter_context(nc.psum_tensor("product", [P, 4, 512], F32))
        B = ctx.enter_context(nc.psum_tensor("banks", [P, 4, 512], F32))

        def pair(p, rows=P):
            return G[0:rows, 2 * p:2 * p + 2, 0:HT]

        def halves(x):
            return x.rearrange("p (a b) -> p a b", a=2)

        def one(i):
            return bass.ds(i, 1)

        def row(x, i):
            return x[:, one(i), :].rearrange("p o n -> p (o n)")

        QOFF = [0, 128, 384, 768]
        KOFF = [0, 512, 896, 1152]
        xt_dram = nc.dram_tensor("x_transposed", (P, KT * T), F32).ap()

        s_raw = [sem(f"weights_loaded_{u}") for u in range(2)]
        s_hi, s_lo, s_used = sem("weights_hi"), sem("weights_lo"), sem("weights_used")
        s_evac = sem("tile_taken")
        s_x = [sem(f"x_loaded_{u}") for u in range(5)]
        (s_cst, s_rot, s_gr, s_lng, s_pt, s_set, s_ssq, s_gt, s_gc, s_xt, s_xr, s_a0h, s_a0, s_spill, s_var, s_sqrt,
         s_diag, s_rbm, s_rbd, s_y, s_yd, s_kvo, s_lnv, s_lns, s_ln, s_kit, s_kitd, s_is, s_rl, s_ic) = (
            sem(n) for n in (
                "consts_loaded", "rotary_loaded", "gains_loaded", "ln_loaded", "pages_listed", "set_up",
                "squares_summed", "gains_turned", "gains_ready", "x_turned", "xr_ready", "a0_hi", "a0_ready", "x_spilled",
                "var_ready", "sqrt_ready", "diag_ready", "rms_spread", "rms_ready", "kv_turned", "kv_taken",
                "kv_stored", "ln_var", "ln_sqrt", "ln_done", "kit_turned", "kit_ready",
                "index_dots", "index_relu", "index_added"))
        (s_pi, s_pk, s_pv, s_qis, s_st, s_sk, s_ss, s_sr, s_sw, s_scs, s_ams, s_qam, s_at, s_ak, s_aq, s_ax,
         s_nms, s_exps, s_ps, s_dg, s_apt, s_so) = (
            sem(n) for n in (
                "ipages_loaded", "kpages_loaded", "vpages_loaded", "sample_iq", "ipages_turned", "sample_ik",
                "sample_dots", "sample_relu", "sample_weighed", "sample_scores", "sample_mask", "sample_q",
                "kpages_turned", "sample_k", "sample_qk", "mask_spread", "sample_max", "sample_exp", "sample_p",
                "own_diag", "sample_p_turned", "sample_o"))
        (s_qc, s_swap, s_rq, s_rk, s_xp, s_xd, s_nm, s_exp, s_pn, s_dh, s_rs, s_rst, s_rso, s_rv, s_vbd, s_sq,
         s_th, s_hs, s_head) = (
            sem(n) for n in (
                "head_q", "halves_swapped", "ret_q", "ret_k", "head_bank_full", "head_bank_taken", "head_max",
                "head_exp", "head_p", "decay_loaded", "state_loaded", "prompt_state_stored",
                "sample_state_stored", "ret_v", "values_diagonal", "ret_squared", "gate_tanh",
                "ret_sqrt", "head_done"))
        (s_t1h, s_t1p, s_t1, s_xb, s_n2, s_n2m, s_n2v, s_n2s, s_rb2, s_t2h, s_t2, s_b, s_nf, s_nfm, s_nfv, s_nfs, s_yt,
         s_yx, s_ye, s_out, s_rn, s_chain) = (
            sem(n) for n in (
                "mixed_hi", "mixed_lo_pool", "mixed_lo", "x_back", "sum2", "sum2_spread", "var2", "sqrt2", "rms2_ready", "h2_hi",
                "h2_lo", "hidden_ready", "sumf", "sumf_spread", "varf", "sqrtf", "y_scaled", "y_turned",
                "y_taken", "y_stored", "rmsf_ready", "vector_step"))

        s_fin = [sem("rows_scaled_vector"), sem("rows_scaled_scalar")]

        block = ctx.enter_context(nc.Block())

        @block.sync
        def _(sp):
            def load_unit(slot, n, src, cols=P):
                if not isinstance(n, int) or n >= 2:
                    sp.wait_ge(s_lo, n - 1)
                sp.dma_start(w_raw[:, slot, :, 0:cols], src.rearrange("(k p) c -> p k c", p=P)).then_inc(s_raw[slot], 16)

            def rows(w, half, col, cols=P):
                return w[half * 1024:half * 1024 + 1024, bass.ds(col, cols)]

            sp.dma_start(const[:, :], shapes_const).then_inc(s_cst, 16)
            sp.dma_start(xs_in[:, :], x_sample.rearrange("b o d -> (b o) d")).then_inc(s_x[4], 16)
            for tb in range(QB):
                if tb == QB - 1:
                    load_unit(0, 0, rows(w_in, 0, OFF_KA))
                sp.dma_start(x_in[:, tb, :], x_prompt[0, tb * P:(tb + 1) * P, :]).then_inc(s_x[tb], 16)
            load_unit(1, 1, rows(w_in, 1, OFF_KA))
            sp.dma_start(pt_i[:, :], page_table.rearrange("b j -> (b j)")[None, :]).then_inc(s_pt, 16)
            load_unit(0, 2, rows(w_in, 0, OFF_KI, KIWI), KIWI)
            load_unit(1, 3, rows(w_in, 1, OFF_KI, KIWI), KIWI)
            sp.wait_ge(s_pt, 16)

            def qi_unit(i, u):
                load_unit(u % 2, unit_of(TILE_QI) + 4 * i + u, rows(w_in, u % 2, OFF_QI + 256 * i + P * (u // 2)))

            def load_page(j, *caches):
                page = sp.value_load(pt_i[0:1, one(j)])
                for dst, cache, s in caches:
                    sp.dma_start(dst[:, one(j), :], cache[one(page), :, :].rearrange("a p d -> p a d")).then_inc(s, 16)

            qi_unit(0, 0)
            qi_unit(0, 1)
            sp.wait_ge(s_spill, 16)
            sp.wait_ge(s_a0, KT)
            qi_unit(0, 2)
            qi_unit(0, 3)
            with sp.Fori(1, 4) as i:
                for u in range(4):
                    qi_unit(i, u)
                    for v in range(3 if u < 2 else 2):
                        load_page(10 * i + (0, 3, 6, 8)[u] + v - 10, (ipages, cache_idx_k, s_pi))
            for j in range(30, NS * PAGES):
                load_page(j, (ipages, cache_idx_k, s_pi))
            with sp.Fori(0, 4) as i:
                for u in range(4):
                    load_unit(u % 2, unit_of(TILE_QA) + 4 * i + u, rows(w_in, u % 2, OFF_QA + 256 * i + P * (u // 2)))
                    for v in range(2):
                        load_page(8 * i + 2 * u + v, (kpages, cache_k, s_pk), (vpages, cache_v, s_pv))
            load_unit(0, unit_of(TILE_VA), rows(w_in, 0, OFF_VA))
            load_unit(1, unit_of(TILE_VA) + 1, rows(w_in, 1, OFF_VA))
            with sp.Fori(0, NH) as i:
                for u in range(8):
                    off = (OFF_VR, OFF_QR, OFF_KR, OFF_GR)[u // 2]
                    load_unit(u % 2, unit_of(TILE_HEAD) + 8 * i + u, rows(w_in, u % 2, off + P * i))
                    if u == 4:
                        sp.wait_ge(s_head, i + 1)
                        sp.dma_start(dh[:, :], decay[one(i), :, :].rearrange("a p n -> (a p) n")).then_inc(s_dh, 16)
                        sp.wait_ge(s_rso, 16 * i + 16)
                        sp.dma_start(rs[:, :, :], state_ret[:, one(i), :, :].rearrange("b a d e -> d (b a) e")
                                     ).then_inc(s_rs, 16)
            with sp.Fori(0, KT // 2) as i:
                for u in range(4):
                    load_unit(u % 2, unit_of(TILE_OUT) + 4 * i + u, rows(w_out, u % 2, 256 * i + P * (u // 2)))
            with sp.Fori(0, NCHUNK) as c:
                n0 = unit_of(TILE_MLP) + 32 * c
                with sp.Fori(0, CH // 2) as i:
                    for u in range(4):
                        load_unit(u % 2, n0 + 4 * i + u, rows(w_up, u % 2, 1024 * c + 256 * i + P * (u // 2)))
                with sp.Fori(0, KT // 4) as i:
                    for u in range(4):
                        load_unit(u % 2, n0 + 16 + 4 * i + u,
                                  w_down[bass.ds(1024 * c, 1024), bass.ds(512 * i + P * u, P)])
            sp.wait_ge(s_kvo, 64)
            sp.wait_ge(s_rst, 16 * NH + 16)
            sp.wait_ge(s_rso, 16 * NH + 16)
            for n, (s, count, tb, half) in enumerate(PIECES):
                sp.wait_ge(s_fin[s], count)
                cols = slice(half * D // 2, (half + 1) * D // 2)
                sp.dma_start(y_p[0, tb * P:(tb + 1) * P, cols], out_t[:, tb, cols]).then_inc(s_out, 16)
            sp.wait_ge(s_fin[1], ACT_PIECES + 1)
            sp.dma_start(y_s.rearrange("b o d -> (b o) d"), out_s[:, :]).then_inc(s_out, 16)
            sp.wait_ge(s_out, 16 * (2 * QB + 1))

        @block.gpsimd
        def _(pool):
            def low(n, slot, raw, cols=P):
                pool.wait_ge(s_hi, n + 1)
                pool.wait_ge(s_raw[raw], 16 * (n // 2 + 1) if isinstance(n, int) else 0)
                nc.gpsimd.tensor_tensor(w_lo[:, slot, :, 0:cols], w_raw[:, raw, :, 0:cols],
                                        w_hi[:, slot, :, 0:cols].bitcast(F32), ALU.subtract).then_inc(s_lo, 1)

            for n in range(6):
                low(n, n % RING, n % 2, KIWI if n in (2, 3) else P)
            def low_units(first, last):
                with pool.Fori(0, (last - first) // RING) as i:
                    for u in range(RING):
                        slot, raw = (first + u) % RING, u % 2
                        pool.wait_ge(s_hi, first + 4 * i + u + 1)
                        pool.wait_ge(s_raw[raw], 16 * (2 * i + (first + u) // 2 + 1))
                        nc.gpsimd.tensor_tensor(w_lo[:, slot, :, :], w_raw[:, raw, :, :],
                                                w_hi[:, slot, :, :].bitcast(F32), ALU.subtract).then_inc(s_lo, 1)

            low_units(6, unit_of(TILE_OUT) + 4)
            for k in range(NH):
                pool.wait_ge(s_t1h, k + 1)
                nc.gpsimd.tensor_tensor(a_lo[:, k, :], mix[:, k, :], a_hi[:, k, :].bitcast(F32), ALU.subtract
                                        ).then_inc(s_t1p, 1)
            low_units(unit_of(TILE_OUT) + 4, UNITS)

        @block.tensor
        def _(pe):
            def unit(n, slot, hi, lo, out, first, last, k0=0, cols=P, ready=None, ready_at=0):
                pe.wait_ge(s_lo, n + 1)
                for k in range(8):
                    if ready is not None:
                        if ready is s_t1:
                            pe.wait_ge(*((s_t1p, k0 + k + 1) if k0 + k < NH else (s_t1, k0 + k + 1 - NH)))
                        else:
                            pe.wait_ge(ready, ready_at + k0 + k + 1)
                    for part, (w, a) in enumerate(((w_hi, hi), (w_hi, lo), (w_lo, hi))):
                        for half in range(2):
                            last_mm = nc.tensor.matmul(
                                out[:, half, :], w[:, slot, k, 0:cols], a[:, k0 + k, half * HT:(half + 1) * HT],
                                start=(first and k == 0 and part == 0), stop=(last and k == 7 and part == 2))
                return last_mm

            def tile(m, m_static, n, base_unit, cols=P, ready=None, between=None):
                out = pair(m_static % 2)[0:cols]
                if m_static >= 2:
                    pe.wait_ge(s_evac, m - 1)
                a = unit(n, base_unit % RING, a_hi, a_lo, out, True, False, 0, cols, ready)
                a.then_inc(s_used, 1)
                if between:
                    between()
                b = unit(n + 1, (base_unit + 1) % RING, a_hi, a_lo, out, False, True, 8, cols, ready)
                b.then_inc(s_used, 1)

            def turn(out, x, n):
                return nc.tensor.transpose(out, x, ident[0:n, 0:n])

            def mm(out, lhsT, rhs, start=True, stop=True):
                return nc.tensor.matmul(out, lhsT, rhs, start=start, stop=stop, skip_group_check=True)

            pe.wait_ge(s_cst, 16)
            pe.wait_ge(s_x[4], 16)
            for f in range(KT):
                last = turn(G[:, 0, f * NS:(f + 1) * NS], xs_in[:, f * P:(f + 1) * P], NS)
            last.then_inc(s_xt, 1)
            pe.wait_ge(s_gr, 48)
            turn(G[:, 1, 0:48], graw[:, :], 48).then_inc(s_gt, 1)
            for tb in range(QB):
                pe.wait_ge(s_x[tb], 16)
                for q in range(4):
                    if tb:
                        pe.wait_ge(s_xr, 4 * tb + q - 2)
                    for r in range(4):
                        last = turn(B[:, q, r * P:(r + 1) * P], x_in[:, tb, (4 * q + r) * P:(4 * q + r + 1) * P], P)
                    last.then_inc(s_xt, 1)
            tile(0, 0, 0, 0, ready=s_a0)

            def spread_rms():
                pe.wait_ge(s_diag, 1)
                for tb in range(QB):
                    mm(B[:, 0, tb * P:(tb + 1) * P], ones[:, :], rdiag[:, tb, :])
                mm(B[:, 1, 0:NS], ones[0:NS, :], rdiag[0:NS, 4, 0:NS]).then_inc(s_rbm, 1)

            def turn_tokens(nth, src, rows_, m, b):
                pe.wait_ge(s_evac, m + 1)
                for tb in range(QB):
                    last = turn(B[:, b, tb * rows_:(tb + 1) * rows_], src[:, tb * P:(tb + 1) * P], rows_)
                last.then_inc(s_y, 1)
                turn(B[0:NS, b + 1, 0:rows_], src[:, NP_:T], rows_).then_inc(s_y, 1)

            def turn_kiwi():
                pe.wait_ge(s_rbd, 1)
                turn_tokens(1, kiwi, KIWI, 1, 0)

            def turn_index_keys():
                pe.wait_ge(s_ln, 1)
                pe.wait_ge(s_yd, 4)
                for tb in range(QB):
                    last = turn(B[:, 0, tb * P:(tb + 1) * P], ki_dup[:, tb, :], P)
                last.then_inc(s_kit, 1)
                turn(B[:, 1, 0:NS], ki_dup[0:NS, 4, :], NS)
                turn(B[:, 1, NS:2 * NS], zw[:, :, :].rearrange("b c h -> b (c h)"), NS).then_inc(s_kit, 1)

            def qi_tile(t, **kw):
                tile(TILE_QI + t, TILE_QI + t, unit_of(TILE_QI + t), unit_of(TILE_QI + t), **kw)

            tile(1, 1, 2, 2, KIWI, between=spread_rms)
            qi_tile(0, between=lambda: turn_tokens(0, kt, P, 0, 2))
            qi_tile(1, between=turn_kiwi)
            with pe.Fori(0, 2) as i:
                for u in range(2):
                    tile(TILE_QI + 2 + 2 * i + u, TILE_QI + 2 + u, unit_of(TILE_QI + 2) + 4 * i + 2 * u,
                         unit_of(TILE_QI + 2 + u))
            qi_tile(6)
            qi_tile(7, between=turn_index_keys)

            pe.wait_ge(s_kitd, 2)
            j = 0
            for h in range(IH):
                for b in range(1, QB):
                    if j >= 4:
                        pe.wait_ge(s_rl, j - 3)
                    if b == 1 and h == IH - 2:
                        pe.wait_ge(s_evac, TILE_QA)
                    mm(B[:, j % 4, 0:P * (b + 1)], qi[:, h // 2, b * P:(b + 1) * P],
                       (kit, kit_o)[h % 2][:, 0:P * (b + 1)]).then_inc(s_is, 1)
                    j += 1
            pe.wait_ge(s_pi, 16 * NS * PAGES)
            pe.wait_ge(s_qis, 1)
            for step in range(NS + 2):
                if step < NS:
                    if step >= 2:
                        pe.wait_ge(s_sk, step - 1)
                    for g in range(0, PAGES, 2):
                        last = turn(G[:, step % 2, g // 2 * P:(g // 2 + 1) * P],
                                    ipages[:, PAGES * step + g:PAGES * step + g + 2, :].rearrange("p a d -> p (a d)"), P)
                    last.then_inc(s_st, 1)
                if step >= 2:
                    b = step - 2
                    pe.wait_ge(s_sk, b + 1)
                    for half in range(2):
                        last = mm(G[:, 2 + half, 0:257], qis[:, P * b:P * b + P], kis[:, b % 2, half, :],
                                  start=(b == 0), stop=(b == NS - 1))
                    last.then_inc(s_ss, 1)
            pe.wait_ge(s_rl, j)
            pe.wait_ge(s_sr, 1)
            for half in range(2):
                last = mm(B[0:NS, half, 0:257], wis[:, :], relu_s[:, half, :])
            last.then_inc(s_sw, 1)

            with pe.Fori(0, 4) as i:
                for u in range(2):
                    tile(TILE_QA + 2 * i + u, TILE_QA + u, unit_of(TILE_QA) + 4 * i + 2 * u, unit_of(TILE_QA) + 2 * u)

            pe.wait_ge(s_pk, 16 * NS * PAGES)
            pe.wait_ge(s_scs, 1)
            for step in range(NS + 1):
                if step < NS:
                    if step >= 2:
                        pe.wait_ge(s_ak, step - 1)
                    for g in range(PAGES):
                        last = turn(B[:, step % 2, g * P:(g + 1) * P], kpages[:, PAGES * step + g, :], P)
                    last.then_inc(s_at, 1)
                if step >= 1:
                    b = step - 1
                    if b == 0:
                        pe.wait_ge(s_qam, 1)
                    pe.wait_ge(s_ak, b + 1)
                    for half in range(2):
                        last = mm(B[0:64, 2 + half, 0:257], qam[:, 64 * b:64 * b + 64],
                                  kt_b[:, b % 2, 257 * half:257 * half + 257], start=(b == 0), stop=(b == NS - 1))
                    last.then_inc(s_aq, 1)
                if step == 2:
                    pe.wait_ge(s_ams, 1)
                    for half in range(2):
                        last = mm(G[0:64, 2 + half, 0:257], expand, score_s[:, 257 * half:257 * half + 257])
                    last.then_inc(s_ax, 1)

            def turn_sample_probs():
                pe.wait_ge(s_ps, 1)
                for g in range(PAGES):
                    last = turn(B[:, 0, g * 64:(g + 1) * 64], p_s[:, g * P:(g + 1) * P], 64)
                last.then_inc(s_apt, 1)
                pe.wait_ge(s_dg, 1)
                mm(B[0:NS, 1, 0:64], fold, diag_s[:, :]).then_inc(s_apt, 1)

            tile(TILE_VA, TILE_VA, unit_of(TILE_VA), unit_of(TILE_VA), between=turn_sample_probs)
            pe.wait_ge(s_xd, TAKEN0)
            pe.wait_ge(s_pv, 16 * NS * PAGES)
            for b in range(NS):
                for g in range(PAGES):
                    mm(B[:, 0, NH * b:NH * b + NH], vpages[:, PAGES * b + g, :], pt_s[:, g, NH * b:NH * b + NH],
                       start=(g == 0), stop=(g == PAGES - 1))
            turn_tokens(2, vt, P, TILE_VA, 2)
            pe.wait_ge(s_yd, 6)
            mm(B[:, 1, 0:64], vs[:, :], pown_s[:, :]).then_inc(s_so, 1)

            with pe.Fori(0, NH) as i:
                m0, n0 = TILE_HEAD + 4 * i, unit_of(TILE_HEAD) + 8 * i
                e0 = 24 * i

                def head_tile(u, between=None):
                    tile(m0 + u, TILE_HEAD + u, n0 + 2 * u, unit_of(TILE_HEAD) + 2 * u, between=between)

                def fill(e):
                    pe.wait_ge(s_xd, e0 + TAKEN0 + max(e - 3, 0))
                    return e % 4

                def values_and_scores():
                    pe.wait_ge(s_evac, m0 + 1)
                    pe.wait_ge(s_head, i + 1)
                    x = fill(0)
                    for k in range(QB):
                        last = turn(B[:, x, k * P:(k + 1) * P], rv[:, k * P:(k + 1) * P], P)
                    last.then_inc(s_xp, 1)
                    turn(B[0:NS, fill(1), 0:P], rv[:, NP_:T], P).then_inc(s_xp, 1)
                    pe.wait_ge(s_qc, i + 1)
                    for b in range(QB):
                        mm(B[:, fill(2 + b), 0:P * (b + 1)], qc[:, b * P:(b + 1) * P], kt[:, 0:P * (b + 1)]
                           ).then_inc(s_xp, 1)

                def output_and_decay():
                    x = fill(10)
                    pe.wait_ge(s_xd, e0 + TAKEN0 + 10)
                    for k in range(QB):
                        last = mm(B[:, x, k * P:NP_], vtok[:, k, :], pt_h[:, KOFF[k]:KOFF[k] + NP_ - k * P],
                                  start=(k == 0), stop=(k == QB - 1))
                    last.then_inc(s_xp, 1)
                    pe.wait_ge(s_rk, i + 1)
                    for k in range(QB):
                        mm(B[:, fill(11 + k), 0:NP_ - k * P], rk[:, k * P:(k + 1) * P], rq[:, k * P:NP_]
                           ).then_inc(s_xp, 1)
                    x = fill(15)
                    for k in range(QB):
                        last = turn(B[:, x, k * P:(k + 1) * P], rk[:, k * P:(k + 1) * P], P)
                    last.then_inc(s_xp, 1)
                    turn(B[0:NS, fill(16), 0:P], rk[:, NP_:T], P).then_inc(s_xp, 1)

                head_tile(0)
                head_tile(1, between=values_and_scores)
                head_tile(2)
                pe.wait_ge(s_pn, i + 1)
                for k in range(QB):
                    x = fill(6 + k)
                    for b in range(k, QB):
                        last = turn(B[:, x, (b - k) * P:(b - k + 1) * P],
                                    p_h[:, QOFF[b] + k * P:QOFF[b] + (k + 1) * P], P)
                    last.then_inc(s_xp, 1)
                head_tile(3, between=output_and_decay)
                pe.wait_ge(s_vbd, i + 1)
                for j in range(2):
                    x = fill(17 + j)
                    pe.wait_ge(s_xd, e0 + TAKEN0 + 17)
                    mm(B[:, x, :], ks_tok[:, :], vbd[:, 4 * j:4 * j + 4, :]).then_inc(s_xp, 1)
                x = fill(19)
                for k in range(QB):
                    last = mm(B[:, x, k * P:NP_], vtok_r[:, k, :], sd_h[:, KOFF[k]:KOFF[k] + NP_ - k * P],
                              start=(k == 0), stop=(k == QB - 1))
                last.then_inc(s_xp, 1)
                x = fill(20)
                for k in range(QB):
                    last = mm(B[:, x, 0:P], ktok[:, k, :], vtok_r[:, k, :], start=(k == 0), stop=(k == QB - 1))
                last.then_inc(s_xp, 1)
                x = fill(21)
                pe.wait_ge(s_xd, e0 + TAKEN0 + 19)
                for b in range(NS):
                    last = mm(B[:, x, b:b + 1], rs[:, b, :], rq[:, NP_ + b:NP_ + b + 1])
                last.then_inc(s_xp, 1)
                for n, cols in enumerate((slice(0, NP_), slice(NP_, T))):
                    pe.wait_ge(s_sq, 2 * i + 1 + n)
                    mm(B[:, fill(22 + n), 0:cols.stop - cols.start], ones[:, :], rv[:, cols]).then_inc(s_xp, 1)

            with pe.Fori(0, KT // 2) as i:
                for u in range(2):
                    tile(TILE_OUT + 2 * i + u, TILE_OUT + u, unit_of(TILE_OUT) + 4 * i + 2 * u,
                         unit_of(TILE_OUT) + 2 * u, ready=s_t1)
            pe.wait_ge(s_n2, KT + 1)
            for half in range(2):
                last = mm(B[:, half, 0:HT], ones[:, :], ssum[:, half * HT:(half + 1) * HT])
            last.then_inc(s_n2m, 1)

            def up(m0, n0):
                with pe.Fori(0, CH // 2) as i:
                    for u in range(2):
                        tile(m0 + 2 * i + u, TILE_MLP + u, n0 + 4 * i + 2 * u, unit_of(TILE_MLP) + 2 * u, ready=s_t2)

            def down(m0, n0, ready_at, t, u):
                pe.wait_ge(s_evac, m0 + CH + t - 1)
                unit(n0 + 16 + t, (unit_of(TILE_MLP) + u) % RING, b_hi, b_lo, pair((TILE_MLP + u) % 2), True, True,
                     ready=s_b, ready_at=ready_at).then_inc(s_used, 1)

            def turn_rows(f):
                pe.wait_ge(s_yt, f + 1)
                if f >= 2:
                    pe.wait_ge(s_ye, f - 1)
                b = 2 * (f % 2)
                for tb in range(QB):
                    turn(B[:, b, tb * P:(tb + 1) * P], yt[:, f % 2, tb * P:(tb + 1) * P], P)
                turn(B[0:NS, b + 1, 0:P], yt[:, f % 2, NP_:T], P).then_inc(s_yx, 1)

            with pe.Fori(0, NCHUNK - 1) as c:
                m0, n0 = TILE_MLP + 24 * c, unit_of(TILE_MLP) + 32 * c
                up(m0, n0)
                with pe.Fori(0, KT // 4) as i:
                    for u in range(4):
                        down(m0, n0, CH * c, 4 * i + u, u)
            up(LAST_TILE, LAST_UNIT)
            for t in range(KT):
                down(LAST_TILE, LAST_UNIT, CH * (NCHUNK - 1), t, t)
                if t:
                    turn_rows(t - 1)
            pe.wait_ge(s_nf, 1)
            for tb in range(5):
                tok = slice(tb * P, min(tb * P + P, T))
                for n, x in enumerate((ssum, sq)):
                    last = mm(G[0:tok.stop - tok.start, 2, tb:tb + 1], x[:, tok], ones[:, 0:1], start=(n == 0),
                              stop=(n == 1))
            last.then_inc(s_nfm, 1)
            turn_rows(KT - 1)

        @block.scalar
        def _(act):
            def high(n, slot, raw, cols=P, first=False):
                act.wait_ge(s_raw[raw], 16 * (n // 2 + 1) if isinstance(n, int) else n)
                if not first:
                    act.wait_ge(s_used, n - 3)
                nc.scalar.copy(w_hi[:, slot, :, 0:cols], w_raw[:, raw, :, 0:cols]).then_inc(s_hi, 1)

            def high_at(base, four_i, u):
                act.wait_ge(s_raw[u % 2], 8 * four_i + 16 * ((base + u) // 2 + 1))
                act.wait_ge(s_used, four_i + base + u - 3)
                nc.scalar.copy(w_hi[:, (base + u) % RING, :, :], w_raw[:, u % 2, :, :]).then_inc(s_hi, 1)

            def act_fn(out, in_, fn, **kw):
                return nc.scalar.activation(out, in_, fn, **kw)

            for n, g in enumerate((norm1_g, norm2_g, final_norm_g)):
                act.dma_start(graw[16 * n:16 * n + 16, :], g.rearrange("(k p) -> k p", p=P)).then_inc(s_gr, 16)
            act.wait_ge(s_set, 1)
            for nth, tb in enumerate((4, 0, 1, 2, 3)):
                act.wait_ge(s_x[tb], 16)
                n = NS if tb == 4 else P
                for half in range(2):
                    if nth or half:
                        act.wait_ge(s_ssq, 2 * nth + half)
                    x = (xs_in[:, :] if tb == 4 else x_in[:, tb, :])[:, half * 1024:(half + 1) * 1024]
                    act_fn(G[0:n, 2:4, :].rearrange("p a b -> p (a b)"), x, ACT.Square,
                           accum_out=st[0:n, 5 * half + tb:5 * half + tb + 1]).then_inc(s_ssq, 1)
                if tb == 2:
                    high(0, 0, 0, first=True)
            act.wait_ge(s_gc, 1)
            for f in range(KT):
                if f == 2:
                    high(1, 1, 1, first=True)
                act.wait_ge(s_xr, 4 * (QB - 1) + f // 4 + 2)
                act_fn(a_hi[:, f, :], xr[:, f, :], ACT.Identity, scale=g1[:, f:f + 1]).then_inc(s_a0h, 1)
            high(2, 2, 0, KIWI, first=True)
            act.wait_ge(s_var, 1)
            act_fn(st[:, 10:15], st[:, 5:10], ACT.Sqrt).then_inc(s_sqrt, 1)
            high(3, 3, 1, KIWI, first=True)
            act.dma_start(cs[:, :, :], rotary).then_inc(s_rot, 16)
            for n, g in enumerate((idx_k_norm_g, idx_k_norm_b)):
                act.dma_start(lng[:, n, :], g[None, :].to_broadcast([P, ID])).then_inc(s_lng, 16)
            for n in range(4, 10):
                if n == 6:
                    act.dma_start(xt_dram, xr[:, :, :].rearrange("p k t -> p (k t)")).then_inc(s_spill, 16)
                high(n, n % RING, n % 2)
            act.wait_ge(s_yd, 2)
            act.dma_start(k_p[0].rearrange("(k p) d -> p k d", p=P), kout[:, :, :]).then_inc(s_kvo, 16)
            act.dma_start(k_s.rearrange("b o d -> (b o) d"), kout_s[:, :]).then_inc(s_kvo, 16)
            act.wait_ge(s_lnv, 1)
            act_fn(st[:, 10:15], st[:, 5:10], ACT.Sqrt).then_inc(s_lns, 1)
            act.wait_ge(s_ln, 1)
            act.dma_start(ik_p[0].rearrange("(k p) d -> p k d", p=P), ki_dup[:, 0:QB, 0:ID]).then_inc(s_rst, 16)
            act.dma_start(ik_s.rearrange("b o d -> (b o) d"), ki_dup[0:NS, 4, 0:ID]).then_inc(s_rso, 16)
            with act.Fori(0, 3) as i:
                for u in range(4):
                    high_at(unit_of(TILE_QI) + 6, 4 * i, u)
            for n in range(22, 24):
                high(n, n % RING, n % 2)
            j = 0
            for h in range(IH):
                for b in range(1, QB):
                    act.wait_ge(s_is, j + 1)
                    if j >= 2:
                        act.wait_ge(s_ic, j - 1)
                    act_fn(relu_p[:, j % 2, 0:P * (b + 1)], B[:, j % 4, 0:P * (b + 1)], ACT.Relu).then_inc(s_rl, 1)
                    j += 1
            act.wait_ge(s_ss, NS)
            act_fn(relu_s[:, :, :], G[:, 2:4, 0:257], ACT.Relu).then_inc(s_sr, 1)
            with act.Fori(0, 4) as i:
                for u in range(4):
                    high_at(unit_of(TILE_QA) + 4, 4 * i, u)
            for b in range(NS):
                act.wait_ge(s_at, b + 1)
                if b >= 2:
                    act.wait_ge(s_aq, b - 1)
                nc.scalar.copy(kt_b[:, b % 2, 0:CL], B[:, b % 2, :])
                nc.scalar.copy(kt_b[:, b % 2, CL:CL + 1], kt[:, NP_ + b:NP_ + b + 1]).then_inc(s_ak, 1)
            act.wait_ge(s_nms, 1)
            act_fn(p_s[:, :], p_s[:, :], ACT.Exp, bias=st[0:64, 42:43], accum_out=st[0:64, 43:44]).then_inc(s_exps, 1)

            for u in range(2):
                high(unit_of(TILE_HEAD) + 2 + u, (unit_of(TILE_HEAD) + 2 + u) % RING, u)
            act.wait_ge(s_yd, 6)
            act.dma_start(v_p[0].rearrange("(k p) d -> p k d", p=P), vtok[:, :, :]).then_inc(s_kvo, 16)
            act.dma_start(v_s.rearrange("b o d -> (b o) d"), vs[:, :]).then_inc(s_kvo, 16)
            with act.Fori(0, NH) as i:
                base, i8 = unit_of(TILE_HEAD) + 4, 8 * i

                def swap(m, done):
                    act.wait_ge(s_used, 2 * m + 2)
                    p = m_pair
                    nc.scalar.copy(t2[0:64, :].rearrange("p (a b) -> p a b", a=2), G[64:128, 2 * p:2 * p + 2, 0:HT])
                    nc.scalar.copy(t2[64:128, :].rearrange("p (a b) -> p a b", a=2), G[0:64, 2 * p:2 * p + 2, 0:HT]
                                   ).then_inc(s_swap, 1)

                high_at(base, i8, 0)
                high_at(base, i8, 1)
                for b in range(QB):
                    act.wait_ge(s_nm, 4 * i + b + 1)
                    n = slice(QOFF[b], QOFF[b] + P * (b + 1))
                    act_fn(p_h[:, n], p_h[:, n], ACT.Exp, bias=st[:, 25 + b:26 + b],
                           accum_out=st[:, 29 + b:30 + b]).then_inc(s_exp, 1)
                high_at(base, i8, 2)
                high_at(base, i8, 3)
                m_pair = (TILE_HEAD + 1) % 2
                swap(TILE_HEAD + 1 + 4 * i, 0)
                high_at(base, i8, 4)
                high_at(base, i8, 5)
                act.wait_ge(s_rq, i + 1)
                m_pair = (TILE_HEAD + 2) % 2
                swap(TILE_HEAD + 2 + 4 * i, 1)
                high_at(base, i8, 6)
                high_at(base, i8, 7)
                act.wait_ge(s_evac, TILE_HEAD + 4 * i + 4)
                act_fn(t2[:, :], rg[:, :], ACT.Tanh, scale=0.5).then_inc(s_th, 1)
                act.wait_ge(s_xd, 24 * i + TAKEN0 + 20)
                act_fn(rv[:, 0:NP_], ro[:, 0:NP_], ACT.Square).then_inc(s_sq, 1)
                act.wait_ge(s_xd, 24 * i + TAKEN0 + 22)
                act_fn(rv[:, NP_:T], ro[:, NP_:T], ACT.Square).then_inc(s_sq, 1)
                act.dma_start(rs_p[0, one(i), :, :].rearrange("a d e -> (a d) e"), rst[:, :]).then_inc(s_rst, 16)
                act.dma_start(rs_s[:, one(i), :, :].rearrange("b a d e -> d (b a) e"), rs[:, :, :]).then_inc(s_rso, 16)
                act.wait_ge(s_xd, 24 * i + TAKEN0 + 24)
                act_fn(rk[:, :], rv[:, :], ACT.Sqrt).then_inc(s_hs, 1)

            act.wait_ge(s_used, unit_of(TILE_OUT))
            for k in range(KT):
                if k == KT - 1:
                    act.wait_ge(s_head, NH + 1)
                nc.scalar.copy(a_hi[:, k, :], mix[:, k, :]).then_inc(s_t1h, 1)
            act.dma_start(xr[:, :, :].rearrange("p k t -> p (k t)"), xt_dram).then_inc(s_xb, 16)
            with act.Fori(0, KT // 2) as i:
                for u in range(4):
                    high_at(unit_of(TILE_OUT) + 4, 4 * i, u)
            act.wait_ge(s_evac, TILE_MLP)
            for k in range(KT):
                act_fn(a_hi[:, k, :], xr[:, k, :], ACT.Identity, scale=g2[:, k:k + 1]).then_inc(s_t2h, 1)
            act.wait_ge(s_n2v, 1)
            act_fn(ny[:, :], nv[:, :], ACT.Sqrt).then_inc(s_n2s, 1)
            first, last_down = unit_of(TILE_MLP) + 4, UNITS - KT
            with act.Fori(0, (last_down - first) // 4) as i:
                for u in range(4):
                    high_at(first, 4 * i, u)

            def rows_of(f):
                act.wait_ge(s_yx, f + 1)
                b = 2 * (f % 2)
                nc.scalar.copy(out_t[:, :, f * P:(f + 1) * P], B[:, b, :].rearrange("p (k d) -> p k d", d=P))
                nc.scalar.copy(out_s[:, f * P:(f + 1) * P], B[0:NS, b + 1, 0:P]).then_inc(s_ye, 1)

            for t in range(KT):
                high(last_down + t, (last_down + t) % RING, t % 2)
                if t >= 5:
                    rows_of(t - 5)
            for f in range(KT - 5, KT):
                if f == KT - 1:
                    act.wait_ge(s_nfv, 1)
                    act_fn(st[:, 75:80], st[:, 70:75], ACT.Sqrt).then_inc(s_nfs, 1)
                rows_of(f)
            act.wait_ge(s_rn, 1)
            act.wait_ge(s_ye, KT)
            for s, _, tb, half in PIECES:
                if s == 1:
                    x = out_t[:, tb, half * D // 2:(half + 1) * D // 2]
                    act_fn(x, x, ACT.Identity, scale=st[:, 75 + tb:76 + tb]).then_inc(s_fin[1], 1)
            act_fn(out_s[:, :], out_s[:, :], ACT.Identity, scale=st[0:NS, 79:80]).then_inc(s_fin[1], 1)

        @block.vector
        def _(dve):
            v = nc.vector
            step = Chain(dve, s_chain)

            def newton(y, var, t):
                step(v.reciprocal(y, y))
                step(v.tensor_tensor(t, var, y, ALU.mult))
                step(v.tensor_tensor(t, t, y, ALU.mult))
                step(v.tensor_scalar(t, t, -0.5, 1.5, ALU.mult, ALU.add))
                step(v.tensor_tensor(y, y, t, ALU.mult))

            step(v.memset(ones[:, :], 1.0))
            v.memset(st[:, :], 1.0).then_inc(s_set, 1)
            dve.wait_ge(s_xt, 1)
            v.tensor_copy(xr[:, :, NP_:T], G[:, 0, 0:KT * NS].rearrange("p (f n) -> p f n", n=NS)).then_inc(s_xr, 1)
            dve.wait_ge(s_gt, 1)
            v.tensor_copy(gcol[:, :], G[:, 1, 0:48]).then_inc(s_gc, 1)
            for tb in range(QB):
                for q in range(4):
                    dve.wait_ge(s_xt, 4 * tb + q + 2)
                    v.tensor_copy(xr[:, 4 * q:4 * q + 4, tb * P:(tb + 1) * P],
                                  B[:, q, :].rearrange("p (f n) -> p f n", n=P)).then_inc(s_xr, 1)
            dve.wait_ge(s_gc, 1)
            for f in range(KT):
                dve.wait_ge(s_a0h, f + 1)
                v.scalar_tensor_tensor(out=a_lo[:, f, :], in0=xr[:, f, :], scalar=g1[:, f:f + 1],
                                       in1=a_hi[:, f, :].bitcast(F32), op0=ALU.mult, op1=ALU.subtract).then_inc(s_a0, 1)
            dve.wait_ge(s_ssq, 10)
            step(v.tensor_tensor(st[:, 5:10], st[:, 0:5], st[:, 5:10], ALU.add))
            v.tensor_scalar(st[:, 5:10], st[:, 5:10], 1.0 / D, EPS, ALU.mult, ALU.add).then_inc(s_var, 1)
            dve.wait_ge(s_sqrt, 1)
            newton(st[:, 10:15], st[:, 5:10], st[:, 15:20])
            dve.wait_ge(s_cst, 16)
            for tb in range(5):
                last = v.tensor_scalar(rdiag[:, tb, :], ident, st[:, 10 + tb:11 + tb], None, ALU.mult)
            last.then_inc(s_diag, 1)
            dve.wait_ge(s_rbm, 1)
            v.tensor_copy(rb[:, 0:NP_], B[:, 0, :])
            v.tensor_copy(rb[:, NP_:T], B[:, 1, 0:NS]).then_inc(s_rbd, 1)
            dve.wait_ge(s_rbd, 1)

            def scaled(out, m, p, rows_=P):
                dve.wait_ge(s_used, 2 * m + 2)
                v.tensor_tensor(out, pair(p, rows_), halves(rb[0:rows_, :]), ALU.mult).then_inc(s_evac, 1)

            scaled(halves(kt[:, :]), 0, 0)
            scaled(halves(kiwi[:, :]), 1, 1, KIWI)
            dve.wait_ge(s_y, 1)
            v.tensor_copy(kout[:, :, :], B[:, 2, :].rearrange("p (k d) -> p k d", d=P)).then_inc(s_yd, 1)
            dve.wait_ge(s_y, 2)
            v.tensor_copy(kout_s[:, :], B[0:NS, 3, 0:P]).then_inc(s_yd, 1)

            def qi_taken(t):
                scaled(halves(qi[:, t, :]), TILE_QI + t, (TILE_QI + t) % 2)

            dve.wait_ge(s_spill, 16)
            qi_taken(0)
            step(v.memset(ki5[:, 4, :], 0.0))
            dve.wait_ge(s_y, 3)
            v.tensor_copy(ki5[:, 0:QB, :], B[:, 0, 0:QB * KIWI].rearrange("p (k d) -> p k d", d=KIWI)).then_inc(s_yd, 1)
            dve.wait_ge(s_y, 4)
            v.tensor_copy(ki5[0:NS, 4, :], B[0:NS, 1, 0:KIWI]).then_inc(s_yd, 1)
            dve.wait_ge(s_yd, 4)
            dve.wait_ge(s_lng, 32)
            ki, mu, var, y5, t5 = ki5[:, :, 0:ID], st[:, 20:25], st[:, 5:10], st[:, 10:15], st[:, 15:20]

            def spread(x):
                return x.unsqueeze(2).to_broadcast([P, 5, ID])

            def per_column(x):
                return x.unsqueeze(1).to_broadcast([P, 5, ID])

            wscale = IH ** -0.5 * ID ** -0.5
            step(v.tensor_scalar(wi[:, :, :], ki5[:, :, ID:KIWI], wscale, None, ALU.mult))
            step(v.tensor_tensor(zw[:, :, :], wi[0:NS, 4, :].unsqueeze(1).to_broadcast([NS, NS, IH]),
                                 ident[0:NS, 0:NS].unsqueeze(2).to_broadcast([NS, NS, IH]), ALU.mult))
            step(v.tensor_reduce(mu, ki, X, ALU.add))
            step(v.tensor_scalar(mu, mu, 1.0 / ID, None, ALU.mult))
            step(v.tensor_tensor(xc[:, :, :], ki, spread(mu), ALU.subtract))
            step(v.tensor_tensor(sq5[:, :, :], xc[:, :, :], xc[:, :, :], ALU.mult))
            step(v.tensor_reduce(var, sq5[:, :, :], X, ALU.add))
            step(v.tensor_scalar(var, var, 1.0 / ID, EPS, ALU.mult, ALU.add))
            last = v.tensor_copy(t5, var)
            last.then_inc(s_lnv, 1)
            dve.wait_ge(s_lns, 1)
            newton(y5, var, t5)
            step(v.tensor_tensor(xc[:, :, :], xc[:, :, :], spread(y5), ALU.mult))
            step(v.tensor_tensor(xc[:, :, :], xc[:, :, :], per_column(lng[:, 0, :]), ALU.mult))
            dve.wait_ge(s_spill, 16)
            v.tensor_tensor(ki_dup[:, :, 0:ID], xc[:, :, :], per_column(lng[:, 1, :]), ALU.add)
            v.tensor_tensor(ki_dup[:, :, ID:2 * ID], xc[:, :, :], per_column(lng[:, 1, :]), ALU.add).then_inc(s_ln, 1)
            dve.wait_ge(s_ln, 1)
            v.memset(kit[ID:P, :], 0.0)
            v.memset(kit_o[0:ID, :], 0.0)
            v.memset(qam[:, :], 0.0)
            v.memset(kis[:, :, :, :], 0.0)
            step(v.memset(qis[:, :], 0.0))
            qi_taken(1)
            dve.wait_ge(s_rot, 16)
            for n in range(2):
                step(v.tensor_tensor(cs[:, n, :], cs[:, n, :], rb[:, :], ALU.mult))
            with dve.Fori(0, 2) as i:
                for u in range(2):
                    t = 2 + 2 * i + u
                    scaled(halves(row(qi, t)), TILE_QI + t, (TILE_QI + u) % 2)
            qi_taken(6)
            dve.wait_ge(s_kit, 2)
            v.tensor_copy(kit[0:ID, 0:NP_], B[0:ID, 0, :])
            v.tensor_copy(kit_o[ID:P, :], B[ID:P, 0, :]).then_inc(s_kitd, 1)
            v.tensor_copy(wis[:, :], B[:, 1, NS:2 * NS])
            v.tensor_copy(kit[0:ID, NP_:T], B[0:ID, 1, 0:NS]).then_inc(s_kitd, 1)
            qi_taken(7)
            dve.wait_ge(s_evac, TILE_QA)
            q4 = qis[:, :].rearrange("p (b x) -> p b x", x=144)[:, :, 0:IH].rearrange("p b (t two) -> p t b two", two=2)
            for rows_ in (slice(0, ID), slice(ID, P)):
                v.tensor_copy(q4[rows_, :, :, 0], qi[0:ID, :, NP_:T])
                last = v.tensor_copy(q4[rows_, :, :, 1], qi[ID:P, :, NP_:T])
            last.then_inc(s_qis, 1)
            dve.wait_ge(s_kvo, 32)
            j = 0
            for h in range(IH):
                for b in range(1, QB):
                    n = P * (b + 1)
                    dve.wait_ge(s_rl, j + 1)
                    if h == 0:
                        ins = v.tensor_scalar(score[:, b - 1, 0:n], relu_p[:, j % 2, 0:n], wi[:, b, h:h + 1], None,
                                              ALU.mult)
                    else:
                        dve.wait_ge(s_ic, j - 2)
                        ins = v.scalar_tensor_tensor(out=score[:, b - 1, 0:n], in0=relu_p[:, j % 2, 0:n],
                                                     scalar=wi[:, b, h:h + 1], in1=score[:, b - 1, 0:n],
                                                     op0=ALU.mult, op1=ALU.add)
                    ins.then_inc(s_ic, 1)
                    j += 1
            for b in range(NS):
                dve.wait_ge(s_st, b + 1)
                if b >= 2:
                    dve.wait_ge(s_ss, b - 1)
                v.tensor_copy(kis[0:ID, b % 2, 0, 0:256], G[0:ID, b % 2, 0:256])
                v.tensor_copy(kis[ID:P, b % 2, 1, 0:256], G[ID:P, b % 2, 0:256])
                v.tensor_copy(kis[0:ID, b % 2, 0, 256:257], kit[0:ID, NP_ + b:NP_ + b + 1]).then_inc(s_sk, 1)
            dve.wait_ge(s_ic, j)
            for b in range(1, QB):
                diag = score[:, b - 1, b * P:(b + 1) * P]
                last = v.tensor_tensor(diag, diag, cmask, ALU.add)
            step(last)
            dve.wait_ge(s_sw, 1)
            v.memset(kt_b[:, :, CL + 1:CW], 0.0)
            v.memset(score_s[:, CL + 1:CW], MASKED)
            v.tensor_copy(score_s[:, CL:CL + 1], B[0:NS, 0, 256:257])
            for half in range(2):
                last = v.tensor_copy(score_s[:, 0:CL].rearrange("b (j two n) -> b two j n", two=2, n=P)[:, half],
                                     B[0:NS, half, 0:256].rearrange("b (j n) -> b j n", n=P))
            last.then_inc(s_scs, 1)
            dve.wait_ge(s_scs, 1)

            dve.wait_ge(s_rst, 16)
            dve.wait_ge(s_rso, 16)
            with step.loop(4, 4 * 4 * 2) as i:
                def take(*blocks):
                    at0 = None
                    for r in range(TOPK // 8 // 4 * 2):
                        for n, scores in enumerate(blocks):
                            m8 = st[0:scores.shape[0], (48, 56)[n]:(48, 56)[n] + 8]
                            if r:
                                step.wait(at0 + n)
                                v.tensor_copy(st[:, 65 + n:66 + n], st[:, 64:65])
                            at = step.mark(v.match_replace(scores, m8, scores, TAKEN) if r % 2 else v.max(m8, scores))
                            if n == 0:
                                first = at
                        at0 = first
                    step.wait(at)
                    v.tensor_copy(st[:, 66:67], st[:, 64:65])

                for u in range(2):
                    if u == 0:
                        take(score[:, 0, 0:2 * P], score[:, 1, 0:3 * P])
                    else:
                        take(score[:, 2, :], score_s[:, :])
                    t = 2 * i + u
                    scaled(halves(row(qa, t)), TILE_QA + t, (TILE_QA + u) % 2)
            dve.wait_ge(s_evac, TILE_VA)
            v.tensor_copy(qam[:, :].rearrange("p (b x) -> p b x", x=72)[:, :, 0:NH],
                          qa[:, :, NP_:T].rearrange("p h b -> p b h")).then_inc(s_qam, 1)
            v.tensor_scalar(score_s[:, :], score_s[:, :], TAKEN, MASKED, ALU.not_equal, ALU.mult).then_inc(s_ams, 1)
            for b in range(1, QB):
                n = P * (b + 1)
                last = v.tensor_scalar(am[:, b - 1, 0:n], score[:, b - 1, 0:n], TAKEN, MASKED, ALU.not_equal, ALU.mult)
            step(last)
            scale = P ** -0.5
            dve.wait_ge(s_ax, 1)
            step(v.tensor_copy(halves(am_s[:, :]), G[0:64, 2:4, 0:257]))
            dve.wait_ge(s_aq, NS)
            step(v.scalar_tensor_tensor(out=halves(p_s[:, :]), in0=B[0:64, 2:4, 0:257], scalar=scale,
                                        in1=halves(am_s[:, :]), op0=ALU.mult, op1=ALU.add))
            v.tensor_reduce(st[0:64, 42:43], p_s[:, :], X, ALU.max, negate=True).then_inc(s_nms, 1)
            dve.wait_ge(s_exps, 1)
            step(v.reciprocal(st[0:64, 44:45], st[0:64, 43:44]))
            v.tensor_scalar(p_s[:, :], p_s[:, :], st[0:64, 44:45], None, ALU.mult).then_inc(s_ps, 1)
            dve.wait_ge(s_ps, 1)
            v.tensor_scalar(diag_s[:, :], ident[0:64, 0:64], p_s[:, CL:CL + 1], None, ALU.mult).then_inc(s_dg, 1)
            dve.wait_ge(s_apt, 1)
            v.tensor_copy(pt_s[:, :, :], B[:, 0, 0:256].rearrange("p (k n) -> p k n", n=64)).then_inc(s_xd, 1)
            dve.wait_ge(s_apt, 2)
            v.tensor_copy(pown_s[:, :], B[0:NS, 1, 0:64]).then_inc(s_xd, 1)
            scaled(halves(vt[:, :]), TILE_VA, TILE_VA % 2)
            dve.wait_ge(s_y, 5)
            v.tensor_copy(vtok[:, :, :], B[:, 2, :].rearrange("p (k d) -> p k d", d=P)).then_inc(s_yd, 1)
            dve.wait_ge(s_y, 6)
            v.tensor_copy(vs[:, :], B[0:NS, 3, 0:P]).then_inc(s_yd, 1)
            dve.wait_ge(s_so, 1)
            o_pages, o_own = (B[:, b, 0:64].rearrange("p (b h) -> p h b", h=NH) for b in range(2))
            step(v.tensor_copy(mix[:, 0:NH, NP_:T], o_pages))
            v.tensor_tensor(mix[:, 0:NH, NP_:T], o_own, mix[:, 0:NH, NP_:T], ALU.add).then_inc(s_head, 1)

            with step.loop(NH, 12) as i:
                m0, e0 = TILE_HEAD + 4 * i, 24 * i

                def full(e):
                    dve.wait_ge(s_xp, e0 + e + 1)
                    return e % 4

                def rotate(out, m, p, s_out, nth, c):
                    dve.wait_ge(s_used, 2 * m + 2)
                    dve.wait_ge(s_swap, 2 * i + nth)
                    v.scalar_tensor_tensor(out=halves(out), in0=pair(p), scalar=c, in1=halves(cs[:, 0, :]),
                                           op0=ALU.mult, op1=ALU.mult)
                    v.scalar_tensor_tensor(out=t2[:, :], in0=t2[:, :], scalar=c, in1=cs[:, 1, :],
                                           op0=ALU.mult, op1=ALU.mult).then_inc(s_evac, 1)
                    dve.wait_ge(s_evac, m + 1)
                    v.tensor_tensor(out, out, t2[:, :], ALU.add).then_inc(s_out, 1)

                v.tensor_copy(st[:, 37:41], zeta[:, :, one(i)].rearrange("p k o -> p (k o)"))
                step(v.tensor_copy(st[:, 41:42], gamma[:, one(i)]))
                v.tensor_copy(qc[:, :], row(qa, i)[:, 0:NP_]).then_inc(s_qc, 1)
                scaled(halves(rv[:, :]), m0, TILE_HEAD % 2)
                v.tensor_copy(vtok_r[:, :, :], B[:, full(0), :].rearrange("p (k d) -> p k d", d=P)).then_inc(s_xd, 1)
                v.tensor_copy(vs_tok[:, :], B[0:NS, full(1), 0:P]).then_inc(s_xd, 1)
                for b in range(QB):
                    n = slice(QOFF[b], QOFF[b] + P * (b + 1))
                    x = full(2 + b)
                    v.scalar_tensor_tensor(out=p_h[:, n], in0=B[:, x, 0:P * (b + 1)], scalar=scale,
                                           in1=cmask if b == 0 else am[:, b - 1, 0:P * (b + 1)],
                                           op0=ALU.mult, op1=ALU.add).then_inc(s_xd, 1)
                    dve.wait_ge(s_xd, e0 + TAKEN0 + b + 3)
                    v.tensor_reduce(st[:, 25 + b:26 + b], p_h[:, n], X, ALU.max, negate=True).then_inc(s_nm, 1)
                for b in range(QB):
                    n = slice(QOFF[b], QOFF[b] + P * (b + 1))
                    dve.wait_ge(s_exp, 4 * i + b + 1)
                    step(v.reciprocal(st[:, 33 + b:34 + b], st[:, 29 + b:30 + b]))
                    last = v.tensor_scalar(p_h[:, n], p_h[:, n], st[:, 33 + b:34 + b], None, ALU.mult)
                last.then_inc(s_pn, 1)
                rotate(rq[:, :], m0 + 1, (TILE_HEAD + 1) % 2, s_rq, 1, 1.0)
                for k in range(QB):
                    n = NP_ - k * P
                    v.tensor_copy(pt_h[:, KOFF[k]:KOFF[k] + n], B[:, full(6 + k), 0:n]).then_inc(s_xd, 1)
                rotate(rk[:, :], m0 + 2, TILE_HEAD % 2, s_rk, 2, P ** -0.5)
                v.tensor_copy(row(mix, i)[:, 0:NP_], B[:, full(10), :]).then_inc(s_xd, 1)
                dve.wait_ge(s_dh, 16 * i + 16)
                for k in range(QB):
                    n = NP_ - k * P
                    v.tensor_tensor(sd_h[:, KOFF[k]:KOFF[k] + n], B[:, full(11 + k), 0:n], dh[:, 0:n], ALU.mult
                                    ).then_inc(s_xd, 1)
                dve.wait_ge(s_rst, 16 * i + 16)
                v.tensor_tensor(ktok[:, :, :], B[:, full(15), :].rearrange("p (k d) -> p k d", d=P),
                                st[:, 37:41].unsqueeze(2).to_broadcast([P, QB, P]), ALU.mult).then_inc(s_xd, 1)
                v.tensor_copy(ks_tok[:, :], B[0:NS, full(16), 0:P]).then_inc(s_xd, 1)
                v.tensor_tensor(vbd[:, :, :], vs_tok[:, :].unsqueeze(1).to_broadcast([NS, NS, P]),
                                ident[0:NS, 0:NS].unsqueeze(2).to_broadcast([NS, NS, P]), ALU.mult).then_inc(s_vbd, 1)
                scaled(halves(rg[:, :]), m0 + 3, (TILE_HEAD + 1) % 2)
                dve.wait_ge(s_rs, 16 * i + 16)
                for j in range(2):
                    r4 = rs[:, 4 * j:4 * j + 4, :]
                    v.scalar_tensor_tensor(out=r4, in0=r4, scalar=st[:, 41:42],
                                           in1=B[:, full(17 + j), :].rearrange("p (b e) -> p b e", e=P),
                                           op0=ALU.mult, op1=ALU.add).then_inc(s_xd, 1)
                v.tensor_copy(ro[:, 0:NP_], B[:, full(19), :]).then_inc(s_xd, 1)
                v.tensor_copy(rst[:, :], B[:, full(20), 0:P]).then_inc(s_xd, 1)
                v.tensor_copy(ro[:, NP_:T], B[:, full(21), 0:NS]).then_inc(s_xd, 1)
                for n, cols in enumerate((slice(0, NP_), slice(NP_, T))):
                    v.tensor_scalar(rv[:, cols], B[:, full(22 + n), 0:cols.stop - cols.start], 1.0 / P, EPS,
                                    ALU.mult, ALU.add).then_inc(s_xd, 1)
                dve.wait_ge(s_th, i + 1)
                step(v.scalar_tensor_tensor(out=rg[:, :], in0=t2[:, :], scalar=1.0, in1=rg[:, :],
                                            op0=ALU.add, op1=ALU.mult))
                dve.wait_ge(s_hs, i + 1)
                newton(rk[:, :], rv[:, :], rq[:, :])
                step(v.tensor_tensor(rk[:, :], rk[:, :], ro[:, :], ALU.mult))
                v.scalar_tensor_tensor(out=row(mix, i + NH), in0=rk[:, :], scalar=0.5, in1=rg[:, :],
                                       op0=ALU.mult, op1=ALU.mult).then_inc(s_head, 1)

            for k in range(NH, KT):
                dve.wait_ge(s_t1h, k + 1)
                v.tensor_tensor(a_lo[:, k, :], mix[:, k, :], a_hi[:, k, :].bitcast(F32), ALU.subtract
                                ).then_inc(s_t1, 1)
            v.memset(ssum[:, :], 0.0).then_inc(s_n2, 1)
            dve.wait_ge(s_xb, 16)
            with step.loop(KT // 2, 2) as i:
                for u in range(2):
                    t = 2 * i + u
                    m = TILE_OUT + t
                    dve.wait_ge(s_used, 2 * m + 2)
                    xt = row(xr, t)
                    v.tensor_tensor(halves(xt), pair((TILE_OUT + u) % 2), halves(xt), ALU.add).then_inc(s_evac, 1)
                    dve.wait_ge(s_evac, m + 1)
                    step(v.tensor_tensor(sq[:, :], xt, xt, ALU.mult))
                    dve.wait_ge(s_n2, t + 1)
                    v.tensor_tensor(ssum[:, :], ssum[:, :], sq[:, :], ALU.add).then_inc(s_n2, 1)

            def inverse_rms(s_m, s_v, s_s, between=None):
                dve.wait_ge(s_m, 1)
                v.tensor_scalar(halves(nv[:, :]), B[:, 0:2, 0:HT], 1.0 / D, EPS, ALU.mult, ALU.add).then_inc(s_v, 1)
                if between:
                    between()
                dve.wait_ge(s_s, 1)
                newton(ny[:, :], nv[:, :], u1[:, :])
                step(v.tensor_copy(rb[:, :], ny[:, :]))

            def split_h2():
                for k in range(KT):
                    dve.wait_ge(s_t2h, k + 1)
                    v.scalar_tensor_tensor(out=a_lo[:, k, :], in0=xr[:, k, :], scalar=g2[:, k:k + 1],
                                           in1=a_hi[:, k, :].bitcast(F32), op0=ALU.mult, op1=ALU.subtract
                                           ).then_inc(s_t2, 1)

            inverse_rms(s_n2m, s_n2v, s_n2s, split_h2)

            def hidden(m0, n0):
                with step.loop(CH // 2, 4) as i:
                    for u in range(2):
                        t = 2 * i + u
                        dve.wait_ge(s_used, n0 + 4 * i + 2 * u + 2)
                        v.scalar_tensor_tensor(out=halves(u1[:, :]), in0=pair((TILE_MLP + u) % 2), scalar=0.0,
                                               in1=halves(rb[:, :]), op0=ALU.max, op1=ALU.mult).then_inc(s_evac, 1)
                        dve.wait_ge(s_evac, m0 + t + 1)
                        step(v.tensor_tensor(u2[:, :], u1[:, :], u1[:, :], ALU.mult))
                        step(v.tensor_copy(row(b_hi, t), u2[:, :]))
                        v.tensor_tensor(row(b_lo, t), u2[:, :], row(b_hi, t).bitcast(F32), ALU.subtract
                                        ).then_inc(s_b, 1)

            def add_down(n0, t, u, xt):
                dve.wait_ge(s_used, n0 + 16 + t + 1)
                v.tensor_tensor(halves(xt), pair((TILE_MLP + u) % 2), halves(xt), ALU.add).then_inc(s_evac, 1)

            with step.loop(NCHUNK - 1, 2 * CH) as c:
                m0, n0 = TILE_MLP + 24 * c, unit_of(TILE_MLP) + 32 * c
                hidden(m0, n0)
                with dve.Fori(0, KT // 4) as i:
                    for u in range(4):
                        t = 4 * i + u
                        add_down(n0, t, u, row(xr, t))
            hidden(LAST_TILE, LAST_UNIT)
            for f in range(KT):
                xt = xr[:, f, :]

                def scaled_tile():
                    if f >= 2:
                        dve.wait_ge(s_yx, f - 1)
                    v.tensor_scalar(yt[:, f % 2, :], xt, gf[:, f:f + 1], None, ALU.mult).then_inc(s_yt, 1)

                add_down(LAST_UNIT, f, f % 2, xt)
                dve.wait_ge(s_evac, LAST_TILE + CH + f + 1)
                if f < KT - 1:
                    scaled_tile()
                    step(v.tensor_tensor(sq[:, :] if f else ssum[:, :], xt, xt, ALU.mult))
                    if f:
                        step(v.tensor_tensor(ssum[:, :], ssum[:, :], sq[:, :], ALU.add))
                else:
                    v.tensor_tensor(sq[:, :], xt, xt, ALU.mult).then_inc(s_nf, 1)
                    scaled_tile()
            dve.wait_ge(s_nfm, 1)
            step(v.tensor_scalar(st[:, 70:74], G[:, 2, 0:4], 1.0 / D, EPS, ALU.mult, ALU.add))
            v.tensor_scalar(st[0:NS, 74:75], G[0:NS, 2, 4:5], 1.0 / D, EPS, ALU.mult, ALU.add).then_inc(s_nfv, 1)
            dve.wait_ge(s_nfs, 1)
            newton(st[:, 75:80], st[:, 70:75], st[:, 80:85])
            v.tensor_copy(st[:, 85:86], st[:, 75:76]).then_inc(s_rn, 1)
            dve.wait_ge(s_ye, KT)
            for s, _, tb, half in PIECES:
                if s == 0:
                    x = out_t[:, tb, half * D // 2:(half + 1) * D // 2]
                    v.tensor_scalar(x, x, st[:, 75 + tb:76 + tb], None, ALU.mult).then_inc(s_fin[0], 1)


_INS = ['x_prompt', 'x_sample', 'cache_k', 'cache_v', 'cache_idx_k', 'state_ret', 'page_table', 'norm1_g', 'w_in',
        'idx_k_norm_g', 'idx_k_norm_b', 'w_out', 'norm2_g', 'w_up', 'w_down', 'final_norm_g']
_OUTS = [(1, 512, 2048), (8, 1, 2048), (1, 512, 128), (1, 512, 128), (1, 512, 64), (1, 8, 128, 128),
         (8, 1, 128), (8, 1, 128), (8, 1, 64), (8, 8, 128, 128)]


def shape_constants():
    import numpy as np
    lg = np.log1p(-np.exp2(-5.0 - np.arange(NH, dtype=np.float64)))
    p = np.arange(P)
    const = np.zeros((P, 368), np.float32)
    const[:, 0:P] = np.eye(P)
    const[:, P:2 * P] = np.where(p[None, :] <= p[:, None], 0.0, MASKED)
    const[:, 256:288] = np.exp((NP_ - 1.0 - (p[:, None, None] + P * np.arange(QB)[None, :, None]))
                               * lg[None, None, :]).reshape(P, 32)
    const[:, 288:296] = np.exp(lg)[None, :]
    const[0:NS, 296:360] = np.repeat(np.eye(NS), 8, axis=1)
    const[0:64, 360:368] = np.repeat(np.eye(NS), 8, axis=0)
    diff = np.arange(NP_)[None, :] - p[:, None]
    decay = np.where(diff[None] >= 0, np.exp(np.maximum(diff, 0)[None] * lg[:, None, None]), 0.0).astype(np.float32)
    inv = (np.float32(10000.0) ** (-np.arange(64, dtype=np.float32) / np.float32(64))).astype(np.float32)
    pos = np.concatenate([np.arange(NP_), np.full(NS, CL)]).astype(np.float32)
    ang = (inv[:, None] * pos[None, :]).astype(np.float32)
    cos, sin = np.cos(ang), np.sin(ang)
    rotary = np.stack([np.concatenate([cos, cos]), np.concatenate([-sin, sin])], axis=1).astype(np.float32)
    return {"shape_const": const, "shape_rotary": rotary, "shape_decay": decay}


def kernel(**inputs):
    import numpy as _np
    import concourse.bacc as _bacc
    from concourse import mybir as _mybir
    from concourse.bass_utils import run_bass_kernel_spmd as _run

    nc = _bacc.Bacc("TRN2", target_bir_lowering=False, num_devices=1)
    arrays, args = {}, []
    for name in _INS:
        arrays[f"in_{name}_dram"] = _np.ascontiguousarray(inputs[name])
    for name, a in shape_constants().items():
        arrays[f"{name}_dram"] = a
    for name, a in arrays.items():
        args.append(nc.dram_tensor(name, a.shape, _mybir.dt.from_np(a.dtype), kind="ExternalInput").ap())
    for i, shape in enumerate(_OUTS):
        args.append(nc.dram_tensor(f"out_{i}_dram", shape, _mybir.dt.float32, kind="ExternalOutput").ap())
    build(nc, *args)
    r = _run(nc, [arrays], core_ids=[0])
    return tuple(r.results[0][f"out_{i}_dram"] for i in range(len(_OUTS)))
```

```python
from contextlib import ExitStack, contextmanager

import concourse.bass as bass
from concourse import mybir

P = 128
D = 2048
KT = D // P
NP_, NS = 512, 8
T = NP_ + NS
HT = T // 2
QB = NP_ // P
NH = 8
IH, ID = 16, 64
TOPK = 128
PAGES = 4
CL = PAGES * P
CW = CL + 2
DFF = 4 * D
CH = 8
NCHUNK = DFF // (CH * P)
THIRDS = (0, 32, 64)
K3 = THIRDS[2] + NS
EPS = 1e-6
MASKED = -1e30
TAKEN = -3.0e38
OFF_QA, OFF_KA, OFF_VA, OFF_QI = 0, 1024, 1152, 1280
OFF_KI, OFF_QR, OFF_KR, OFF_VR, OFF_GR = 2304, 2384, 3408, 4432, 5456
KIWI = ID + IH
RING = 4

TILE_QI, TILE_QA, TILE_VA, TILE_HEAD, TILE_OUT, TILE_MLP = 2, 10, 18, 19, 51, 67
TAKEN0 = 2
UNITS = 2 * TILE_MLP + NCHUNK * (2 * CH + KT)
LAST_TILE, LAST_UNIT = TILE_MLP + 24 * (NCHUNK - 1), UNITS - 2 * CH - KT

PIECES = [(0, 1, 0, 0), (1, 1, 2, 1), (0, 2, 0, 1), (0, 3, 1, 0), (1, 2, 3, 0), (0, 4, 1, 1), (0, 5, 2, 0), (1, 3, 3, 1)]
ACT_PIECES = 3

F32, F32R, BF16, I32 = mybir.dt.float32, mybir.dt.float32r, mybir.dt.bfloat16, mybir.dt.int32
ALU = mybir.AluOpType
ACT = mybir.ActivationFunctionType
X = mybir.AxisListType.X


def unit_of(tile):
    return 2 * tile


class Chain:

    def __init__(self, eng, sem):
        self.eng, self.sem, self.n, self.at = eng, sem, 0, 0

    def __call__(self, ins):
        ins.then_inc(self.sem, 1)
        self.n += 1
        self.eng.wait_ge(self.sem, self.at + self.n)

    def mark(self, ins):
        ins.then_inc(self.sem, 1)
        self.n += 1
        return self.n

    def wait(self, n):
        self.eng.wait_ge(self.sem, self.at + n)

    @contextmanager
    def loop(self, count, per):
        at, n = self.at, self.n
        with self.eng.Fori(0, count) as i:
            self.at, self.n = at + i * per, n
            yield i
            assert self.n - n == per, f"{self.n - n} steps in a round, not {per}"
        self.at, self.n = at, n + count * per


def build(nc, x_prompt, x_sample, cache_k, cache_v, cache_idx_k, state_ret, page_table, norm1_g, w_in,
          idx_k_norm_g, idx_k_norm_b, w_out, norm2_g, w_up, w_down, final_norm_g, shapes_const, rotary, decay,
          y_p, y_s, k_p, v_p, ik_p, rs_p, k_s, v_s, ik_s, rs_s):
    ctx = ExitStack()
    with ctx:
        BASE = 16512

        def at(name, offset, shape, dt=F32):
            return nc.alloc_sbuf_tensor_at(name, shape, dt, offset=BASE + offset)

        def sem(name):
            return ctx.enter_context(nc.semaphore(name))

        a_hi = at("a_hi", 0, [P, KT, T], F32R)
        a_lo = at("a_lo", 33280, [P, KT, T], F32R)
        w_raw = at("w_raw", 66560, [P, 2, 8, P])
        w_hi = at("w_hi", 74752, [P, RING, 8, P], F32R)
        w_lo = at("w_lo", 91136, [P, RING, 8, P], F32R)
        M0 = 107520
        mix = at("mix", M0, [P, KT, T])
        b_hi = at("b_hi", M0, [P, CH, T], F32R)
        b_lo = at("b_lo", M0 + 16640, [P, CH, T], F32R)
        x_in = at("x_in", M0, [P, QB, D])
        kpages = at("kpages", M0, [P, NS * PAGES, P])
        vpages = at("vpages", M0 + 16640, [P, NS * PAGES, P])
        R0 = 140800
        xr = at("xr", R0, [P, KT, T])
        qi = at("qi", R0, [P, 8, T])
        qa = at("qa", R0 + 16640, [P, NH, T])
        ipages = at("ipages", R0 + 16640, [P, NS * PAGES, ID])
        relu_p = at("relu_p", R0 + 16640 + 8192, [P, 2, NP_])
        ki_dup = at("ki_dup", R0 + 16640 + 12288, [P, 5, 2 * ID])
        kt_b = at("kt_b", R0, [P, 2, CW])
        am_s = at("am_s", R0 + 4128, [64, CW])
        p_s = at("p_s", R0 + 6208, [64, CW])
        pt_s = at("pt_s", R0 + 8288, [P, PAGES, 64])
        diag_s = at("diag_s", R0 + 9312, [64, 64])
        pown_s = at("pown_s", R0 + 9568, [NS, 64])
        vt = at("vt", R0 + 9856, [P, T])
        relu_s = at("relu_s", R0, [P, 2, 257])
        rq = at("rq", R0, [P, T])
        rk = at("rk", R0 + 2080, [P, T])
        rv = at("rv", R0 + 4160, [P, T])
        rg = at("rg", R0 + 6240, [P, T])
        dh = at("dh", R0 + 8320, [P, NP_])
        ro = at("ro", R0 + 10368, [P, T])
        rs = at("rs", R0 + 12448, [P, NS, P])

        o = 174080
        small = {}
        for name, shape, dt, nbytes in (
                ("const", [P, 376], F32, 1504), ("ones", [P, P], F32, 512), ("gcol", [P, 48], F32, 192),
                ("rb", [P, T], F32, 2080), ("kt", [P, T], F32, 2080), ("vtok", [P, QB, P], F32, 2048),
                ("vs", [NS, P], F32, 512), ("kit", [P, T], F32, 2080), ("wi", [P, 5, IH], F32, 320),
                ("am", [P, QB - 1, NP_], BF16, 3072), ("st", [P, 88], F32, 352), ("pt_i", [1, 32], I32, 128)):
            if name == "am":
                AM_OFFSET = o - 174080
            small[name] = at(name, o, shape, dt)
            o += nbytes
        const, ones, gcol, rb, kt, vtok, vs, kit, wi, am, st, pt_i = small.values()
        assert o <= 188960
        kit_o = at("kit_o", 174080 + AM_OFFSET, [P, NP_])
        cs = at("cs", 188960, [P, 2, T])
        H0 = 193120
        xs_in = at("xs_in", H0, [NS, D])
        graw = at("graw", H0 + 8192, [48, P])
        lng = at("lng", H0 + 8704, [P, 2, ID])
        rdiag = at("rdiag", H0 + 11296, [P, 5, P])
        kout = at("kout", H0, [P, QB, P])
        kout_s = at("kout_s", H0 + 2048, [NS, P])
        zw = at("zw", H0 + 5120, [NS, NS, IH])
        kiwi = at("kiwi", H0 + 11296, [KIWI, T])
        ki5 = at("ki5", H0 + 13376, [P, 5, KIWI])
        xc = at("xc", H0 + 14976, [P, 5, ID])
        sq5 = at("sq5", H0 + 16256, [P, 5, ID])
        score = at("score", H0, [P, QB - 1, NP_])
        score_s = at("score_s", H0 + 6144, [NS, CW])
        qam = at("qam", H0 + 8224, [P, NS * 72])
        kis = at("kis", H0 + 10528, [P, 2, 2, 257])
        qis = at("qis", H0 + 14656, [P, NS * 144])
        wis = at("wis", H0 + 19264, [P, NS])
        p_h = at("p_h", H0, [P, 1280])
        sd_h = at("sd_h", H0, [P, 1280])
        pt_h = at("pt_h", H0 + 5120, [P, 1280])
        vbd = at("vbd", H0 + 5120, [K3, NS, P], F32R)
        ktok = at("ktok", H0 + 10240, [P, QB, P])
        rst = at("rst", H0 + 10240, [P, P])
        ks_tok = at("ks_tok", H0 + 12288, [K3, P], F32R)
        vtok_r = at("vtok_r", H0 + 12800, [P, QB, P])
        vs_tok = at("vs_tok", H0 + 14848, [K3, P], F32R)
        qc = at("qc", H0 + 15360, [P, NP_])
        t2 = at("t2", H0 + 17408, [P, T])
        sq = at("sq", H0, [P, T])
        ssum = at("ssum", H0 + 2080, [P, T])
        u1 = at("u1", H0 + 4160, [P, T])
        u2 = at("u2", H0 + 6240, [P, T])
        nv = at("nv", H0 + 8320, [P, T])
        ny = at("ny", H0 + 10400, [P, T])
        yt = at("yt", H0 + 12480, [P, 2, T])
        out_t = at("out_t", 0, [P, QB, D])
        out_s = at("out_s", 33280, [NS, D])

        ident, cmask = const[:, 0:P], const[:, P:2 * P]
        zeta, gamma = const[:, 256:288].rearrange("p (k h) -> p k h", h=NH), const[:, 288:296]
        expand, fold, ident3 = const[0:NS, 296:360], const[0:64, 360:368], const[0:K3, 368:376]
        g1, g2, gf = gcol[:, 0:16], gcol[:, 16:32], gcol[:, 32:48]

        G = ctx.enter_context(nc.psum_tensor("product", [P, 4, 512], F32))
        B = ctx.enter_context(nc.psum_tensor("banks", [P, 4, 512], F32))

        def pair(p, rows=P):
            return G[0:rows, 2 * p:2 * p + 2, 0:HT]

        def halves(x):
            return x.rearrange("p (a b) -> p a b", a=2)

        def one(i):
            return bass.ds(i, 1)

        def row(x, i):
            return x[:, one(i), :].rearrange("p o n -> p (o n)")

        QOFF = [0, 128, 384, 768]
        KOFF = [0, 512, 896, 1152]
        xt_dram = nc.dram_tensor("x_transposed", (P, KT, T), F32).ap()

        s_raw = [sem(f"weights_loaded_{u}") for u in range(2)]
        s_hi, s_lo, s_used = sem("weights_hi"), sem("weights_lo"), sem("weights_used")
        s_evac = sem("tile_taken")
        s_x = [sem(f"x_loaded_{u}") for u in range(5)]
        (s_cst, s_rot, s_gr, s_lng, s_pt, s_set, s_ssq, s_gt, s_gc, s_xt, s_xr, s_a0h, s_a0, s_spill, s_var, s_sqrt,
         s_diag, s_rbm, s_rbd, s_y, s_yd, s_kvo, s_lnv, s_lns, s_ln, s_kit, s_kitd, s_is, s_rl, s_ic) = (
            sem(n) for n in (
                "consts_loaded", "rotary_loaded", "gains_loaded", "ln_loaded", "pages_listed", "set_up",
                "squares_summed", "gains_turned", "gains_ready", "x_turned", "xr_ready", "a0_hi", "a0_ready", "x_spilled",
                "var_ready", "sqrt_ready", "diag_ready", "rms_spread", "rms_ready", "kv_turned", "kv_taken",
                "kv_stored", "ln_var", "ln_sqrt", "ln_done", "kit_turned", "kit_ready",
                "index_dots", "index_relu", "index_added"))
        (s_pi, s_pk, s_pv, s_qis, s_st, s_sk, s_ss, s_sr, s_sw, s_scs, s_ams, s_qam, s_at, s_ak, s_aq, s_ax,
         s_nms, s_exps, s_ps, s_dg, s_apt, s_so) = (
            sem(n) for n in (
                "ipages_loaded", "kpages_loaded", "vpages_loaded", "sample_iq", "ipages_turned", "sample_ik",
                "sample_dots", "sample_relu", "sample_weighed", "sample_scores", "sample_mask", "sample_q",
                "kpages_turned", "sample_k", "sample_qk", "mask_spread", "sample_max", "sample_exp", "sample_p",
                "own_diag", "sample_p_turned", "sample_o"))
        (s_qc, s_swap, s_rq, s_rk, s_xp, s_xd, s_nm, s_exp, s_pn, s_dh, s_rs, s_rst, s_rso, s_vbd, s_sq,
         s_th, s_hs, s_head) = (
            sem(n) for n in (
                "head_q", "halves_swapped", "ret_q", "ret_k", "head_bank_full", "head_bank_taken", "head_max",
                "head_exp", "head_p", "decay_loaded", "state_loaded", "prompt_state_stored",
                "sample_state_stored", "values_diagonal", "ret_squared", "gate_tanh",
                "ret_sqrt", "head_done"))
        (s_t1h, s_t1p, s_t1, s_xb, s_n2, s_n2m, s_n2v, s_n2s, s_t2h, s_t2, s_b, s_nf, s_nfm, s_nfv, s_nfs, s_yt,
         s_yx, s_ye, s_out, s_rn, s_chain) = (
            sem(n) for n in (
                "mixed_hi", "mixed_lo_pool", "mixed_lo", "x_back", "sum2", "sum2_spread", "var2", "sqrt2",
                "h2_hi", "h2_lo", "hidden_ready", "sumf", "sumf_spread", "varf", "sqrtf", "y_scaled", "y_turned",
                "y_taken", "y_stored", "rmsf_ready", "vector_step"))

        s_fin = [sem("rows_scaled_vector"), sem("rows_scaled_scalar")]

        block = ctx.enter_context(nc.Block())

        @block.sync
        def _(sp):
            def load_unit(slot, n, src, cols=P):
                if not isinstance(n, int) or n >= 2:
                    sp.wait_ge(s_lo, n - 1)
                sp.dma_start(w_raw[:, slot, :, 0:cols], src.rearrange("(k p) c -> p k c", p=P)).then_inc(s_raw[slot], 16)

            def rows(w, half, col, cols=P):
                return w[half * 1024:half * 1024 + 1024, bass.ds(col, cols)]

            sp.dma_start(const[:, :], shapes_const).then_inc(s_cst, 16)
            sp.dma_start(xs_in[:, :], x_sample.rearrange("b o d -> (b o) d")).then_inc(s_x[4], 16)
            for tb in range(QB):
                if tb == QB - 1:
                    load_unit(0, 0, rows(w_in, 0, OFF_KA))
                sp.dma_start(x_in[:, tb, :], x_prompt[0, tb * P:(tb + 1) * P, :]).then_inc(s_x[tb], 16)
            load_unit(1, 1, rows(w_in, 1, OFF_KA))
            sp.dma_start(pt_i[:, :], page_table.rearrange("b j -> (b j)")[None, :]).then_inc(s_pt, 16)
            load_unit(0, 2, rows(w_in, 0, OFF_KI, KIWI), KIWI)
            load_unit(1, 3, rows(w_in, 1, OFF_KI, KIWI), KIWI)
            sp.wait_ge(s_pt, 16)

            def qi_unit(i, u):
                load_unit(u % 2, unit_of(TILE_QI) + 4 * i + u, rows(w_in, u % 2, OFF_QI + 256 * i + P * (u // 2)))

            def load_page(j, *caches):
                page = sp.value_load(pt_i[0:1, one(j)])
                for dst, cache, s in caches:
                    sp.dma_start(dst[:, one(j), :], cache[one(page), :, :].rearrange("a p d -> p a d")).then_inc(s, 16)

            qi_unit(0, 0)
            qi_unit(0, 1)
            sp.wait_ge(s_spill, 32)
            sp.wait_ge(s_a0, KT)
            qi_unit(0, 2)
            qi_unit(0, 3)
            with sp.Fori(1, 4) as i:
                for u in range(4):
                    qi_unit(i, u)
                    for v in range(3 if u < 2 else 2):
                        load_page(10 * i + (0, 3, 6, 8)[u] + v - 10, (ipages, cache_idx_k, s_pi))
            for j in range(30, NS * PAGES):
                load_page(j, (ipages, cache_idx_k, s_pi))
            with sp.Fori(0, 4) as i:
                for u in range(4):
                    load_unit(u % 2, unit_of(TILE_QA) + 4 * i + u, rows(w_in, u % 2, OFF_QA + 256 * i + P * (u // 2)))
                    for v in range(2):
                        load_page(8 * i + 2 * u + v, (kpages, cache_k, s_pk), (vpages, cache_v, s_pv))
            load_unit(0, unit_of(TILE_VA), rows(w_in, 0, OFF_VA))
            load_unit(1, unit_of(TILE_VA) + 1, rows(w_in, 1, OFF_VA))
            with sp.Fori(0, NH) as i:
                for u in range(8):
                    off = (OFF_VR, OFF_QR, OFF_KR, OFF_GR)[u // 2]
                    load_unit(u % 2, unit_of(TILE_HEAD) + 8 * i + u, rows(w_in, u % 2, off + P * i))
                    if u == 4:
                        sp.wait_ge(s_head, i + 1)
                        sp.dma_start(dh[:, :], decay[one(i), :, :].rearrange("a p n -> (a p) n")).then_inc(s_dh, 16)
                        sp.wait_ge(s_rso, 16 * i + 16)
                        sp.dma_start(rs[:, :, :], state_ret[:, one(i), :, :].rearrange("b a d e -> d (b a) e")
                                     ).then_inc(s_rs, 16)
            for n, (t, half) in enumerate(((0, 0), (1, 0), (0, 1), (1, 1))):
                load_unit(n % 2, unit_of(TILE_OUT) + n, rows(w_out, half, P * t))
            with sp.Fori(1, KT // 2) as i:
                for u in range(4):
                    load_unit(u % 2, unit_of(TILE_OUT) + 4 * i + u, rows(w_out, u % 2, 256 * i + P * (u // 2)))
            with sp.Fori(0, NCHUNK) as c:
                n0 = unit_of(TILE_MLP) + 32 * c
                with sp.Fori(0, CH // 2) as i:
                    for u in range(4):
                        load_unit(u % 2, n0 + 4 * i + u, rows(w_up, u % 2, 1024 * c + 256 * i + P * (u // 2)))
                with sp.Fori(0, KT // 4) as i:
                    for u in range(4):
                        load_unit(u % 2, n0 + 16 + 4 * i + u,
                                  w_down[bass.ds(1024 * c, 1024), bass.ds(512 * i + P * u, P)])
            sp.wait_ge(s_kvo, 64)
            sp.wait_ge(s_rst, 16 * NH + 16)
            sp.wait_ge(s_rso, 16 * NH + 16)
            for n, (s, count, tb, half) in enumerate(PIECES):
                sp.wait_ge(s_fin[s], count)
                cols = slice(half * D // 2, (half + 1) * D // 2)
                sp.dma_start(y_p[0, tb * P:(tb + 1) * P, cols], out_t[:, tb, cols]).then_inc(s_out, 16)
            sp.wait_ge(s_fin[1], ACT_PIECES + 1)
            sp.dma_start(y_s.rearrange("b o d -> (b o) d"), out_s[:, :]).then_inc(s_out, 16)
            sp.wait_ge(s_out, 16 * (2 * QB + 1))

        @block.gpsimd
        def _(pool):
            def low(n, four_i=0, cols=P):
                slot, raw = n % RING, n % 2
                pool.wait_ge(s_hi, four_i + n + 1)
                pool.wait_ge(s_raw[raw], 8 * four_i + 16 * (n // 2 + 1))
                nc.gpsimd.tensor_tensor(w_lo[:, slot, :, 0:cols], w_raw[:, raw, :, 0:cols],
                                        w_hi[:, slot, :, 0:cols].bitcast(F32), ALU.subtract).then_inc(s_lo, 1)

            def low_units(first, last):
                with pool.Fori(0, (last - first) // RING) as i:
                    for u in range(RING):
                        low(first + u, 4 * i)

            for n in range(6):
                low(n, cols=KIWI if n in (2, 3) else P)

            low_units(6, unit_of(TILE_OUT) + 4)
            for k in range(NH):
                pool.wait_ge(s_t1h, k + 1)
                nc.gpsimd.tensor_tensor(a_lo[:, k, :], mix[:, k, :], a_hi[:, k, :].bitcast(F32), ALU.subtract
                                        ).then_inc(s_t1p, 1)
            low_units(unit_of(TILE_OUT) + 4, UNITS)

        @block.tensor
        def _(pe):
            def unit(n, slot, hi, lo, out, first, last, k0=0, cols=P, ready=None):
                pe.wait_ge(s_lo, n + 1)
                for k in range(8):
                    if ready:
                        ready(k0 + k)
                    for part, (w, a) in enumerate(((w_hi, hi), (w_hi, lo), (w_lo, hi))):
                        for half in range(2):
                            last_mm = nc.tensor.matmul(
                                out[:, half, :], w[:, slot, k, 0:cols], a[:, k0 + k, half * HT:(half + 1) * HT],
                                start=(first and k == 0 and part == 0), stop=(last and k == 7 and part == 2))
                return last_mm

            def tile(m, m_static, n, base_unit, cols=P, ready=None, between=None):
                out = pair(m_static % 2)[0:cols]
                if m_static >= 2:
                    pe.wait_ge(s_evac, m - 1)
                a = unit(n, base_unit % RING, a_hi, a_lo, out, True, False, 0, cols, ready)
                a.then_inc(s_used, 1)
                if between:
                    between()
                b = unit(n + 1, (base_unit + 1) % RING, a_hi, a_lo, out, False, True, 8, cols, ready)
                b.then_inc(s_used, 1)

            def x_split(k):
                pe.wait_ge(s_a0, k + 1)

            def mixed_split(k):
                if k < NH:
                    pe.wait_ge(s_t1p, k + 1)
                else:
                    pe.wait_ge(s_t1, k + 1 - NH)

            def h2_split(k):
                pe.wait_ge(s_t2, k + 1)

            def turn(out, x, n):
                return nc.tensor.transpose(out, x, ident[0:n, 0:n])

            def mm(out, lhsT, rhs, start=True, stop=True):
                return nc.tensor.matmul(out, lhsT, rhs, start=start, stop=stop, skip_group_check=True)

            pe.wait_ge(s_cst, 16)
            pe.wait_ge(s_x[4], 16)
            for f in range(KT):
                last = turn(G[:, 0, f * NS:(f + 1) * NS], xs_in[:, f * P:(f + 1) * P], NS)
            last.then_inc(s_xt, 1)
            pe.wait_ge(s_gr, 48)
            turn(G[:, 1, 0:48], graw[:, :], 48).then_inc(s_gt, 1)
            for tb in range(QB):
                pe.wait_ge(s_x[tb], 16)
                for q in range(4):
                    if tb:
                        pe.wait_ge(s_xr, 4 * tb + q - 2)
                    for r in range(4):
                        last = turn(B[:, q, r * P:(r + 1) * P], x_in[:, tb, (4 * q + r) * P:(4 * q + r + 1) * P], P)
                    last.then_inc(s_xt, 1)
            tile(0, 0, 0, 0, ready=x_split)

            def spread_rms():
                pe.wait_ge(s_diag, 1)
                for tb in range(QB):
                    mm(B[:, 0, tb * P:(tb + 1) * P], ones[:, :], rdiag[:, tb, :])
                mm(B[:, 1, 0:NS], ones[0:NS, :], rdiag[0:NS, 4, 0:NS]).then_inc(s_rbm, 1)

            def turn_tokens(src, rows_, m, b):
                pe.wait_ge(s_evac, m + 1)
                for tb in range(QB):
                    last = turn(B[:, b, tb * rows_:(tb + 1) * rows_], src[:, tb * P:(tb + 1) * P], rows_)
                last.then_inc(s_y, 1)
                turn(B[0:NS, b + 1, 0:rows_], src[:, NP_:T], rows_).then_inc(s_y, 1)

            def turn_kiwi():
                pe.wait_ge(s_rbd, 1)
                turn_tokens(kiwi, KIWI, 1, 0)

            def turn_index_keys():
                pe.wait_ge(s_ln, 1)
                pe.wait_ge(s_yd, 4)
                for tb in range(QB):
                    last = turn(B[:, 0, tb * P:(tb + 1) * P], ki_dup[:, tb, :], P)
                last.then_inc(s_kit, 1)
                turn(B[:, 1, 0:NS], ki_dup[0:NS, 4, :], NS)
                turn(B[:, 1, NS:2 * NS], zw[:, :, :].rearrange("b c h -> b (c h)"), NS).then_inc(s_kit, 1)

            def qi_tile(t, **kw):
                tile(TILE_QI + t, TILE_QI + t, unit_of(TILE_QI + t), unit_of(TILE_QI + t), **kw)

            tile(1, 1, 2, 2, KIWI, between=spread_rms)
            qi_tile(0, between=lambda: turn_tokens(kt, P, 0, 2))
            qi_tile(1, between=turn_kiwi)
            with pe.Fori(0, 2) as i:
                for u in range(2):
                    tile(TILE_QI + 2 + 2 * i + u, TILE_QI + 2 + u, unit_of(TILE_QI + 2) + 4 * i + 2 * u,
                         unit_of(TILE_QI + 2 + u))
            qi_tile(6)
            qi_tile(7, between=turn_index_keys)

            pe.wait_ge(s_kitd, 2)
            j = 0
            for h in range(IH):
                for b in range(1, QB):
                    if j >= 4:
                        pe.wait_ge(s_rl, j - 3)
                    if b == 1 and h == IH - 2:
                        pe.wait_ge(s_evac, TILE_QA)
                    mm(B[:, j % 4, 0:P * (b + 1)], qi[:, h // 2, b * P:(b + 1) * P],
                       (kit, kit_o)[h % 2][:, 0:P * (b + 1)]).then_inc(s_is, 1)
                    j += 1
            pe.wait_ge(s_pi, 16 * NS * PAGES)
            pe.wait_ge(s_qis, 1)
            for step in range(NS + 2):
                if step < NS:
                    if step >= 2:
                        pe.wait_ge(s_sk, step - 1)
                    for g in range(0, PAGES, 2):
                        last = turn(G[:, step % 2, g // 2 * P:(g // 2 + 1) * P],
                                    ipages[:, PAGES * step + g:PAGES * step + g + 2, :].rearrange("p a d -> p (a d)"), P)
                    last.then_inc(s_st, 1)
                if step >= 2:
                    b = step - 2
                    pe.wait_ge(s_sk, b + 1)
                    for half in range(2):
                        last = mm(G[:, 2 + half, 0:257], qis[:, P * b:P * b + P], kis[:, b % 2, half, :],
                                  start=(b == 0), stop=(b == NS - 1))
                    last.then_inc(s_ss, 1)
            pe.wait_ge(s_rl, j)
            pe.wait_ge(s_sr, 1)
            for half in range(2):
                last = mm(B[0:NS, half, 0:257], wis[:, :], relu_s[:, half, :])
            last.then_inc(s_sw, 1)

            with pe.Fori(0, 4) as i:
                for u in range(2):
                    tile(TILE_QA + 2 * i + u, TILE_QA + u, unit_of(TILE_QA) + 4 * i + 2 * u, unit_of(TILE_QA) + 2 * u)

            pe.wait_ge(s_pk, 16 * NS * PAGES)
            pe.wait_ge(s_scs, 1)
            for step in range(NS + 1):
                if step < NS:
                    if step >= 2:
                        pe.wait_ge(s_ak, step - 1)
                    for g in range(PAGES):
                        last = turn(B[:, step % 2, g * P:(g + 1) * P], kpages[:, PAGES * step + g, :], P)
                    last.then_inc(s_at, 1)
                if step >= 1:
                    b = step - 1
                    if b == 0:
                        pe.wait_ge(s_qam, 1)
                    pe.wait_ge(s_ak, b + 1)
                    for half in range(2):
                        last = mm(B[0:64, 2 + half, 0:257], qam[:, 64 * b:64 * b + 64],
                                  kt_b[:, b % 2, 257 * half:257 * half + 257], start=(b == 0), stop=(b == NS - 1))
                    last.then_inc(s_aq, 1)
                if step == 2:
                    pe.wait_ge(s_ams, 1)
                    for half in range(2):
                        last = mm(G[0:64, 2 + half, 0:257], expand, score_s[:, 257 * half:257 * half + 257])
                    last.then_inc(s_ax, 1)

            def turn_sample_probs():
                pe.wait_ge(s_ps, 1)
                for g in range(PAGES):
                    last = turn(B[:, 0, g * 64:(g + 1) * 64], p_s[:, g * P:(g + 1) * P], 64)
                last.then_inc(s_apt, 1)
                pe.wait_ge(s_dg, 1)
                mm(B[0:NS, 1, 0:64], fold, diag_s[:, :]).then_inc(s_apt, 1)

            tile(TILE_VA, TILE_VA, unit_of(TILE_VA), unit_of(TILE_VA), between=turn_sample_probs)
            pe.wait_ge(s_xd, TAKEN0)
            pe.wait_ge(s_pv, 16 * NS * PAGES)
            for b in range(NS):
                for g in range(PAGES):
                    mm(B[:, 0, NH * b:NH * b + NH], vpages[:, PAGES * b + g, :], pt_s[:, g, NH * b:NH * b + NH],
                       start=(g == 0), stop=(g == PAGES - 1))
            turn_tokens(vt, P, TILE_VA, 2)
            pe.wait_ge(s_yd, 6)
            mm(B[:, 1, 0:64], vs[:, :], pown_s[:, :]).then_inc(s_so, 1)

            with pe.Fori(0, NH) as i:
                m0, n0 = TILE_HEAD + 4 * i, unit_of(TILE_HEAD) + 8 * i
                e0 = 24 * i

                def head_tile(u, between=None):
                    tile(m0 + u, TILE_HEAD + u, n0 + 2 * u, unit_of(TILE_HEAD) + 2 * u, between=between)

                def fill(e):
                    pe.wait_ge(s_xd, e0 + TAKEN0 + max(e - 3, 0))
                    return e % 4

                def values_and_scores():
                    pe.wait_ge(s_evac, m0 + 1)
                    pe.wait_ge(s_head, i + 1)
                    x = fill(0)
                    for k in range(QB):
                        last = turn(B[:, x, k * P:(k + 1) * P], rv[:, k * P:(k + 1) * P], P)
                    last.then_inc(s_xp, 1)
                    turn(B[0:NS, fill(1), 0:P], rv[:, NP_:T], P).then_inc(s_xp, 1)
                    pe.wait_ge(s_qc, i + 1)
                    for b in range(QB):
                        mm(B[:, fill(2 + b), 0:P * (b + 1)], qc[:, b * P:(b + 1) * P], kt[:, 0:P * (b + 1)]
                           ).then_inc(s_xp, 1)

                def output_and_decay():
                    x = fill(10)
                    pe.wait_ge(s_xd, e0 + TAKEN0 + 10)
                    for k in range(QB):
                        last = mm(B[:, x, k * P:NP_], vtok[:, k, :], pt_h[:, KOFF[k]:KOFF[k] + NP_ - k * P],
                                  start=(k == 0), stop=(k == QB - 1))
                    last.then_inc(s_xp, 1)
                    pe.wait_ge(s_rk, i + 1)
                    for k in range(QB):
                        mm(B[:, fill(11 + k), 0:NP_ - k * P], rk[:, k * P:(k + 1) * P], rq[:, k * P:NP_]
                           ).then_inc(s_xp, 1)
                    x = fill(15)
                    for k in range(QB):
                        last = turn(B[:, x, k * P:(k + 1) * P], rk[:, k * P:(k + 1) * P], P)
                    last.then_inc(s_xp, 1)
                    turn(B[0:NS, fill(16), 0:P], rk[:, NP_:T], P).then_inc(s_xp, 1)

                head_tile(0)
                head_tile(1, between=values_and_scores)
                head_tile(2)
                pe.wait_ge(s_pn, i + 1)
                for k in range(QB):
                    x = fill(6 + k)
                    for b in range(k, QB):
                        last = turn(B[:, x, (b - k) * P:(b - k + 1) * P],
                                    p_h[:, QOFF[b] + k * P:QOFF[b] + (k + 1) * P], P)
                    last.then_inc(s_xp, 1)
                head_tile(3, between=output_and_decay)
                pe.wait_ge(s_vbd, i + 1)
                for j in range(2):
                    x = fill(17 + j)
                    pe.wait_ge(s_xd, e0 + TAKEN0 + 17)
                    mm(B[:, x, :], ks_tok[:, :], vbd[:, 4 * j:4 * j + 4, :]).then_inc(s_xp, 1)
                x = fill(19)
                for k in range(QB):
                    last = mm(B[:, x, k * P:NP_], vtok_r[:, k, :], sd_h[:, KOFF[k]:KOFF[k] + NP_ - k * P],
                              start=(k == 0), stop=(k == QB - 1))
                last.then_inc(s_xp, 1)
                x = fill(20)
                for k in range(QB):
                    last = mm(B[:, x, 0:P], ktok[:, k, :], vtok_r[:, k, :], start=(k == 0), stop=(k == QB - 1))
                last.then_inc(s_xp, 1)
                x = fill(21)
                pe.wait_ge(s_xd, e0 + TAKEN0 + 19)
                for b in range(NS):
                    last = mm(B[:, x, b:b + 1], rs[:, b, :], rq[:, NP_ + b:NP_ + b + 1])
                last.then_inc(s_xp, 1)
                for n, cols in enumerate((slice(0, NP_), slice(NP_, T))):
                    pe.wait_ge(s_sq, 2 * i + 1 + n)
                    mm(B[:, fill(22 + n), 0:cols.stop - cols.start], ones[:, :], rv[:, cols]).then_inc(s_xp, 1)

            for n, (t, half) in enumerate(((0, 0), (1, 0), (0, 1), (1, 1))):
                if half == 0:
                    pe.wait_ge(s_evac, TILE_OUT + t - 1)
                n += unit_of(TILE_OUT)
                unit(n, n % RING, a_hi, a_lo, pair((TILE_OUT + t) % 2), half == 0, half == 1, 8 * half,
                     ready=mixed_split).then_inc(s_used, 1)
            with pe.Fori(1, KT // 2) as i:
                for u in range(2):
                    tile(TILE_OUT + 2 * i + u, TILE_OUT + u, unit_of(TILE_OUT) + 4 * i + 2 * u,
                         unit_of(TILE_OUT) + 2 * u)

            def spread_squares():
                pe.wait_ge(s_n2, KT + 1)
                for half in range(2):
                    last = mm(B[:, half, 0:HT], ones[:, :], ssum[:, half * HT:(half + 1) * HT])
                last.then_inc(s_n2m, 1)

            def up(m0, n0, first=0):
                with pe.Fori(first, CH // 2) as i:
                    for u in range(2):
                        tile(m0 + 2 * i + u, TILE_MLP + u, n0 + 4 * i + 2 * u, unit_of(TILE_MLP) + 2 * u)

            def down(m0, n0, ready_at, t, u):
                pe.wait_ge(s_evac, m0 + CH + t - 1)
                unit(n0 + 16 + t, (unit_of(TILE_MLP) + u) % RING, b_hi, b_lo, pair((TILE_MLP + u) % 2), True, True,
                     ready=lambda k: pe.wait_ge(s_b, ready_at + k + 1)).then_inc(s_used, 1)

            def turn_rows(f):
                pe.wait_ge(s_yt, f + 1)
                if f >= 2:
                    pe.wait_ge(s_ye, f - 1)
                b = 2 * (f % 2)
                for tb in range(QB):
                    turn(B[:, b, tb * P:(tb + 1) * P], yt[:, f % 2, tb * P:(tb + 1) * P], P)
                turn(B[0:NS, b + 1, 0:P], yt[:, f % 2, NP_:T], P).then_inc(s_yx, 1)

            def down_all(m0, n0, ready_at):
                with pe.Fori(0, KT // 4) as i:
                    for u in range(4):
                        down(m0, n0, ready_at, 4 * i + u, u)

            m0, n0 = TILE_MLP, unit_of(TILE_MLP)
            tile(m0, m0, n0, n0, ready=h2_split, between=spread_squares)
            tile(m0 + 1, m0 + 1, n0 + 2, n0 + 2)
            up(m0, n0, first=1)
            down_all(m0, n0, 0)
            with pe.Fori(1, NCHUNK - 1) as c:
                m0, n0 = TILE_MLP + 24 * c, unit_of(TILE_MLP) + 32 * c
                up(m0, n0)
                down_all(m0, n0, CH * c)
            up(LAST_TILE, LAST_UNIT)
            for t in range(KT):
                down(LAST_TILE, LAST_UNIT, CH * (NCHUNK - 1), t, t)
                if t:
                    turn_rows(t - 1)
            for n, x in enumerate((ssum, sq)):
                pe.wait_ge(s_nf, n + 1)
                for tb in range(5):
                    tok = slice(tb * P, min(tb * P + P, T))
                    last = mm(G[0:tok.stop - tok.start, 2 - 2 * n, tb:tb + 1], x[:, tok], ones[:, 0:1])
                last.then_inc(s_nfm, 1)
            turn_rows(KT - 1)

        @block.scalar
        def _(act):
            def high(n, four_i=0, cols=P):
                act.wait_ge(s_raw[n % 2], 8 * four_i + 16 * (n // 2 + 1))
                if n >= RING:
                    act.wait_ge(s_used, four_i + n - 3)
                nc.scalar.copy(w_hi[:, n % RING, :, 0:cols], w_raw[:, n % 2, :, 0:cols]).then_inc(s_hi, 1)

            def act_fn(out, in_, fn, **kw):
                return nc.scalar.activation(out, in_, fn, **kw)

            for n, g in enumerate((norm1_g, norm2_g, final_norm_g)):
                act.dma_start(graw[16 * n:16 * n + 16, :], g.rearrange("(k p) -> k p", p=P)).then_inc(s_gr, 16)
            act.wait_ge(s_set, 1)
            for nth, tb in enumerate((4, 0, 1, 2, 3)):
                act.wait_ge(s_x[tb], 16)
                n = NS if tb == 4 else P
                for half in range(2):
                    if nth or half:
                        act.wait_ge(s_ssq, 2 * nth + half)
                    x = (xs_in[:, :] if tb == 4 else x_in[:, tb, :])[:, half * 1024:(half + 1) * 1024]
                    act_fn(G[0:n, 2:4, :].rearrange("p a b -> p (a b)"), x, ACT.Square,
                           accum_out=st[0:n, 5 * half + tb:5 * half + tb + 1]).then_inc(s_ssq, 1)
                if tb == 2:
                    high(0)
            act.wait_ge(s_gc, 1)
            for f in range(KT):
                if f == 2:
                    high(1)
                if f == KT // 2:
                    act.dma_start(xt_dram[:, 0:KT // 2, :], xr[:, 0:KT // 2, :]).then_inc(s_spill, 16)
                act.wait_ge(s_xr, 4 * (QB - 1) + f // 4 + 2)
                act_fn(a_hi[:, f, :], xr[:, f, :], ACT.Identity, scale=g1[:, f:f + 1]).then_inc(s_a0h, 1)
            high(2, cols=KIWI)
            act.wait_ge(s_var, 1)
            act_fn(st[:, 10:15], st[:, 5:10], ACT.Sqrt).then_inc(s_sqrt, 1)
            high(3, cols=KIWI)
            act.dma_start(cs[:, :, :], rotary).then_inc(s_rot, 16)
            for n, g in enumerate((idx_k_norm_g, idx_k_norm_b)):
                act.dma_start(lng[:, n, :], g[None, :].to_broadcast([P, ID])).then_inc(s_lng, 16)
            for n in range(4, 10):
                if n == 6:
                    act.dma_start(xt_dram[:, KT // 2:, :], xr[:, KT // 2:, :]).then_inc(s_spill, 16)
                high(n)
            act.wait_ge(s_yd, 2)
            act.dma_start(k_p[0].rearrange("(k p) d -> p k d", p=P), kout[:, :, :]).then_inc(s_kvo, 16)
            act.dma_start(k_s.rearrange("b o d -> (b o) d"), kout_s[:, :]).then_inc(s_kvo, 16)
            act.wait_ge(s_lnv, 1)
            act_fn(st[:, 10:15], st[:, 5:10], ACT.Sqrt).then_inc(s_lns, 1)
            act.wait_ge(s_ln, 1)
            act.dma_start(ik_p[0].rearrange("(k p) d -> p k d", p=P), ki_dup[:, 0:QB, 0:ID]).then_inc(s_rst, 16)
            act.dma_start(ik_s.rearrange("b o d -> (b o) d"), ki_dup[0:NS, 4, 0:ID]).then_inc(s_rso, 16)
            with act.Fori(0, 3) as i:
                for u in range(4):
                    high(unit_of(TILE_QI) + 6 + u, 4 * i)
            for n in range(unit_of(TILE_QA) + 2, unit_of(TILE_QA) + 4):
                high(n)
            j = 0
            for h in range(IH):
                for b in range(1, QB):
                    act.wait_ge(s_is, j + 1)
                    if j >= 2:
                        act.wait_ge(s_ic, j - 1)
                    act_fn(relu_p[:, j % 2, 0:P * (b + 1)], B[:, j % 4, 0:P * (b + 1)], ACT.Relu).then_inc(s_rl, 1)
                    j += 1
            act.wait_ge(s_ss, NS)
            act_fn(relu_s[:, :, :], G[:, 2:4, 0:257], ACT.Relu).then_inc(s_sr, 1)
            with act.Fori(0, 4) as i:
                for u in range(4):
                    high(unit_of(TILE_QA) + 4 + u, 4 * i)
            for b in range(NS):
                act.wait_ge(s_at, b + 1)
                if b >= 2:
                    act.wait_ge(s_aq, b - 1)
                nc.scalar.copy(kt_b[:, b % 2, 0:CL], B[:, b % 2, :])
                nc.scalar.copy(kt_b[:, b % 2, CL:CL + 1], kt[:, NP_ + b:NP_ + b + 1]).then_inc(s_ak, 1)
            act.wait_ge(s_nms, 1)
            act_fn(p_s[:, :], p_s[:, :], ACT.Exp, bias=st[0:64, 42:43], accum_out=st[0:64, 43:44]).then_inc(s_exps, 1)

            for u in range(2):
                high(unit_of(TILE_HEAD) + 2 + u)
            act.wait_ge(s_yd, 6)
            act.dma_start(v_p[0].rearrange("(k p) d -> p k d", p=P), vtok[:, :, :]).then_inc(s_kvo, 16)
            act.dma_start(v_s.rearrange("b o d -> (b o) d"), vs[:, :]).then_inc(s_kvo, 16)

            def mixed(first, last):
                for k in range(first, last):
                    nc.scalar.copy(a_hi[:, k, :], mix[:, k, :]).then_inc(s_t1h, 1)

            def act_head(i, last=False):
                base, i8 = unit_of(TILE_HEAD) + 4, 8 * i

                def swap(m, p):
                    act.wait_ge(s_used, 2 * m + 2)
                    for low, high_ in ((0, 64), (64, 0)):
                        ins = nc.scalar.copy(halves(t2[low:low + 64, :]), G[high_:high_ + 64, 2 * p:2 * p + 2, 0:HT])
                    ins.then_inc(s_swap, 1)

                high(base, i8)
                high(base + 1, i8)
                for b in range(QB):
                    act.wait_ge(s_nm, 4 * i + b + 1)
                    n = slice(QOFF[b], QOFF[b] + P * (b + 1))
                    act_fn(p_h[:, n], p_h[:, n], ACT.Exp, bias=st[:, 25 + b:26 + b],
                           accum_out=st[:, 29 + b:30 + b]).then_inc(s_exp, 1)
                high(base + 2, i8)
                high(base + 3, i8)
                swap(TILE_HEAD + 1 + 4 * i, (TILE_HEAD + 1) % 2)
                high(base + 4, i8)
                high(base + 5, i8)
                act.wait_ge(s_rq, i + 1)
                swap(TILE_HEAD + 2 + 4 * i, TILE_HEAD % 2)
                high(base + 6, i8)
                high(base + 7, i8)
                act.wait_ge(s_evac, TILE_HEAD + 4 * i + 4)
                act_fn(t2[:, :], rg[:, :], ACT.Tanh, scale=0.5).then_inc(s_th, 1)
                if last:
                    mixed(0, 4)
                act.wait_ge(s_xd, 24 * i + TAKEN0 + 20)
                act_fn(rv[:, 0:NP_], ro[:, 0:NP_], ACT.Square).then_inc(s_sq, 1)
                act.wait_ge(s_xd, 24 * i + TAKEN0 + 22)
                act_fn(rv[:, NP_:T], ro[:, NP_:T], ACT.Square).then_inc(s_sq, 1)
                act.dma_start(rs_p[0, one(i), :, :].rearrange("a d e -> (a d) e"), rst[:, :]).then_inc(s_rst, 16)
                act.dma_start(rs_s[:, one(i), :, :].rearrange("b a d e -> d (b a) e"), rs[:, :, :]).then_inc(s_rso, 16)
                if last:
                    mixed(4, 5)
                act.wait_ge(s_xd, 24 * i + TAKEN0 + 24)
                act_fn(rk[:, :], rv[:, :], ACT.Sqrt).then_inc(s_hs, 1)

            with act.Fori(0, NH - 1) as i:
                act_head(i)
            act_head(NH - 1, last=True)

            mixed(5, KT - 1)
            act.wait_ge(s_head, NH + 1)
            mixed(KT - 1, KT)
            act.dma_start(xr[:, :, :], xt_dram).then_inc(s_xb, 16)
            with act.Fori(0, KT // 2 - 1) as i:
                for u in range(4):
                    high(unit_of(TILE_OUT) + 4 + u, 4 * i)
            first = unit_of(TILE_MLP)
            for n in range(first, first + 3):
                high(n)
            for k in range(KT):
                if k == 0:
                    act.wait_ge(s_used, first - 1)
                    act.wait_ge(s_evac, TILE_MLP - 1)
                elif k == 8:
                    high(first + 3)
                elif k == KT - 1:
                    act.wait_ge(s_evac, TILE_MLP)
                act_fn(a_hi[:, k, :], xr[:, k, :], ACT.Identity, scale=g2[:, k:k + 1]).then_inc(s_t2h, 1)
            act.wait_ge(s_n2v, 1)
            act_fn(ny[:, :], nv[:, :], ACT.Sqrt).then_inc(s_n2s, 1)
            first, last_down = unit_of(TILE_MLP) + 4, UNITS - KT
            with act.Fori(0, (last_down - first) // 4) as i:
                for u in range(4):
                    high(first + u, 4 * i)

            def rows_of(f):
                act.wait_ge(s_yx, f + 1)
                b = 2 * (f % 2)
                nc.scalar.copy(out_t[:, :, f * P:(f + 1) * P], B[:, b, :].rearrange("p (k d) -> p k d", d=P))
                nc.scalar.copy(out_s[:, f * P:(f + 1) * P], B[0:NS, b + 1, 0:P]).then_inc(s_ye, 1)

            for t in range(KT):
                high(last_down + t)
                if t >= 5:
                    rows_of(t - 5)
            for f in range(KT - 5, KT):
                if f == KT - 1:
                    act.wait_ge(s_nfv, 1)
                    act_fn(st[:, 75:80], st[:, 70:75], ACT.Sqrt).then_inc(s_nfs, 1)
                rows_of(f)
            act.wait_ge(s_rn, 1)
            act.wait_ge(s_ye, KT)
            for s, _, tb, half in PIECES:
                if s == 1:
                    x = out_t[:, tb, half * D // 2:(half + 1) * D // 2]
                    act_fn(x, x, ACT.Identity, scale=st[:, 75 + tb:76 + tb]).then_inc(s_fin[1], 1)
            act_fn(out_s[:, :], out_s[:, :], ACT.Identity, scale=st[0:NS, 79:80]).then_inc(s_fin[1], 1)

        @block.vector
        def _(dve):
            v = nc.vector
            step = Chain(dve, s_chain)

            def newton(y, var, t, done=None):
                step(v.reciprocal(y, y))
                step(v.tensor_tensor(t, var, y, ALU.mult))
                step(v.tensor_tensor(t, t, y, ALU.mult))
                step(v.tensor_scalar(t, t, -0.5, 1.5, ALU.mult, ALU.add))
                ins = v.tensor_tensor(y, y, t, ALU.mult)
                if done:
                    ins.then_inc(done, 1)
                else:
                    step(ins)

            step(v.memset(ones[:, :], 1.0))
            v.memset(st[:, :], 1.0).then_inc(s_set, 1)
            dve.wait_ge(s_xt, 1)
            v.tensor_copy(xr[:, :, NP_:T], G[:, 0, 0:KT * NS].rearrange("p (f n) -> p f n", n=NS)).then_inc(s_xr, 1)
            dve.wait_ge(s_gt, 1)
            v.tensor_copy(gcol[:, :], G[:, 1, 0:48]).then_inc(s_gc, 1)
            for tb in range(QB):
                for q in range(4):
                    dve.wait_ge(s_xt, 4 * tb + q + 2)
                    v.tensor_copy(xr[:, 4 * q:4 * q + 4, tb * P:(tb + 1) * P],
                                  B[:, q, :].rearrange("p (f n) -> p f n", n=P)).then_inc(s_xr, 1)
            dve.wait_ge(s_gc, 1)
            for f in range(KT):
                dve.wait_ge(s_a0h, f + 1)
                v.scalar_tensor_tensor(out=a_lo[:, f, :], in0=xr[:, f, :], scalar=g1[:, f:f + 1],
                                       in1=a_hi[:, f, :].bitcast(F32), op0=ALU.mult, op1=ALU.subtract).then_inc(s_a0, 1)
            dve.wait_ge(s_ssq, 10)
            step(v.tensor_tensor(st[:, 5:10], st[:, 0:5], st[:, 5:10], ALU.add))
            v.tensor_scalar(st[:, 5:10], st[:, 5:10], 1.0 / D, EPS, ALU.mult, ALU.add).then_inc(s_var, 1)
            dve.wait_ge(s_sqrt, 1)
            newton(st[:, 10:15], st[:, 5:10], st[:, 15:20])
            dve.wait_ge(s_cst, 16)
            for tb in range(5):
                last = v.tensor_scalar(rdiag[:, tb, :], ident, st[:, 10 + tb:11 + tb], None, ALU.mult)
            last.then_inc(s_diag, 1)
            dve.wait_ge(s_rbm, 1)
            v.tensor_copy(rb[:, 0:NP_], B[:, 0, :])
            v.tensor_copy(rb[:, NP_:T], B[:, 1, 0:NS]).then_inc(s_rbd, 1)
            dve.wait_ge(s_rbd, 1)

            def scaled(out, m, p, rows_=P):
                dve.wait_ge(s_used, 2 * m + 2)
                v.tensor_tensor(out, pair(p, rows_), halves(rb[0:rows_, :]), ALU.mult).then_inc(s_evac, 1)

            scaled(halves(kt[:, :]), 0, 0)
            scaled(halves(kiwi[:, :]), 1, 1, KIWI)
            dve.wait_ge(s_y, 1)
            v.tensor_copy(kout[:, :, :], B[:, 2, :].rearrange("p (k d) -> p k d", d=P)).then_inc(s_yd, 1)
            dve.wait_ge(s_y, 2)
            v.tensor_copy(kout_s[:, :], B[0:NS, 3, 0:P]).then_inc(s_yd, 1)

            def qi_taken(t):
                scaled(halves(qi[:, t, :]), TILE_QI + t, (TILE_QI + t) % 2)

            dve.wait_ge(s_spill, 32)
            qi_taken(0)
            step(v.memset(ki5[:, 4, :], 0.0))
            dve.wait_ge(s_y, 3)
            v.tensor_copy(ki5[:, 0:QB, :], B[:, 0, 0:QB * KIWI].rearrange("p (k d) -> p k d", d=KIWI)).then_inc(s_yd, 1)
            dve.wait_ge(s_y, 4)
            v.tensor_copy(ki5[0:NS, 4, :], B[0:NS, 1, 0:KIWI]).then_inc(s_yd, 1)
            dve.wait_ge(s_yd, 4)
            dve.wait_ge(s_lng, 32)
            ki, mu, var, y5, t5 = ki5[:, :, 0:ID], st[:, 20:25], st[:, 5:10], st[:, 10:15], st[:, 15:20]

            def spread(x):
                return x.unsqueeze(2).to_broadcast([P, 5, ID])

            def per_column(x):
                return x.unsqueeze(1).to_broadcast([P, 5, ID])

            wscale = IH ** -0.5 * ID ** -0.5
            step(v.tensor_scalar(wi[:, :, :], ki5[:, :, ID:KIWI], wscale, None, ALU.mult))
            step(v.tensor_tensor(zw[:, :, :], wi[0:NS, 4, :].unsqueeze(1).to_broadcast([NS, NS, IH]),
                                 ident[0:NS, 0:NS].unsqueeze(2).to_broadcast([NS, NS, IH]), ALU.mult))
            step(v.tensor_reduce(mu, ki, X, ALU.add))
            step(v.tensor_scalar(mu, mu, 1.0 / ID, None, ALU.mult))
            step(v.tensor_tensor(xc[:, :, :], ki, spread(mu), ALU.subtract))
            step(v.tensor_tensor(sq5[:, :, :], xc[:, :, :], xc[:, :, :], ALU.mult))
            step(v.tensor_reduce(var, sq5[:, :, :], X, ALU.add))
            step(v.tensor_scalar(var, var, 1.0 / ID, EPS, ALU.mult, ALU.add))
            last = v.tensor_copy(t5, var)
            last.then_inc(s_lnv, 1)
            dve.wait_ge(s_lns, 1)
            newton(y5, var, t5)
            step(v.tensor_tensor(xc[:, :, :], xc[:, :, :], spread(y5), ALU.mult))
            step(v.tensor_tensor(xc[:, :, :], xc[:, :, :], per_column(lng[:, 0, :]), ALU.mult))
            dve.wait_ge(s_spill, 32)
            v.tensor_tensor(ki_dup[:, :, 0:ID], xc[:, :, :], per_column(lng[:, 1, :]), ALU.add)
            v.tensor_tensor(ki_dup[:, :, ID:2 * ID], xc[:, :, :], per_column(lng[:, 1, :]), ALU.add).then_inc(s_ln, 1)
            dve.wait_ge(s_ln, 1)
            v.memset(kit[ID:P, :], 0.0)
            v.memset(kit_o[0:ID, :], 0.0)
            v.memset(qam[:, :], 0.0)
            v.memset(kis[:, :, :, :], 0.0)
            step(v.memset(qis[:, :], 0.0))
            qi_taken(1)
            dve.wait_ge(s_rot, 16)
            for n in range(2):
                step(v.tensor_tensor(cs[:, n, :], cs[:, n, :], rb[:, :], ALU.mult))
            with dve.Fori(0, 2) as i:
                for u in range(2):
                    t = 2 + 2 * i + u
                    scaled(halves(row(qi, t)), TILE_QI + t, (TILE_QI + u) % 2)
            qi_taken(6)
            dve.wait_ge(s_kit, 2)
            v.tensor_copy(kit[0:ID, 0:NP_], B[0:ID, 0, :])
            v.tensor_copy(kit_o[ID:P, :], B[ID:P, 0, :]).then_inc(s_kitd, 1)
            v.tensor_copy(wis[:, :], B[:, 1, NS:2 * NS])
            v.tensor_copy(kit[0:ID, NP_:T], B[0:ID, 1, 0:NS]).then_inc(s_kitd, 1)
            qi_taken(7)
            dve.wait_ge(s_evac, TILE_QA)
            q4 = qis[:, :].rearrange("p (b x) -> p b x", x=144)[:, :, 0:IH].rearrange("p b (t two) -> p t b two", two=2)
            for rows_ in (slice(0, ID), slice(ID, P)):
                v.tensor_copy(q4[rows_, :, :, 0], qi[0:ID, :, NP_:T])
                last = v.tensor_copy(q4[rows_, :, :, 1], qi[ID:P, :, NP_:T])
            last.then_inc(s_qis, 1)
            dve.wait_ge(s_kvo, 32)
            j = 0
            for h in range(IH):
                for b in range(1, QB):
                    n = P * (b + 1)
                    dve.wait_ge(s_rl, j + 1)
                    if h == 0:
                        ins = v.tensor_scalar(score[:, b - 1, 0:n], relu_p[:, j % 2, 0:n], wi[:, b, h:h + 1], None,
                                              ALU.mult)
                    else:
                        dve.wait_ge(s_ic, j - 2)
                        ins = v.scalar_tensor_tensor(out=score[:, b - 1, 0:n], in0=relu_p[:, j % 2, 0:n],
                                                     scalar=wi[:, b, h:h + 1], in1=score[:, b - 1, 0:n],
                                                     op0=ALU.mult, op1=ALU.add)
                    ins.then_inc(s_ic, 1)
                    j += 1
            for b in range(NS):
                dve.wait_ge(s_st, b + 1)
                if b >= 2:
                    dve.wait_ge(s_ss, b - 1)
                v.tensor_copy(kis[0:ID, b % 2, 0, 0:256], G[0:ID, b % 2, 0:256])
                v.tensor_copy(kis[ID:P, b % 2, 1, 0:256], G[ID:P, b % 2, 0:256])
                v.tensor_copy(kis[0:ID, b % 2, 0, 256:257], kit[0:ID, NP_ + b:NP_ + b + 1]).then_inc(s_sk, 1)
            dve.wait_ge(s_ic, j)
            for b in range(1, QB):
                diag = score[:, b - 1, b * P:(b + 1) * P]
                last = v.tensor_tensor(diag, diag, cmask, ALU.add)
            step(last)
            dve.wait_ge(s_sw, 1)
            v.memset(kt_b[:, :, CL + 1:CW], 0.0)
            v.memset(score_s[:, CL + 1:CW], MASKED)
            v.tensor_copy(score_s[:, CL:CL + 1], B[0:NS, 0, 256:257])
            for half in range(2):
                last = v.tensor_copy(score_s[:, 0:CL].rearrange("b (j two n) -> b two j n", two=2, n=P)[:, half],
                                     B[0:NS, half, 0:256].rearrange("b (j n) -> b j n", n=P))
            last.then_inc(s_scs, 1)
            dve.wait_ge(s_scs, 1)

            dve.wait_ge(s_rst, 16)
            dve.wait_ge(s_rso, 16)
            with step.loop(4, 4 * 4 * 2) as i:
                def take(*blocks):
                    done = {}
                    for r in range(TOPK // 8 // 4):
                        for find in (True, False):
                            for n, scores in enumerate(blocks):
                                m8 = st[0:scores.shape[0], 48 + 8 * n:56 + 8 * n]
                                if n in done:
                                    step.wait(done[n])
                                    v.tensor_copy(st[:, 65 + n:66 + n], st[:, 64:65])
                                done[n] = step.mark(v.max(m8, scores) if find else
                                                    v.match_replace(scores, m8, scores, TAKEN))
                    step.wait(done[1])
                    v.tensor_copy(st[:, 66:67], st[:, 64:65])

                for u in range(2):
                    take(*((score[:, 0, 0:2 * P], score[:, 1, 0:3 * P]), (score[:, 2, :], score_s[:, :]))[u])
                    t = 2 * i + u
                    scaled(halves(row(qa, t)), TILE_QA + t, (TILE_QA + u) % 2)
            dve.wait_ge(s_evac, TILE_VA)
            v.tensor_copy(qam[:, :].rearrange("p (b x) -> p b x", x=72)[:, :, 0:NH],
                          qa[:, :, NP_:T].rearrange("p h b -> p b h")).then_inc(s_qam, 1)
            v.tensor_scalar(score_s[:, :], score_s[:, :], TAKEN, MASKED, ALU.not_equal, ALU.mult).then_inc(s_ams, 1)
            for b in range(1, QB):
                n = P * (b + 1)
                last = v.tensor_scalar(am[:, b - 1, 0:n], score[:, b - 1, 0:n], TAKEN, MASKED, ALU.not_equal, ALU.mult)
            step(last)
            scale = P ** -0.5
            dve.wait_ge(s_ax, 1)
            step(v.tensor_copy(halves(am_s[:, :]), G[0:64, 2:4, 0:257]))
            dve.wait_ge(s_aq, NS)
            step(v.scalar_tensor_tensor(out=halves(p_s[:, :]), in0=B[0:64, 2:4, 0:257], scalar=scale,
                                        in1=halves(am_s[:, :]), op0=ALU.mult, op1=ALU.add))
            v.tensor_reduce(st[0:64, 42:43], p_s[:, :], X, ALU.max, negate=True).then_inc(s_nms, 1)
            dve.wait_ge(s_exps, 1)
            step(v.reciprocal(st[0:64, 44:45], st[0:64, 43:44]))
            v.tensor_scalar(p_s[:, :], p_s[:, :], st[0:64, 44:45], None, ALU.mult).then_inc(s_ps, 1)
            dve.wait_ge(s_ps, 1)
            v.tensor_scalar(diag_s[:, :], ident[0:64, 0:64], p_s[:, CL:CL + 1], None, ALU.mult).then_inc(s_dg, 1)
            dve.wait_ge(s_apt, 1)
            v.tensor_copy(pt_s[:, :, :], B[:, 0, 0:256].rearrange("p (k n) -> p k n", n=64)).then_inc(s_xd, 1)
            dve.wait_ge(s_apt, 2)
            v.tensor_copy(pown_s[:, :], B[0:NS, 1, 0:64]).then_inc(s_xd, 1)
            scaled(halves(vt[:, :]), TILE_VA, TILE_VA % 2)
            dve.wait_ge(s_y, 5)
            v.tensor_copy(vtok[:, :, :], B[:, 2, :].rearrange("p (k d) -> p k d", d=P)).then_inc(s_yd, 1)
            dve.wait_ge(s_y, 6)
            v.tensor_copy(vs[:, :], B[0:NS, 3, 0:P]).then_inc(s_yd, 1)
            dve.wait_ge(s_so, 1)
            o_pages, o_own = (B[:, b, 0:64].rearrange("p (b h) -> p h b", h=NH) for b in range(2))
            step(v.tensor_copy(mix[:, 0:NH, NP_:T], o_pages))
            v.tensor_tensor(mix[:, 0:NH, NP_:T], o_own, mix[:, 0:NH, NP_:T], ALU.add).then_inc(s_head, 1)

            def split_thirds(out, x, parts):
                hi = out[0:NS, :]
                step(v.tensor_copy(hi, x))
                for r, part in list(zip(THIRDS, parts))[1:]:
                    dst = out[r:r + NS, :]
                    last = v.tensor_copy(dst, x) if part == "hi" else v.tensor_tensor(dst, x, hi.bitcast(F32), ALU.subtract)
                return last

            v.memset(ks_tok[:, :].bitcast(F32), 0.0)
            step(v.memset(vs_tok[:, :].bitcast(F32), 0.0))
            with step.loop(NH, 14) as i:
                m0, e0 = TILE_HEAD + 4 * i, 24 * i

                def full(e):
                    dve.wait_ge(s_xp, e0 + e + 1)
                    return e % 4

                def rotate(out, m, p, s_out, nth, c):
                    dve.wait_ge(s_used, 2 * m + 2)
                    dve.wait_ge(s_swap, 2 * i + nth)
                    v.scalar_tensor_tensor(out=halves(out), in0=pair(p), scalar=c, in1=halves(cs[:, 0, :]),
                                           op0=ALU.mult, op1=ALU.mult)
                    v.scalar_tensor_tensor(out=t2[:, :], in0=t2[:, :], scalar=c, in1=cs[:, 1, :],
                                           op0=ALU.mult, op1=ALU.mult).then_inc(s_evac, 1)
                    dve.wait_ge(s_evac, m + 1)
                    v.tensor_tensor(out, out, t2[:, :], ALU.add).then_inc(s_out, 1)

                v.tensor_copy(st[:, 37:41], zeta[:, :, one(i)].rearrange("p k o -> p (k o)"))
                step(v.tensor_copy(st[:, 41:42], gamma[:, one(i)]))
                v.tensor_copy(qc[:, :], row(qa, i)[:, 0:NP_]).then_inc(s_qc, 1)
                scaled(halves(rv[:, :]), m0, TILE_HEAD % 2)
                v.tensor_copy(vtok_r[:, :, :], B[:, full(0), :].rearrange("p (k d) -> p k d", d=P)).then_inc(s_xd, 1)
                split_thirds(vs_tok, B[0:NS, full(1), 0:P], ("hi", "lo", "hi")).then_inc(s_xd, 1)
                for b in range(QB):
                    n = slice(QOFF[b], QOFF[b] + P * (b + 1))
                    x = full(2 + b)
                    v.scalar_tensor_tensor(out=p_h[:, n], in0=B[:, x, 0:P * (b + 1)], scalar=scale,
                                           in1=cmask if b == 0 else am[:, b - 1, 0:P * (b + 1)],
                                           op0=ALU.mult, op1=ALU.add).then_inc(s_xd, 1)
                    dve.wait_ge(s_xd, e0 + TAKEN0 + b + 3)
                    v.tensor_reduce(st[:, 25 + b:26 + b], p_h[:, n], X, ALU.max, negate=True).then_inc(s_nm, 1)
                for b in range(QB):
                    n = slice(QOFF[b], QOFF[b] + P * (b + 1))
                    dve.wait_ge(s_exp, 4 * i + b + 1)
                    step(v.reciprocal(st[:, 33 + b:34 + b], st[:, 29 + b:30 + b]))
                    last = v.tensor_scalar(p_h[:, n], p_h[:, n], st[:, 33 + b:34 + b], None, ALU.mult)
                last.then_inc(s_pn, 1)
                rotate(rq[:, :], m0 + 1, (TILE_HEAD + 1) % 2, s_rq, 1, 1.0)
                for k in range(QB):
                    n = NP_ - k * P
                    v.tensor_copy(pt_h[:, KOFF[k]:KOFF[k] + n], B[:, full(6 + k), 0:n]).then_inc(s_xd, 1)
                rotate(rk[:, :], m0 + 2, TILE_HEAD % 2, s_rk, 2, P ** -0.5)
                v.tensor_copy(row(mix, i)[:, 0:NP_], B[:, full(10), :]).then_inc(s_xd, 1)
                dve.wait_ge(s_dh, 16 * i + 16)
                for k in range(QB):
                    n = NP_ - k * P
                    v.tensor_tensor(sd_h[:, KOFF[k]:KOFF[k] + n], B[:, full(11 + k), 0:n], dh[:, 0:n], ALU.mult
                                    ).then_inc(s_xd, 1)
                dve.wait_ge(s_rst, 16 * i + 16)
                v.tensor_tensor(ktok[:, :, :], B[:, full(15), :].rearrange("p (k d) -> p k d", d=P),
                                st[:, 37:41].unsqueeze(2).to_broadcast([P, QB, P]), ALU.mult).then_inc(s_xd, 1)
                split_thirds(ks_tok, B[0:NS, full(16), 0:P], ("hi", "hi", "lo")).then_inc(s_xd, 1)
                v.tensor_tensor(vbd[:, :, :], vs_tok[:, :].bitcast(F32).unsqueeze(1).to_broadcast([K3, NS, P]),
                                ident3.unsqueeze(2).to_broadcast([K3, NS, P]), ALU.mult).then_inc(s_vbd, 1)
                scaled(halves(rg[:, :]), m0 + 3, (TILE_HEAD + 1) % 2)
                dve.wait_ge(s_rs, 16 * i + 16)
                for j in range(2):
                    r4 = rs[:, 4 * j:4 * j + 4, :]
                    v.scalar_tensor_tensor(out=r4, in0=r4, scalar=st[:, 41:42],
                                           in1=B[:, full(17 + j), :].rearrange("p (b e) -> p b e", e=P),
                                           op0=ALU.mult, op1=ALU.add).then_inc(s_xd, 1)
                v.tensor_copy(ro[:, 0:NP_], B[:, full(19), :]).then_inc(s_xd, 1)
                v.tensor_copy(rst[:, :], B[:, full(20), 0:P]).then_inc(s_xd, 1)
                v.tensor_copy(ro[:, NP_:T], B[:, full(21), 0:NS]).then_inc(s_xd, 1)
                for n, cols in enumerate((slice(0, NP_), slice(NP_, T))):
                    v.tensor_scalar(rv[:, cols], B[:, full(22 + n), 0:cols.stop - cols.start], 1.0 / P, EPS,
                                    ALU.mult, ALU.add).then_inc(s_xd, 1)
                dve.wait_ge(s_th, i + 1)
                step(v.scalar_tensor_tensor(out=rg[:, :], in0=t2[:, :], scalar=1.0, in1=rg[:, :],
                                            op0=ALU.add, op1=ALU.mult))
                dve.wait_ge(s_hs, i + 1)
                newton(rk[:, :], rv[:, :], rq[:, :])
                step(v.tensor_tensor(rk[:, :], rk[:, :], ro[:, :], ALU.mult))
                v.scalar_tensor_tensor(out=row(mix, i + NH), in0=rk[:, :], scalar=0.5, in1=rg[:, :],
                                       op0=ALU.mult, op1=ALU.mult).then_inc(s_head, 1)

            for k in range(NH, KT):
                dve.wait_ge(s_t1h, k + 1)
                v.tensor_tensor(a_lo[:, k, :], mix[:, k, :], a_hi[:, k, :].bitcast(F32), ALU.subtract
                                ).then_inc(s_t1, 1)
            v.memset(ssum[:, :], 0.0).then_inc(s_n2, 1)
            dve.wait_ge(s_xb, 16)

            def split_h2(first, last):
                for k in range(first, last):
                    dve.wait_ge(s_t2h, k + 1)
                    v.scalar_tensor_tensor(out=a_lo[:, k, :], in0=xr[:, k, :], scalar=g2[:, k:k + 1],
                                           in1=a_hi[:, k, :].bitcast(F32), op0=ALU.mult, op1=ALU.subtract
                                           ).then_inc(s_t2, 1)

            def add_out(t, u, used):
                dve.wait_ge(s_used, used)
                xt = row(xr, t)
                v.tensor_tensor(halves(xt), pair((TILE_OUT + u) % 2), halves(xt), ALU.add).then_inc(s_evac, 1)
                dve.wait_ge(s_evac, TILE_OUT + t + 1)
                step(v.tensor_tensor(sq[:, :], xt, xt, ALU.mult))
                dve.wait_ge(s_n2, t + 1)
                v.tensor_tensor(ssum[:, :], ssum[:, :], sq[:, :], ALU.add).then_inc(s_n2, 1)

            for t in range(2):
                add_out(t, t, unit_of(TILE_OUT) + 3 + t)
            with step.loop(KT // 2 - 2, 2) as i:
                for u in range(2):
                    add_out(2 * i + 2 + u, u, unit_of(TILE_OUT) + 4 * i + 4 + 2 * u + 2)
            add_out(KT - 2, 0, unit_of(TILE_MLP) - 2)
            split_h2(0, 8)
            add_out(KT - 1, 1, unit_of(TILE_MLP))
            split_h2(8, KT)

            dve.wait_ge(s_n2m, 1)
            v.tensor_scalar(halves(nv[:, :]), B[:, 0:2, 0:HT], 1.0 / D, EPS, ALU.mult, ALU.add).then_inc(s_n2v, 1)
            dve.wait_ge(s_n2s, 1)
            newton(ny[:, :], nv[:, :], u1[:, :])
            step(v.tensor_copy(rb[:, :], ny[:, :]))

            def hidden(m0, n0):
                with step.loop(CH // 2, 4) as i:
                    for u in range(2):
                        t = 2 * i + u
                        dve.wait_ge(s_used, n0 + 4 * i + 2 * u + 2)
                        v.scalar_tensor_tensor(out=halves(u1[:, :]), in0=pair((TILE_MLP + u) % 2), scalar=0.0,
                                               in1=halves(rb[:, :]), op0=ALU.max, op1=ALU.mult).then_inc(s_evac, 1)
                        dve.wait_ge(s_evac, m0 + t + 1)
                        step(v.tensor_tensor(u2[:, :], u1[:, :], u1[:, :], ALU.mult))
                        step(v.tensor_copy(row(b_hi, t), u2[:, :]))
                        v.tensor_tensor(row(b_lo, t), u2[:, :], row(b_hi, t).bitcast(F32), ALU.subtract
                                        ).then_inc(s_b, 1)

            def add_down(n0, t, u, xt):
                dve.wait_ge(s_used, n0 + 16 + t + 1)
                v.tensor_tensor(halves(xt), pair((TILE_MLP + u) % 2), halves(xt), ALU.add).then_inc(s_evac, 1)

            with step.loop(NCHUNK - 1, 2 * CH) as c:
                m0, n0 = TILE_MLP + 24 * c, unit_of(TILE_MLP) + 32 * c
                hidden(m0, n0)
                with dve.Fori(0, KT // 4) as i:
                    for u in range(4):
                        t = 4 * i + u
                        add_down(n0, t, u, row(xr, t))
            hidden(LAST_TILE, LAST_UNIT)
            for f in range(KT):
                xt = xr[:, f, :]

                def scaled_tile():
                    if f >= 2:
                        dve.wait_ge(s_yx, f - 1)
                    v.tensor_scalar(yt[:, f % 2, :], xt, gf[:, f:f + 1], None, ALU.mult).then_inc(s_yt, 1)

                add_down(LAST_UNIT, f, f % 2, xt)
                dve.wait_ge(s_evac, LAST_TILE + CH + f + 1)
                if f < KT - 1:
                    scaled_tile()
                    step(v.tensor_tensor(sq[:, :] if f else ssum[:, :], xt, xt, ALU.mult))
                    if f == KT - 2:
                        v.tensor_tensor(ssum[:, :], ssum[:, :], sq[:, :], ALU.add).then_inc(s_nf, 1)
                        dve.wait_ge(s_nf, 1)
                    elif f:
                        step(v.tensor_tensor(ssum[:, :], ssum[:, :], sq[:, :], ALU.add))
                else:
                    v.tensor_tensor(sq[:, :], xt, xt, ALU.mult).then_inc(s_nf, 1)
                    scaled_tile()
            dve.wait_ge(s_nfm, 1)
            parts = ((st[:, 70:74], slice(0, P), slice(0, 4)), (st[0:NS, 74:75], slice(0, NS), slice(4, 5)))
            for var, rows_, cols in parts:
                ins = v.tensor_scalar(var, G[rows_, 2, cols], 1.0 / D, EPS, ALU.mult, ALU.add)
            step(ins)
            dve.wait_ge(s_nfm, 2)
            for var, rows_, cols in parts:
                ins = v.scalar_tensor_tensor(out=var, in0=G[rows_, 0, cols], scalar=1.0 / D, in1=var,
                                             op0=ALU.mult, op1=ALU.add)
            ins.then_inc(s_nfv, 1)
            dve.wait_ge(s_nfs, 1)
            newton(st[:, 75:80], st[:, 70:75], st[:, 80:85], s_rn)
            dve.wait_ge(s_rn, 1)
            dve.wait_ge(s_ye, KT)
            for s, _, tb, half in PIECES:
                if s == 0:
                    x = out_t[:, tb, half * D // 2:(half + 1) * D // 2]
                    v.tensor_scalar(x, x, st[:, 75 + tb:76 + tb], None, ALU.mult).then_inc(s_fin[0], 1)


_INS = ['x_prompt', 'x_sample', 'cache_k', 'cache_v', 'cache_idx_k', 'state_ret', 'page_table', 'norm1_g', 'w_in',
        'idx_k_norm_g', 'idx_k_norm_b', 'w_out', 'norm2_g', 'w_up', 'w_down', 'final_norm_g']
_OUTS = [(1, 512, 2048), (8, 1, 2048), (1, 512, 128), (1, 512, 128), (1, 512, 64), (1, 8, 128, 128),
         (8, 1, 128), (8, 1, 128), (8, 1, 64), (8, 8, 128, 128)]


def shape_constants():
    import numpy as np
    lg = np.log1p(-np.exp2(-5.0 - np.arange(NH, dtype=np.float64)))
    p = np.arange(P)
    const = np.zeros((P, 376), np.float32)
    const[:, 0:P] = np.eye(P)
    const[:, P:2 * P] = np.where(p[None, :] <= p[:, None], 0.0, MASKED)
    const[:, 256:288] = np.exp((NP_ - 1.0 - (p[:, None, None] + P * np.arange(QB)[None, :, None]))
                               * lg[None, None, :]).reshape(P, 32)
    const[:, 288:296] = np.exp(lg)[None, :]
    const[0:NS, 296:360] = np.repeat(np.eye(NS), 8, axis=1)
    const[0:64, 360:368] = np.repeat(np.eye(NS), 8, axis=0)
    for r in THIRDS:
        const[r:r + NS, 368:376] = np.eye(NS)
    diff = np.arange(NP_)[None, :] - p[:, None]
    decay = np.where(diff[None] >= 0, np.exp(np.maximum(diff, 0)[None] * lg[:, None, None]), 0.0).astype(np.float32)
    inv = (np.float32(10000.0) ** (-np.arange(64, dtype=np.float32) / np.float32(64))).astype(np.float32)
    pos = np.concatenate([np.arange(NP_), np.full(NS, CL)]).astype(np.float32)
    ang = (inv[:, None] * pos[None, :]).astype(np.float32)
    cos, sin = np.cos(ang), np.sin(ang)
    rotary = np.stack([np.concatenate([cos, cos]), np.concatenate([-sin, sin])], axis=1).astype(np.float32)
    return {"shape_const": const, "shape_rotary": rotary, "shape_decay": decay}


def kernel(**inputs):
    import numpy as _np
    import concourse.bacc as _bacc
    from concourse import mybir as _mybir
    from concourse.bass_utils import run_bass_kernel_spmd as _run

    nc = _bacc.Bacc("TRN2", target_bir_lowering=False, num_devices=1)
    arrays, args = {}, []
    for name in _INS:
        arrays[f"in_{name}_dram"] = _np.ascontiguousarray(inputs[name])
    for name, a in shape_constants().items():
        arrays[f"{name}_dram"] = a
    for name, a in arrays.items():
        args.append(nc.dram_tensor(name, a.shape, _mybir.dt.from_np(a.dtype), kind="ExternalInput").ap())
    for i, shape in enumerate(_OUTS):
        args.append(nc.dram_tensor(f"out_{i}_dram", shape, _mybir.dt.float32, kind="ExternalOutput").ap())
    build(nc, *args)
    r = _run(nc, [arrays], core_ids=[0])
    return tuple(r.results[0][f"out_{i}_dram"] for i in range(len(_OUTS)))
```
